# Optimizing a Trainium2 kernel written in Bass

```python
import math
import jax
import jax.numpy as jnp
from jax import lax
import numpy as np
import jax, jax.numpy as jnp

D_MODEL = 1024
BATCH = 1
SEQ = 256
DEPTH = 1

H_A = 8
HD_A = 64
W_A = H_A * HD_A
MOBA_BLOCK = 256
MOBA_TOPK = 3
Q_CHUNK = 64
NUM_BUCKETS = 32
MAX_EXACT = NUM_BUCKETS // 2
MAX_DISTANCE = 128
H_B = 4
HD_B = 128
W_B = H_B * HD_B
CONV_K = 4
DN_CHUNK = 64
N_GROUPS = 4
EXPERTS_PER_GROUP = 8
TOPK_IN_GROUP = 2
D_FF_EXPERT = 256
D_IN = 3 * W_A + 4 * W_B + 2 * H_B + 2 * D_MODEL
N_MOD = 6
EPS = 1e-6
NEG = -1e30


def rms_norm(x, w):
    xf = x.astype(jnp.float32)
    y = xf * lax.rsqrt(jnp.mean(xf * xf, axis=-1, keepdims=True) + EPS)
    return (y * w.astype(jnp.float32)).astype(x.dtype)

def l2_normalize(t):
    return t * lax.rsqrt(jnp.sum(t * t, axis=-1, keepdims=True) + EPS)

def t5_bucket(dist):
    n = jnp.maximum(dist, 0)
    nf = jnp.maximum(n, 1).astype(jnp.float32)
    large = MAX_EXACT + (jnp.log(nf / MAX_EXACT) / math.log(MAX_DISTANCE / MAX_EXACT)
                         * (NUM_BUCKETS - MAX_EXACT)).astype(jnp.int32)
    large = jnp.minimum(large, NUM_BUCKETS - 1)
    return jnp.where(n < MAX_EXACT, n, large)

def moba_attention(q, k, v, rel_bias):
    B, H, S, hd = q.shape
    L = MOBA_BLOCK
    Sp = -(-S // L) * L
    pad = ((0, 0), (0, 0), (0, Sp - S), (0, 0))
    q, k, v = jnp.pad(q, pad), jnp.pad(k, pad), jnp.pad(v, pad)
    NB, NQ = Sp // L, Sp // Q_CHUNK
    topk = min(MOBA_TOPK, NB)
    scale = HD_A ** -0.5
    k_blocks = k.reshape(B, H, NB, L, hd)
    v_blocks = v.reshape(B, H, NB, L, hd)
    k_mean = jnp.mean(k_blocks.astype(jnp.float32), axis=3)
    q_blk = jnp.arange(Sp) // L
    gate = jnp.einsum('bhsd,bhnd->bhsn', q.astype(jnp.float32), k_mean)
    gate = jnp.where(jnp.arange(NB)[None, :] < q_blk[:, None], gate, NEG)
    _, sel = lax.top_k(gate, topk)
    q_c = q.reshape(B, H, NQ, Q_CHUNK, hd).transpose(2, 0, 1, 3, 4)
    sel_c = sel.reshape(B, H, NQ, Q_CHUNK, topk).transpose(2, 0, 1, 3, 4)
    bi = jnp.arange(B)[:, None, None, None]
    hi = jnp.arange(H)[None, :, None, None]
    hi5 = hi[..., None]
    offs = jnp.arange(L)

    def one_chunk(args):
        q_i, sel_i, i = args
        qb = (i * Q_CHUNK) // L
        q_pos = i * Q_CHUNK + jnp.arange(Q_CHUNK)
        k_sel = k_blocks[bi, hi, sel_i]
        v_sel = v_blocks[bi, hi, sel_i]
        dist_sel = q_pos[None, None, :, None, None] - (sel_i[..., None] * L + offs)
        bias_sel = rel_bias[t5_bucket(dist_sel), hi5].astype(jnp.float32)
        s_sel = jnp.einsum('bhqd,bhqkld->bhqkl', q_i, k_sel).astype(jnp.float32) * scale + bias_sel
        s_sel = jnp.where((sel_i < qb)[..., None], s_sel, NEG)
        k_own = lax.dynamic_index_in_dim(k_blocks, qb, axis=2, keepdims=False)
        v_own = lax.dynamic_index_in_dim(v_blocks, qb, axis=2, keepdims=False)
        dist_own = q_pos[:, None] - (qb * L + offs)[None, :]
        bias_own = rel_bias[t5_bucket(dist_own)].transpose(2, 0, 1).astype(jnp.float32)
        s_own = jnp.einsum('bhqd,bhld->bhql', q_i, k_own).astype(jnp.float32) * scale + bias_own
        s_own = jnp.where(dist_own >= 0, s_own, NEG)
        p = jax.nn.softmax(jnp.concatenate(
            [s_sel.reshape(B, H, Q_CHUNK, topk * L), s_own], axis=-1), axis=-1)
        p_sel = p[..., :topk * L].reshape(B, H, Q_CHUNK, topk, L).astype(v.dtype)
        p_own = p[..., topk * L:].astype(v.dtype)
        return (jnp.einsum('bhqkl,bhqkld->bhqd', p_sel, v_sel)
                + jnp.einsum('bhql,bhld->bhqd', p_own, v_own))

    o = lax.map(one_chunk, (q_c, sel_c, jnp.arange(NQ)))
    o = o.transpose(1, 2, 0, 3, 4).reshape(B, H, Sp, hd)
    return o[:, :, :S]

def causal_depthwise_conv(x, w):
    C = x.shape[-1]
    return lax.conv_general_dilated(
        x, w[:, None, :].astype(x.dtype), window_strides=(1,), padding=[(CONV_K - 1, 0)],
        dimension_numbers=('NWC', 'WIO', 'NWC'), feature_group_count=C)

def gated_delta_rule(q, k, v, beta, g):
    out_dtype = v.dtype
    B, S, H, DK = q.shape
    DV = v.shape[-1]
    C = DN_CHUNK
    N = S // C
    f32 = jnp.float32
    q = l2_normalize(q.astype(f32)) * (DK ** -0.5)
    k = l2_normalize(k.astype(f32))
    v = v.astype(f32)

    def chunk(t):
        return t.reshape(B, N, C, H, -1).transpose(0, 3, 1, 2, 4)

    q, k, v = chunk(q), chunk(k), chunk(v)
    beta = beta.astype(f32).reshape(B, N, C, H).transpose(0, 3, 1, 2)
    G = jnp.cumsum(g.astype(f32).reshape(B, N, C, H).transpose(0, 3, 1, 2), axis=-1)
    tril = jnp.tril(jnp.ones((C, C), bool))
    strict = jnp.tril(jnp.ones((C, C), bool), -1)
    dec = jnp.exp(jnp.where(tril, G[..., :, None] - G[..., None, :], -jnp.inf))
    kb = k * beta[..., None]
    A = jnp.eye(C, dtype=f32) + jnp.where(strict, jnp.einsum('bhnid,bhnjd->bhnij', kb, k) * dec, 0.0)
    u = lax.linalg.triangular_solve(A, v * beta[..., None], left_side=True, lower=True, unit_diagonal=True)
    w = lax.linalg.triangular_solve(A, kb * jnp.exp(G)[..., None], left_side=True, lower=True, unit_diagonal=True)
    P = jnp.einsum('bhnid,bhnjd->bhnij', q, k) * dec
    qg = q * jnp.exp(G)[..., None]
    kd = k * jnp.exp(G[..., -1:] - G)[..., None]
    gl = jnp.exp(G[..., -1])
    xs = tuple(jnp.moveaxis(t, 2, 0) for t in (u, w, qg, P, kd, gl))

    def step(state, inp):
        u_n, w_n, qg_n, P_n, kd_n, gl_n = inp
        v_new = u_n - jnp.einsum('bhck,bhkv->bhcv', w_n, state)
        o_n = jnp.einsum('bhck,bhkv->bhcv', qg_n, state) + jnp.einsum('bhcj,bhjv->bhcv', P_n, v_new)
        state = state * gl_n[..., None, None] + jnp.einsum('bhck,bhcv->bhkv', kd_n, v_new)
        return state, o_n

    _, o = lax.scan(step, jnp.zeros((B, H, DK, DV), f32), xs)
    return o.transpose(1, 0, 3, 2, 4).reshape(B, S, H, DV).astype(out_dtype)

def token_mixer(h, rel_bias, w_in, conv_w, a_log, dt_bias, onorm_w, w_up_a, w_up_b, w_out):
    B, S, _ = h.shape
    proj = h @ w_in
    sizes = (W_A, W_A, W_A, 3 * W_B, W_B, H_B, H_B, D_MODEL, D_MODEL)
    offs = np.cumsum(sizes)[:-1].tolist()
    qa, ka, va, qkv_b, z_b, b_b, a_b, gate_a, gate_b = jnp.split(proj, offs, axis=-1)
    heads_a = lambda t: t.reshape(B, S, H_A, HD_A).transpose(0, 2, 1, 3)
    y_a = moba_attention(heads_a(qa), heads_a(ka), heads_a(va), rel_bias)
    y_a = y_a.transpose(0, 2, 1, 3).reshape(B, S, W_A)
    qkv_b = jax.nn.silu(causal_depthwise_conv(qkv_b, conv_w))
    q_b, k_b, v_b = (t.reshape(B, S, H_B, HD_B) for t in jnp.split(qkv_b, 3, axis=-1))
    beta = jax.nn.sigmoid(b_b)
    g = -jnp.exp(a_log) * jax.nn.softplus(a_b + dt_bias)
    o_b = gated_delta_rule(q_b, k_b, v_b, beta, g)
    o_b = rms_norm(o_b, onorm_w) * jax.nn.silu(z_b.reshape(B, S, H_B, HD_B))
    y_b = o_b.reshape(B, S, W_B)
    m = jax.nn.sigmoid(gate_a) * (y_a @ w_up_a) + jax.nn.sigmoid(gate_b) * (y_b @ w_up_b)
    return m @ w_out

def hier_moe(h, w_rg, b_rg, w_re, b_re, w_e_gate, w_e_up, w_e_down):
    B, S, D = h.shape
    t = h.reshape(-1, D)
    T = t.shape[0]
    pg = jax.nn.softmax((t @ w_rg + b_rg).astype(jnp.float32), axis=-1)
    p_top, g_top = lax.top_k(pg, 1)
    oh_g = jax.nn.one_hot(g_top[:, 0], N_GROUPS, dtype=jnp.float32)
    le = (t @ w_re + b_re).astype(jnp.float32).reshape(T, N_GROUPS, EXPERTS_PER_GROUP)
    le_g = jnp.einsum('tge,tg->te', le, oh_g)
    v2, e2 = lax.top_k(le_g, TOPK_IN_GROUP)
    w2 = jax.nn.softmax(v2, axis=-1) * p_top
    comb_e = jnp.sum(w2[..., None] * jax.nn.one_hot(e2, EXPERTS_PER_GROUP, dtype=jnp.float32), axis=1)
    comb = (oh_g[:, :, None] * comb_e[:, None, :]).astype(t.dtype)
    y = jnp.zeros_like(t)
    for gi in range(N_GROUPS):
        a = jax.nn.silu(jnp.einsum('td,edf->tef', t, w_e_gate[gi])) * jnp.einsum('td,edf->tef', t, w_e_up[gi])
        y = y + jnp.einsum('tef,te,efd->td', a, comb[:, gi], w_e_down[gi])
    return y.reshape(B, S, D)

def first_inputs(seed: int = 0) -> dict:
    key = jax.random.key(seed)
    ks = iter(jax.random.split(key, 32))
    L, D = DEPTH, D_MODEL
    G, E, F = N_GROUPS, EXPERTS_PER_GROUP, D_FF_EXPERT

    def nrm(shape, std):
        return std * jax.random.normal(next(ks), shape, jnp.float32)

    x = nrm((BATCH, SEQ, D), 1.0)
    c = nrm((BATCH, D), 1.0)
    rel_bias = nrm((NUM_BUCKETS, H_A), 0.5)
    final_norm_w = 1.0 + nrm((D,), 0.02)
    norm1_w = 1.0 + nrm((L, D), 0.02)
    norm2_w = 1.0 + nrm((L, D), 0.02)
    w_mod = nrm((L, D, N_MOD * D), 0.5 * D ** -0.5)
    b_mod = nrm((L, N_MOD * D), 0.02)
    w_in = nrm((L, D, D_IN), D ** -0.5)
    conv_w = nrm((L, CONV_K, 3 * W_B), CONV_K ** -0.5)
    a_log = jnp.log(jax.random.uniform(next(ks), (L, H_B), jnp.float32, 1.0, 16.0))
    dt = jnp.exp(jax.random.uniform(next(ks), (L, H_B), jnp.float32, math.log(1e-3), math.log(1e-1)))
    dt_bias = dt + jnp.log(-jnp.expm1(-dt))
    onorm_w = 1.0 + nrm((L, HD_B), 0.02)
    w_up_a = nrm((L, W_A, D), W_A ** -0.5)
    w_up_b = nrm((L, W_B, D), W_B ** -0.5)
    w_out = nrm((L, D, D), D ** -0.5)
    w_rg = nrm((L, D, G), D ** -0.5)
    b_rg = nrm((L, G), 0.01)
    w_re = nrm((L, D, G * E), D ** -0.5)
    b_re = nrm((L, G * E), 0.01)
    w_e_gate = nrm((L, G, E, D, F), D ** -0.5)
    w_e_up = nrm((L, G, E, D, F), D ** -0.5)
    w_e_down = nrm((L, G, E, F, D), F ** -0.5)
    return {"x": x, "c": c, "rel_bias": rel_bias, "final_norm_w": final_norm_w,
            "norm1_w": norm1_w, "norm2_w": norm2_w, "w_mod": w_mod, "b_mod": b_mod,
            "w_in": w_in, "conv_w": conv_w, "a_log": a_log, "dt_bias": dt_bias,
            "onorm_w": onorm_w, "w_up_a": w_up_a, "w_up_b": w_up_b, "w_out": w_out,
            "w_rg": w_rg, "b_rg": b_rg, "w_re": w_re, "b_re": b_re,
            "w_e_gate": w_e_gate, "w_e_up": w_e_up, "w_e_down": w_e_down}

def first_block(x, c, rel_bias, final_norm_w, norm1_w, norm2_w, w_mod, b_mod, w_in, conv_w,
              a_log, dt_bias, onorm_w, w_up_a, w_up_b, w_out, w_rg, b_rg, w_re, b_re,
              w_e_gate, w_e_up, w_e_down):
    c_act = jax.nn.silu(c)
    for l in range(DEPTH):
        mod = (c_act @ w_mod[l] + b_mod[l])[:, None, :]
        sh1, sc1, g1, sh2, sc2, g2 = jnp.split(mod, N_MOD, axis=-1)
        h = rms_norm(x, norm1_w[l]) * (1.0 + sc1) + sh1
        x = x + g1 * token_mixer(h, rel_bias, w_in[l], conv_w[l], a_log[l], dt_bias[l],
                                 onorm_w[l], w_up_a[l], w_up_b[l], w_out[l])
        h = rms_norm(x, norm2_w[l]) * (1.0 + sc2) + sh2
        x = x + g2 * hier_moe(h, w_rg[l], b_rg[l], w_re[l], b_re[l],
                              w_e_gate[l], w_e_up[l], w_e_down[l])
    return rms_norm(x, final_norm_w)


DEPTH_2 = 4

N_MIXERS = 3
SB_HEADS = 16
SB_HEAD_DIM = D_MODEL // SB_HEADS
SB_Q_BLOCK = 128
CONV_WIDTH = 3
GLA_HEADS = 4
GLA_DK = D_MODEL // 2
GLA_DV = D_MODEL
GLA_DK_HEAD = GLA_DK // GLA_HEADS
GLA_DV_HEAD = GLA_DV // GLA_HEADS
GLA_GATE_RANK = 16
GLA_GATE_NORMALIZER = 16.0
GLA_CHUNK = 64
D_FF = 4 * D_MODEL
RMS_EPS = 1e-6


def rms_norm_2(x, gain):
    xf = x.astype(jnp.float32)
    y = xf * lax.rsqrt(jnp.mean(xf * xf, axis=-1, keepdims=True) + RMS_EPS) * gain.astype(jnp.float32)
    return y.astype(x.dtype)

def stick_breaking_mixer(xn, w_qkv, w_o):
    b, s, _ = xn.shape
    qkv = (xn @ w_qkv).reshape(b, s, 3, SB_HEADS, SB_HEAD_DIM)
    q, k, v = [qkv[:, :, i].transpose(0, 2, 1, 3).astype(jnp.float32) for i in range(3)]
    scale = SB_HEAD_DIM ** -0.5
    n_blocks = s // SB_Q_BLOCK
    q_blocks = q.reshape(b, SB_HEADS, n_blocks, SB_Q_BLOCK, SB_HEAD_DIM).transpose(2, 0, 1, 3, 4)
    key_pos = jnp.arange(s)

    def one_block(args):
        qb, start = args
        z = jnp.einsum('bhqd,bhkd->bhqk', qb, k) * scale
        q_pos = start + jnp.arange(SB_Q_BLOCK)
        mask = key_pos[None, :] < q_pos[:, None]
        log_beta = jax.nn.log_sigmoid(z)
        log_1m_beta = jnp.where(mask, jax.nn.log_sigmoid(-z), 0.0)
        suffix = lax.cumsum(log_1m_beta, axis=3, reverse=True) - log_1m_beta
        weights = jnp.where(mask, jnp.exp(log_beta + suffix), 0.0)
        return jnp.einsum('bhqk,bhkd->bhqd', weights, v)

    o = lax.map(one_block, (q_blocks, jnp.arange(n_blocks) * SB_Q_BLOCK))
    o = o.transpose(1, 0, 3, 2, 4).reshape(b, s, D_MODEL).astype(xn.dtype)
    return o @ w_o

def short_conv_mixer(xn, w_in, conv_w, w_out):
    s = xn.shape[1]
    bcu = xn @ w_in
    b_gate, c_gate, u = jnp.split(bcu, 3, axis=-1)
    h = c_gate * u
    hp = jnp.pad(h, ((0, 0), (CONV_WIDTH - 1, 0), (0, 0)))
    conv = sum(conv_w[i] * hp[:, i:i + s] for i in range(CONV_WIDTH))
    return (b_gate * conv) @ w_out

def gla_mixer(xn, w_in, w_gate_up, b_gate, head_norm, w_o):
    b, s, _ = xn.shape
    n_chunks = s // GLA_CHUNK
    proj = xn @ w_in
    q, k, v, g, a_low = jnp.split(
        proj, np.cumsum([GLA_DK, GLA_DK, GLA_DV, GLA_DV]).tolist(), axis=-1)
    log_gate = jax.nn.log_sigmoid(
        (a_low @ w_gate_up + b_gate).astype(jnp.float32)) / GLA_GATE_NORMALIZER

    def to_chunks(t, dh):
        t = t.astype(jnp.float32).reshape(b, n_chunks, GLA_CHUNK, GLA_HEADS, dh)
        return t.transpose(1, 0, 3, 2, 4)

    qc = to_chunks(q, GLA_DK_HEAD) * (GLA_DK_HEAD ** -0.5)
    kc = to_chunks(k, GLA_DK_HEAD)
    vc = to_chunks(v, GLA_DV_HEAD)
    gc = to_chunks(log_gate, GLA_DK_HEAD)
    causal = jnp.tril(jnp.ones((GLA_CHUNK, GLA_CHUNK), dtype=bool))

    def step(state, inp):
        qi, ki, vi, gi = inp
        cum = jnp.cumsum(gi, axis=2)
        inter = jnp.einsum('bhcd,bhde->bhce', qi * jnp.exp(cum), state)
        diff = cum[:, :, :, None, :] - cum[:, :, None, :, :]
        decay = jnp.exp(jnp.where(causal[None, None, :, :, None], diff, -jnp.inf))
        scores = jnp.einsum('bhid,bhjd,bhijd->bhij', qi, ki, decay)
        out = inter + jnp.einsum('bhij,bhje->bhie', scores, vi)
        last = cum[:, :, -1:, :]
        new_state = jnp.exp(last)[:, :, 0, :, None] * state + jnp.einsum(
            'bhcd,bhce->bhde', ki * jnp.exp(last - cum), vi)
        return new_state, out

    state0 = jnp.zeros((b, GLA_HEADS, GLA_DK_HEAD, GLA_DV_HEAD), jnp.float32)
    _, o = lax.scan(step, state0, (qc, kc, vc, gc))
    o = o.transpose(1, 0, 3, 2, 4).reshape(b, s, GLA_HEADS, GLA_DV_HEAD)
    o = rms_norm_2(o, head_norm).reshape(b, s, GLA_DV).astype(xn.dtype)
    return (o * jax.nn.silu(g)) @ w_o

def squared_relu_mlp(xn, w_up, w_down):
    return jnp.square(jax.nn.relu(xn @ w_up)) @ w_down

def second_inputs(seed: int = 0) -> dict:
    key = jax.random.key(seed)
    ks = jax.random.split(key, 16)
    n_sb = (DEPTH_2 + 2) // 3
    n_conv = (DEPTH_2 + 1) // 3
    n_gla = DEPTH_2 // 3
    f32 = jnp.float32

    def nrm(k, shape, scale):
        return jax.random.normal(k, shape, f32) * scale

    d_in_gla = 2 * GLA_DK + 2 * GLA_DV + GLA_GATE_RANK
    return {
        "x": nrm(ks[0], (BATCH, SEQ, D_MODEL), 1.0),
        "norm_gains": 1.0 + nrm(ks[1], (DEPTH_2, 4, D_MODEL), 0.02),
        "sb_w_qkv": nrm(ks[2], (n_sb, D_MODEL, 3 * D_MODEL), D_MODEL ** -0.5),
        "sb_w_o": nrm(ks[3], (n_sb, D_MODEL, D_MODEL), D_MODEL ** -0.5),
        "conv_w_in": nrm(ks[4], (n_conv, D_MODEL, 3 * D_MODEL), D_MODEL ** -0.5),
        "conv_w": nrm(ks[5], (n_conv, CONV_WIDTH, D_MODEL), CONV_WIDTH ** -0.5),
        "conv_w_out": nrm(ks[6], (n_conv, D_MODEL, D_MODEL), D_MODEL ** -0.5),
        "gla_w_in": nrm(ks[7], (n_gla, D_MODEL, d_in_gla), D_MODEL ** -0.5),
        "gla_w_gate_up": nrm(ks[8], (n_gla, GLA_GATE_RANK, GLA_DK), GLA_GATE_RANK ** -0.5),
        "gla_b_gate": nrm(ks[9], (n_gla, GLA_DK), 0.1),
        "gla_head_norm": 1.0 + nrm(ks[10], (n_gla, GLA_HEADS, GLA_DV_HEAD), 0.02),
        "gla_w_o": nrm(ks[11], (n_gla, GLA_DV, D_MODEL), GLA_DV ** -0.5),
        "ffn_w_up": nrm(ks[12], (DEPTH_2, D_MODEL, D_FF), D_MODEL ** -0.5),
        "ffn_w_down": nrm(ks[13], (DEPTH_2, D_FF, D_MODEL), D_FF ** -0.5),
    }

def second_block(x, norm_gains, sb_w_qkv, sb_w_o, conv_w_in, conv_w, conv_w_out,
              gla_w_in, gla_w_gate_up, gla_b_gate, gla_head_norm, gla_w_o,
              ffn_w_up, ffn_w_down):
    h = x
    for i in range(DEPTH_2):
        kind, j = i % N_MIXERS, i // N_MIXERS
        xn = rms_norm_2(h, norm_gains[i, 0])
        if kind == 0:
            m = stick_breaking_mixer(xn, sb_w_qkv[j], sb_w_o[j])
        elif kind == 1:
            m = short_conv_mixer(xn, conv_w_in[j], conv_w[j], conv_w_out[j])
        else:
            m = gla_mixer(xn, gla_w_in[j], gla_w_gate_up[j], gla_b_gate[j],
                          gla_head_norm[j], gla_w_o[j])
        h = h + rms_norm_2(m, norm_gains[i, 1])
        f = squared_relu_mlp(rms_norm_2(h, norm_gains[i, 2]), ffn_w_up[i], ffn_w_down[i])
        h = h + rms_norm_2(f, norm_gains[i, 3])
    return h


def setup_inputs(seed=0):
    out = dict(first_inputs(seed))
    for name, value in second_inputs(seed + 1).items():
        if name != "x":
            out[name + "_2"] = value
    return out


def reference(
    x, c, rel_bias, final_norm_w, norm1_w, norm2_w, w_mod, b_mod, w_in, conv_w, a_log, dt_bias,
    onorm_w, w_up_a, w_up_b, w_out, w_rg, b_rg, w_re, b_re, w_e_gate, w_e_up, w_e_down,
    norm_gains_2, sb_w_qkv_2, sb_w_o_2, conv_w_in_2, conv_w_2, conv_w_out_2, gla_w_in_2,
    gla_w_gate_up_2, gla_b_gate_2, gla_head_norm_2, gla_w_o_2, ffn_w_up_2, ffn_w_down_2,
):
    x = first_block(
        x, c, rel_bias, final_norm_w, norm1_w, norm2_w, w_mod, b_mod, w_in, conv_w, a_log,
        dt_bias, onorm_w, w_up_a, w_up_b, w_out, w_rg, b_rg, w_re, b_re, w_e_gate, w_e_up,
        w_e_down,
    )
    return second_block(
        x, norm_gains_2, sb_w_qkv_2, sb_w_o_2, conv_w_in_2, conv_w_2, conv_w_out_2, gla_w_in_2,
        gla_w_gate_up_2, gla_b_gate_2, gla_head_norm_2, gla_w_o_2, ffn_w_up_2, ffn_w_down_2,
    )


_drawn_inputs = setup_inputs


def setup_inputs(seed=0):
    import zlib

    import numpy as np

    out = dict(_drawn_inputs(seed))
    spreads = {}
    factors = {'norm1_w': 5.984,
     'norm2_w': 3.417,
     'onorm_w': 4.948,
     'b_rg': 8.0,
     'b_re': 3.589,
     'gla_b_gate_2': 3.036,
     'gla_head_norm_2': 6.724}
    for name, (base, spread) in spreads.items():
        noise = np.random.default_rng([zlib.crc32(name.encode()), seed]).standard_normal(out[name].shape)
        drawn = base * np.exp(spread * noise) if base else spread * noise
        out[name] = jnp.asarray(drawn.astype(out[name].dtype))
    for name, factor in factors.items():
        out[name] = (out[name] * factor).astype(out[name].dtype)
    return out
```

```python
from contextlib import ExitStack

import numpy as np
import concourse.bass as bass
from concourse import mybir

F32 = mybir.dt.float32
F32R = mybir.dt.float32r
ALU = mybir.AluOpType
ACT = mybir.ActivationFunctionType
AX = mybir.AxisListType.X

P = 128
D = 1024
KC = D // P
S = 256
NT = S // P
EPS = 1e-6
NEG = -1e30

HA, HDA = 8, 64
HB = 4
NG, NE, FE = 4, 8, 256
EXPERTS = NG * NE
FF = 4096
FBLK = FF // 512
SBH = 16
GH = 4
GSUB = 32
GCLAMP = 60.0
LEVELS = 7

RAW = 8
SPL = 4
WB = 4

C_QA, C_KA, C_VA, C_QKVB, C_Z, C_BA, C_GA, C_GB = 0, 512, 1024, 1536, 3072, 3584, 3592, 4616


class Step:

    def __init__(self, name, arg, nu, nk):
        self.name, self.arg, self.nu, self.nk = name, arg, nu, nk
        self.u = self.k = 0
        self.sb = 0


def schedule():
    st = []

    def add(name, arg=None, nu=0, nk=0, sb=0):
        st.append(Step(name, arg, nu, nk))
        st[-1].sb = sb

    add("params", None, 1)
    add("cond")
    for n in range(4):
        add("mod", n, 1, 4)
    add("norm", 0, 4)
    add("bias", None, HA)
    for c in range(6):
        add("tblk", ("pre", c), 1, 2)
    add("ba", None, 1)
    mods = [("mod", n, 1, 4) for n in range(4, 12)]
    add("conv_b")
    add("dtok", None, 6)
    add("decay", None, 1)
    add("decay_rows", None, 2)
    add("dtr", None, 6)
    add("dmat", None, 4)
    for lev in range(LEVELS):
        add("inv_y", lev, 2)
        add(*mods[lev])
        add("inv_x", lev, 4 if lev < LEVELS - 1 else 2)
    add(*mods[7])
    add("du", None, 3)
    add("nblk", ("z", 0), 2, 4)
    add("dstate", None, 2)
    for c in range(2):
        add("tblk", ("qa", c), 1, 2)
    add("dnew", None, 1)
    for c in range(2):
        add("tblk", ("ka", c), 1, 2)
    add("dout", None, 1)
    add("nblk", ("va", 0), 2, 4)
    add("dyt", None, 2)
    for item in range(HA * 2 + 2):
        nu = (item < 16) + (1 <= item < 17) + (item >= 2 and (item - 2) % 4 == 3)
        add("moba", item, nu)
    for c in range(4):
        add("tblk", ("ga", c), 1, 2)
    for c in range(4):
        add("tblk", ("gb", c), 1, 2)
    for c in range(4):
        add("up", c, 2, 2)
    add("wout", 0, 0, 8)
    add("res1")
    add("norm", 1, 4)
    add("router", None, 1)
    add("moe", None, EXPERTS * 3, EXPERTS * 6)
    add("res2")
    for layer in range(4):
        add("norm", 2 + 2 * layer, 4)
        if layer in (0, 3):
            for d in ("sq", "sk"):
                for c in range(4):
                    add("tblk", (d, c), 1, 2, layer // 3)
            for c in range(2):
                add("nblk", ("sv", c), 2, 4, layer // 3)
            for h in range(SBH + 2):
                add("sb", h, (h < SBH) + (h >= 2 and h % 2 == 1), 0, layer // 3)
        elif layer == 1:
            for d in ("cc", "cu", "cb"):
                for c in range(4):
                    add("tblk", (d, c), 1, 2)
        else:
            add("galow", None, 3)
            for d in ("gq", "gk"):
                for c in range(2):
                    add("tblk", (d, c), 1, 2)
            add("gcum", None, 4)
            for c in range(2):
                add("nblk", ("gv", c), 2, 4)
            add("gscore", None, 2)
            for c in range(2):
                add("nblk", ("gg", c), 2, 4)
            add("gout", None, 6)
            add("gyt", None, 4)
        add("wout", layer + 1, 0, 8)
        add("post", ("mix", layer))
        add("norm", 3 + 2 * layer, 4)
        add("ffn", layer, FBLK * 4, FBLK * 8)
        add("post", ("ffn", layer))
    u = k = 0
    for s in st:
        s.u, s.k = u, k
        u += s.nu
        k += s.nk
    return st


def release_plan(steps):
    rel, used, acc = {}, 0, 0

    def count(k):
        nonlocal used
        used += 1
        rel[k] = ("used", used)

    def unit(k, u):
        rel[k] = ("unit", u)

    for s in steps:
        k = s.k
        if s.name == "up":
            unit(k, s.u)
            unit(k + 1, s.u + 1)
        elif s.name in ("tblk", "mod", "nblk"):
            for j in range(s.nk - 1):
                count(k + j)
            unit(k + s.nk - 1, s.u + s.nu - 1)
        elif s.name == "wout":
            for j in range(7):
                count(k + j)
            acc += 1
            rel[k + 7] = ("acc", acc)
        elif s.name in ("ffn", "moe"):
            blocks, nd, per = (FBLK, 4, 4) if s.name == "ffn" else (EXPERTS, 2, 3)
            for b in range(blocks + 1):
                if b < blocks:
                    for j in range(3):
                        count(k + j)
                    unit(k + 3, s.u + per * b + 1)
                    k += 4
                if b > 0:
                    for j in range(nd):
                        if b == blocks and j == nd - 1:
                            acc += 1
                            rel[k + j] = ("acc", acc)
                        else:
                            count(k + j)
                    k += nd
    return rel


def tile_t(w, c):
    b = w[:, c:c + 256].reshape(2, 4, P, 256)
    return [x.transpose(1, 0, 2).reshape(P, 1024) for x in b]


def tile_n(w, c):
    b = w[:, c:c + 512].reshape(4, 2, P, 512)
    return [x.transpose(1, 0, 2).reshape(P, 1024) for x in b]


def tile_rows(w):
    return list(w.reshape(-1, P, 1024))


def weight_tiles(i, steps):
    out = []
    win = i["w_in"][0]
    for s in steps:
        if s.name == "mod":
            out += tile_n(i["w_mod"][0], 512 * s.arg)
        elif s.name in ("tblk", "nblk"):
            kind, c = s.arg
            layer3 = s.sb
            w, c0 = {
                "pre": (win, C_QKVB), "qa": (win, C_QA), "ka": (win, C_KA), "va": (win, C_VA),
                "z": (win, C_Z), "ga": (win, C_GA), "gb": (win, C_GB),
                "sq": (i["sb_w_qkv_2"][layer3], 0), "sk": (i["sb_w_qkv_2"][layer3], D),
                "sv": (i["sb_w_qkv_2"][layer3], 2 * D),
                "cb": (i["conv_w_in_2"][0], 0), "cc": (i["conv_w_in_2"][0], D),
                "cu": (i["conv_w_in_2"][0], 2 * D),
                "gq": (i["gla_w_in_2"][0], 0), "gk": (i["gla_w_in_2"][0], 512),
                "gv": (i["gla_w_in_2"][0], D), "gg": (i["gla_w_in_2"][0], 2 * D),
            }[kind]
            out += tile_t(w, c0 + 256 * c) if s.name == "tblk" else tile_n(w, c0 + 512 * c)
        elif s.name == "up":
            for w in (i["w_up_a"][0], i["w_up_b"][0]):
                b = w[:, 256 * s.arg:256 * s.arg + 256].reshape(4, P, 256)
                out.append(b.transpose(1, 0, 2).reshape(P, 1024))
        elif s.name == "wout":
            w = [i["w_out"][0], i["sb_w_o_2"][0], i["conv_w_out_2"][0], i["gla_w_o_2"][0],
                 i["sb_w_o_2"][1]][s.arg]
            out += tile_rows(w)
        elif s.name == "moe":
            for e in range(EXPERTS + 1):
                if e < EXPERTS:
                    g, x = divmod(e, NE)
                    gu = np.concatenate([i["w_e_gate"][0, g, x], i["w_e_up"][0, g, x]], axis=1)
                    out += tile_n(gu, 0)
                if e > 0:
                    g, x = divmod(e - 1, NE)
                    out += tile_rows(i["w_e_down"][0, g, x])
        elif s.name == "ffn":
            up, down = i["ffn_w_up_2"][s.arg], i["ffn_w_down_2"][s.arg]
            for b in range(FBLK + 1):
                if b < FBLK:
                    out += tile_n(up, 512 * b)
                if b > 0:
                    out += tile_rows(down[512 * (b - 1):512 * b])
    return np.ascontiguousarray(np.stack(out))


def constants():
    j = np.arange(P)[:, None]
    i = np.arange(P)[None, :]
    parts = {
        "ident": (i == j), "tri": (j <= i), "neg_ge": -1.0 * (j >= i), "neg_one": -np.ones((P, P)),
        "after": (j > i), "strict": (i > j), "one": np.ones((P, P)),
        "levels": np.concatenate([((i >> (v + 1)) == (j >> (v + 1))) & ((i >> v) & 1 == 1)
                                  & ((j >> v) & 1 == 0) for v in range(LEVELS)], axis=1),
        "sbmask": np.concatenate([i > j, np.ones((P, P)), i > j], axis=1),
        "iota": np.broadcast_to(np.arange(NE)[None, :], (P, NE)),
    }
    at, cols = {}, 0
    for n, a in parts.items():
        at[n] = (cols, a.shape[1])
        cols += a.shape[1]
    return np.concatenate([np.asarray(a, np.float32) for a in parts.values()], axis=1), at


def bucket_rows():
    m = np.arange(512)
    n = np.maximum(255 - m, 0)
    nf = np.maximum(n, 1).astype(np.float32)
    large = 16 + (np.log(nf / np.float32(16)) / np.float32(np.log(8.0)) * np.float32(16)).astype(np.int32)
    b = np.where(n < 16, n, np.minimum(large, 31))
    rows = np.zeros((33, 512), np.float32)
    rows[b, m] = 1.0
    rows[:, m > 255] = 0.0
    rows[32, m > 255] = NEG
    return rows


R_N1, R_N2, R_BM, R_PRE, R_CW, R_CW2 = 0, 8, 16, 64, 128, 176
ROWS1, ROWS2 = 128, 72
B_G1, B_G2, B_FINAL, B_POST, B_HEAD = 0, 1, 2, 3, 11
S_DT, S_AL, S_BR, S_ON, S_W = 0, 4, 8, 44, 172


def build(nc, aps, dbg=None):
    steps = schedule()
    rel = release_plan(steps)
    cst_host, cst_at = constants()
    NCST = cst_host.shape[1]
    NTILES = sum(s.nk for s in steps)
    NUNITS = sum(s.nu for s in steps)
    wall, out = aps["weights"], aps["out"]
    bias_rows = nc.dram_tensor("bias_rows", (HA, P, 512), F32, kind="Internal")

    with ExitStack() as ctx:
        def sb(name, shape, dt=F32):
            return ctx.enter_context(nc.sbuf_tensor("s_" + name, shape, dt))

        def sem(name):
            return ctx.enter_context(nc.semaphore(name))

        raw = sb("raw", [P, RAW, 1024])
        whi = sb("whi", [P, SPL, 1024], F32R)
        wlo = sb("wlo", [P, SPL, 1024], F32R)
        H = sb("h", [P, NT, D])
        XS = sb("xs", [P, NT, D])
        XF = sb("xf", [P, KC, S])
        XTh, XTl = sb("xth", [P, KC, S], F32R), sb("xtl", [P, KC, S], F32R)
        OTh, OTl = sb("oth", [P, KC, S], F32R), sb("otl", [P, KC, S], F32R)
        GB = sb("gb", [P, 2, D])
        CST = sb("cst", [P, NCST])
        COLP = sb("colp", [P, ROWS1 + ROWS2])
        SROW = sb("srow", [P, S_W])
        SMW = sb("smw", [P, KC, 60])
        GUP = sb("gup", [17, 512])
        CC = sb("cc", [P, 3, KC])
        MODC = sb("modc", [P, 5, KC])
        SS = sb("ss", [P, 16])
        VAR = sb("var", [P, 16])
        RS = sb("rs", [P, 16])
        MH = sb("mh", [P, 16])
        BA = sb("ba", [P, 2, 8])
        BT = sb("bt", [P, 8, 8])
        GC = sb("gc", [P, 24])
        EG = sb("eg", [P, 24])
        REL = sb("rel", [33, HA])
        RT = sb("rt", [P, 2, 160])
        COMB = sb("comb", [P, 2, EXPERTS])
        AR = sb("arena", [P, 15648])

        def area(start, *shape):
            n = int(np.prod(shape))
            v = AR[:, start:start + n]
            if len(shape) == 1:
                return v
            names = "abcd"[:len(shape)]
            pat = f"p ({' '.join(names)}) -> p {' '.join(names)}"
            return v.rearrange(pat, **dict(zip(names, shape)))

        def cst(name):
            a, w = cst_at[name]
            return CST[:, a:a + w]

        IDENT, TRI = cst("ident"), cst("tri")

        def over(v, n):
            return v.unsqueeze(1).broadcast_to([P, n, v.shape[1]])

        PRE, POST = area(0, 12, 259), area(3108, 12, S)
        KNT, KBT, QNT = area(0, 2, HB, P), area(1024, 2, HB, P), area(2048, 2, HB, P)
        DTI, DTS, NMT = area(3108, 8, P), area(4132, 8, P), area(5156, 8, P)
        TOK = area(6180, 3, NT, 512)
        KBK = area(9252, NT, 512)
        KBG, KD = area(10276, 512), area(10788, 512)
        ER, WT, S1B, VNW = area(11300, 512), area(11812, 512), area(12324, 512), area(12836, 512)
        PTM = area(13348, 8, P)
        NTL = area(14372, 8, P)
        QGT = area(11300, 512)
        XI = XS[:, 0, :].rearrange("p (a b) -> p a b", a=8)
        XTI = XS[:, 1, :].rearrange("p (a b) -> p a b", a=8)
        YI = XF[:, 0:4, :].rearrange("p a b -> p (a b)").rearrange("p (a b) -> p a b", a=8)
        UI = XF[:, 4:8, :].rearrange("p a b -> p (a b)").rearrange("p (a b) -> p a b", a=8)
        ZS = area(5156, NT, 512)
        OB = area(6180, NT, 512)
        QAT, KAT, VA = area(0, 4, S), area(1024, 4, S), area(2048, NT, 512)
        BIAS = area(9252, HA, NT, S)
        MS_, MP = area(3108, 2, S), area(3620, 2, S)
        MPT = area(13348, 4, NT, S)
        BST = area(8228, 2, 512)
        RB, PR, OH = area(9252, HA, P)[0:33], area(10276, 2, P), area(10788, 512)[0:33]
        SGA, SGB = area(0, KC, S), area(2048, KC, S)
        MTMP = area(4096, 2, S)
        SG, AE = area(0, NT, 256), area(512, NT, 256)
        HID = area(0, NT, 512)
        QT, KT, VT = area(0, KC, S), area(2048, KC, S), area(4096, NT, D)
        AB, LN, SPB = area(6144, 2, 384), area(6912, 2, 384), area(7680, 2, 384)
        SPM, WX, WM = area(8448, 2, 384), area(9216, 4, 384), area(10752, 4, 384)
        CB, HP, CV = area(0, KC, S), area(2048, KC, 258), area(4112, 2, S)
        GQ, GK, GV, GG = area(0, GH, S), area(1024, GH, S), area(2048, NT, D), area(4096, NT, D)
        ALT = area(6144, S)
        LG, CUM, QGL = area(6400, NT, 512), area(7424, GH, S), area(8448, GH, S)
        KBB = area(9472, 2, GH, S)
        STT = area(11520, NT, GH, P)
        QI, KDG, KTK, ES = area(12544, GH, P), area(13056, 512), area(13568, 512), area(14080, 512)
        S1G = area(14592, GH, 256)
        REF = area(15616, GH * NT, 4)
        GTM = area(14592, NT, 512)

        work = [ctx.enter_context(nc.psum_tensor(f"work{b}", [P, 512], F32)) for b in range(WB)]
        ACC = ctx.enter_context(nc.psum_tensor("acc", [P, 4, 512], F32))

        load_const = sem("load_const")
        loaded = [sem(f"loaded{i}") for i in range(RAW)]
        hi_made, lo_made, used = sem("hi_made"), sem("lo_made"), sem("used")
        full = [sem(f"full{b}") for b in range(WB)]
        done = [sem(f"done{b}") for b in range(WB)]
        acc_full, acc_free = sem("acc_full"), sem("acc_free")
        hi_out = sem("hi_out")
        x_hi, x_lo = sem("x_hi"), sem("x_lo")
        xf_ready = sem("xf_ready")
        var_ready, rs_ready = sem("var_ready"), sem("rs_ready")
        gb_loaded, gb_free = [sem("gb_loaded0"), sem("gb_loaded1")], sem("gb_free")
        act_chain, dve_chain = sem("act_chain"), sem("dve_chain")
        a2d, d2a = sem("act_to_dve"), sem("dve_to_act")
        d2p = sem("dve_to_pe")
        z_full = sem("z_full")
        hid_ready = sem("hid_ready")
        h_final = sem("h_final")
        conv_ready = sem("conv_ready")
        RS2 = sb("rs2", [P, 2])
        bias_written = [sem("bias_written0"), sem("bias_written1")]
        bias_read = sem("bias_read")
        logs_ready, weights_ready, pool_masked = sem("logs_ready"), sem("weights_ready"), sem("pool_masked")
        out_sem = sem("out_written")

        def full_wait(eng, u, extra=0):
            eng.wait_ge(full[u % WB], u // WB + 1 + extra)

        def done_wait(eng, u, extra=0):
            eng.wait_ge(done[u % WB], u // WB + 1 + extra)

        def bank(u):
            return work[u % WB]

        block = ctx.enter_context(nc.Block())

        NCONST = 10

        @block.sync
        def _(sp):
            for dst, src in (
                (H[:], aps["x"].rearrange("b (t p) d -> p (b t) d", p=P)),
                (CST[:], aps["cst"]), (PR[:, 0, :], aps["prows"][0:ROWS1, :]),
                (PR[0:ROWS2, 1, :], aps["prows"][ROWS1:ROWS1 + ROWS2, :]),
                (CC[:, 0, :], aps["c"].rearrange("b (k p) -> p (b k)", p=P)),
                (SROW[:], aps["srow"].partition_broadcast(P)),
                (SMW[:], aps["smw"]), (GUP[:], aps["gup"]), (REL[0:32, :], aps["rel_bias"]),
                (OH[:], aps["oh"]),
            ):
                with nc.allow_non_contiguous_dma("small parameters"):
                    sp.dma_start(dst, src).then_inc(load_const, 16)
            first = NTILES % RAW + RAW
            for k in range(first):
                if k >= RAW:
                    sp.wait_ge(lo_made, k - RAW + 1)
                sp.dma_start(raw[:, k % RAW, :], wall[k]).then_inc(loaded[k % RAW], 16)
            with sp.Fori(0, (NTILES - first) // RAW) as it:
                for j in range(RAW):
                    k = first + j
                    sp.wait_ge(lo_made, it * RAW + (k - RAW + 1))
                    sp.dma_start(raw[:, k % RAW, :], wall[it * RAW + k]).then_inc(loaded[k % RAW], 16)
            sp.wait_ge(h_final, 1)
            for t in range(NT):
                sp.dma_start(out[0, t * P:(t + 1) * P, :], H[:, t, :]).then_inc(out_sem, 16)
            sp.wait_ge(out_sem, 16 * NT)

        def tile_wait(eng, k, it=None, per=None):
            kind, v = rel[k]
            extra = 0 if it is None else it * per[kind]
            if kind == "used":
                eng.wait_ge(used, v + extra)
            elif kind == "acc":
                eng.wait_ge(acc_full, v)
            else:
                full_wait(eng, v, extra)

        class Splitter:

            def __init__(self, one):
                self.next, self.one = 0, one

            def upto(self, k):
                while self.next < min(k, NTILES):
                    self.one(self.next)
                    self.next += 1

        def make_hi(k, it=None, per=None):
            act = nc.scalar
            n = 0 if it is None else it * per["tiles"]
            nr = 0 if it is None else it * (16 * per["tiles"] // RAW)
            act.wait_ge(loaded[k % RAW], 16 * (k // RAW + 1) + nr)
            if k >= SPL:
                tile_wait(act, k - SPL, it, per)
            act.copy(whi[:, k % SPL, :], raw[:, k % RAW, :]).then_inc(hi_made, 1)

        def make_lo(k, it=None, per=None):
            dve = nc.vector
            n = 0 if it is None else it * per["tiles"]
            dve.wait_ge(hi_made, n + (k + 1))
            dve.tensor_tensor(wlo[:, k % SPL, :], raw[:, k % RAW, :],
                              whi[:, k % SPL, :].bitcast(F32), ALU.subtract).then_inc(lo_made, 1)

        FFN_PER = {"tiles": 8, "used": 7, "unit": 1}
        MOE_PER = {"tiles": 24, "used": 20, "unit": 3}

        def post_row(which, layer):
            return B_POST + 2 * layer + (which == "ffn")

        gb_rows = [B_G1, B_G2, B_FINAL]
        for layer in range(4):
            if layer == 2:
                gb_rows.append(B_HEAD)
            gb_rows += [post_row("mix", layer), post_row("ffn", layer)]

        @block.gpsimd
        def _(pool):
            asked = masked = n_logs = n_weights = uses = loads = 0

            def load_rows():
                nonlocal loads
                while loads < min(uses + 2, len(gb_rows)):
                    if loads >= 2:
                        pool.wait_ge(gb_free, loads - 1)
                    pool.dma_start(GB[:, loads % 2, :], aps["brow"][gb_rows[loads]].partition_broadcast(P))\
                        .then_inc(gb_loaded[loads % 2], 16)
                    loads += 1

            def inv_sqrt():
                nonlocal asked
                asked += 1
                pool.wait_ge(var_ready, asked)
                pool.tensor_tensor(RS[:], VAR[:], MH[:], ALU.pow).then_inc(rs_ready, 1)

            def mask(dst, src):
                pool.tensor_tensor(dst, src, cst("sbmask"), ALU.mult).then_inc(pool_masked, 1)

            load_rows()
            for s in steps:
                if s.name == "norm":
                    inv_sqrt()
                    load_rows()
                elif s.name in ("conv_b", "dyt", "gyt"):
                    inv_sqrt()
                elif s.name == "res2":
                    inv_sqrt()
                elif s.name == "post":
                    inv_sqrt()
                if s.name == "bias":
                    for h in range(HA):
                        done_wait(pool, s.u + h)
                        with nc.allow_non_contiguous_dma("rows"):
                            pool.dma_start(bias_rows.ap()[h], BST[:, h % 2, :]).then_inc(bias_written[h % 2], 16)
                elif s.name == "dyt":
                    for b in range(2):
                        pool.wait_ge(bias_written[b], 8 * HA)
                    done_wait(pool, s.u + 1)
                    for t in range(NT):
                        src = bass.AP(tensor=bias_rows, offset=255 - P * t,
                                      ap=[[511, P], [P * 512, HA], [1, S]])
                        pool.dma_start(BIAS[:, :, t, :], src).then_inc(bias_read, 16)
                if s.name in ("res1", "gyt"):
                    uses += 1
                elif s.name == "post":
                    uses += 1
                elif s.name == "res2":
                    uses += 2
                if s.name == "sb":
                    h = s.arg
                    if h < SBH:
                        n_logs += 1
                        pool.wait_ge(logs_ready, n_logs)
                        mask(SPM[:, h % 2, :], SPB[:, h % 2, :])
                    if 1 <= h <= SBH:
                        n_weights += 1
                        pool.wait_ge(weights_ready, n_weights)
                        mask(WM[:, (h - 1) % 4, :], WX[:, (h - 1) % 4, :])

        @block.scalar
        def _(act):
            chain = n_a2d = n_d2a = n_hi = nx = nacc = nxf = 0

            def link(ins):
                nonlocal chain
                chain += 1
                ins.then_inc(act_chain, 1)

            def sync():
                act.wait_ge(act_chain, chain)

            def tell_dve(ins):
                nonlocal n_a2d
                n_a2d += 1
                ins.then_inc(a2d, 1)

            def hear_dve():
                nonlocal n_d2a
                n_d2a += 1
                act.wait_ge(d2a, n_d2a)

            split = Splitter(make_hi)

            def ev_hi(u, dst, src=None, extra=0):
                full_wait(act, u, extra)
                src = bank(u)[:] if src is None else src
                act.copy(dst, src).then_inc(hi_out, 1)

            def ev(u, dst, func=ACT.Copy, src=None, scale=1.0):
                full_wait(act, u)
                act.activation(dst, bank(u)[:] if src is None else src, func, scale=scale)\
                    .then_inc(done[u % WB], 1)

            def x_split(j, dst):
                nonlocal nx
                act.copy(dst[:, 2 * j:2 * j + 2, :], XF[:, 2 * j:2 * j + 2, :]).then_inc(x_hi, 1)
                nx += 1

            def v2(u):
                return bank(u)[:].rearrange("p (a b) -> p a b", a=2)

            def v4(u):
                return bank(u)[:].rearrange("p (a b) -> p a b", a=4)

            act.wait_ge(load_const, 16 * NCONST)
            for s in steps:
                u, a = s.u, s.arg
                if s.name in ("tblk", "mod", "nblk", "up", "wout"):
                    split.upto(s.k + s.nk + SPL)
                if s.name == "mod" and a in (3, 9):
                    hear_dve()
                elif s.name == "cond":
                    link(act.activation(CC[:, 1, :], CC[:, 0, :], ACT.Silu))
                    sync()
                    tell_dve(act.copy(CC[:, 2, :], CC[:, 1, :]))
                    hear_dve()
                    act.copy(OTh[:, :, 0:P], XF[:, :, 0:P]).then_inc(x_hi, 1)
                    nx += 1
                elif s.name == "norm":
                    j = a
                    for q in range(4):
                        full_wait(act, u + q)
                        for c in range(2):
                            ch = 2 * q + c
                            if j < 2:
                                sc, bi = MODC[:, 2 * j + 1, ch:ch + 1], MODC[:, 2 * j, ch:ch + 1]
                            else:
                                sc, bi = COLP[:, R_PRE + 8 * (j - 2) + ch:][:, 0:1], 0.0
                            ins = act.activation(XF[:, ch, :], v2(u + q)[:, c, :], ACT.Identity,
                                                 bias=bi, scale=sc)
                        ins.then_inc(done[(u + q) % WB], 1)
                        done_wait(act, u + q)
                        x_split(q, XTh)
                elif s.name == "bias":
                    for h in range(HA):
                        if h >= 2:
                            act.wait_ge(bias_written[h % 2], 16 * (h // 2))
                        ev(u + h, BST[:, h % 2, :])
                elif s.name == "tblk":
                    kind, c = a
                    if kind == "pre":
                        ev(u, PRE[:, 2 * c:2 * c + 2, 3:259], src=v2(u))
                    elif kind in ("qa", "ka"):
                        ev(u, (QAT if kind == "qa" else KAT)[:, 2 * c:2 * c + 2, :], src=v2(u))
                    elif kind in ("ga", "gb"):
                        ev(u, (SGA if kind == "ga" else SGB)[:, 2 * c:2 * c + 2, :], ACT.Sigmoid, v2(u))
                    elif kind in ("sq", "gq"):
                        ev(u, (QT if kind == "sq" else GQ)[:, 2 * c:2 * c + 2, :], src=v2(u),
                           scale=0.125 if kind == "sq" else float(P) ** -0.5)
                    elif kind in ("sk", "gk"):
                        ev(u, (KT if kind == "sk" else GK)[:, 2 * c:2 * c + 2, :], src=v2(u))
                    elif kind == "cc":
                        ev(u, CB[:, 2 * c:2 * c + 2, :], src=v2(u))
                    elif kind == "cb":
                        done_wait(act, u)
                        x_split(c, OTh)
                elif s.name == "nblk":
                    kind, c = a
                    for t in range(NT):
                        dst = {"z": ZS, "va": VA}[kind][:, t, :] if kind in ("z", "va") else \
                            {"sv": VT, "gv": GV, "gg": GG}[kind][:, t, 512 * c:512 * c + 512]
                        ev(u + t, dst, ACT.Silu if kind in ("z", "gg") else ACT.Copy)
                elif s.name == "ba":
                    hear_dve()
                    link(act.activation(BT[:, 2, :], BT[:, 0, :], ACT.Exp, scale=-1.0))
                    link(act.activation(BT[:, 3, :], BT[:, 1, :], ACT.Abs))
                    link(act.activation(BT[:, 6, 0:4], SROW[:, S_AL:S_AL + 4], ACT.Exp))
                    sync()
                    link(act.activation(BT[:, 4, :], BT[:, 3, :], ACT.Exp, scale=-1.0))
                    sync()
                    tell_dve(act.activation(BT[:, 5, :], BT[:, 4, :], ACT.Ln, bias=1.0))
                elif s.name == "conv_b":
                    for q in range(3):
                        hear_dve()
                        act.activation(POST[:, 4 * q:4 * q + 4, :], POST[:, 4 * q:4 * q + 4, :],
                                       ACT.Silu).then_inc(conv_ready, 1)
                elif s.name == "dtok":
                    for b in range(2):
                        act.wait_ge(bias_written[b], 8 * HA)
                    for q in range(6):
                        ev(u + q, TOK[:, q // 2, q % 2, :])
                elif s.name == "decay":
                    full_wait(act, u)
                    act.activation(EG[:], bank(u)[:, 0:24], ACT.Exp).then_inc(a2d, 1)
                    n_a2d += 1
                elif s.name == "decay_rows":
                    full_wait(act, u + 1)
                    tell_dve(act.activation(ER, bank(u + 1)[:], ACT.Exp))
                    done_wait(act, u)
                    done_wait(act, u + 1)
                    tell_dve(act.activation(DTI, DTI, ACT.Exp))
                elif s.name == "dtr":
                    for q in range(6):
                        ev(u + q, (KNT, KBT, QNT)[q // 2][:, q % 2], src=v4(u + q))
                elif s.name == "inv_y":
                    for q in range(2):
                        ev(u + q, YI[:, 4 * q:4 * q + 4, :], src=v4(u + q))
                elif s.name == "du":
                    for q in range(2):
                        ev(u + q, UI[:, 4 * q:4 * q + 4, :], src=v4(u + q))
                    ev(u + 2, WT)
                elif s.name == "dstate":
                    ev(u, OB[:, 0, :])
                    ev(u + 1, S1B)
                elif s.name == "dout":
                    ev(u, OB[:, 1, :])
                elif s.name in ("dyt", "gyt"):
                    for q in range(s.nu):
                        c0 = 4 + 2 * q if s.name == "dyt" else 2 * q
                        ev_hi(u + q, OTh[:, c0:c0 + 2, :], v2(u + q))
                elif s.name == "moba":
                    n = a
                    if n < 16:
                        kk = P * (n % 2 + 1)
                        hear_dve()
                        tell_dve(act.activation(MP[:, n % 2, 0:kk], MS_[:, n % 2, 0:kk], ACT.Exp,
                                                bias=SS[:, n % 2:n % 2 + 1],
                                                accum_out=RS2[:, n % 2:n % 2 + 1]))
                    if 1 <= n <= 16:
                        h, t = divmod(n - 1, 2)
                        w = s.u + (n < 16)
                        for_k = bank(w)[:, 0:P * (t + 1)].rearrange("p (a b) -> p a b", a=t + 1)
                        ev(w, MPT[:, h % 4, 0:t + 1, t * P:t * P + P], src=for_k)
                    if n >= 2 and (n - 2) % 4 == 3:
                        w = s.u + s.nu - 1
                        ev_hi(w, OTh[:, (n - 2) // 4, :], bank(w)[:, 0:S])
                elif s.name == "up":
                    nxf += 1
                    act.wait_ge(xf_ready, nxf)
                    x_split(a, XTh)
                elif s.name == "router":
                    hear_dve()
                    for t in range(NT):
                        r = RT[:, t, :]
                        tell_dve(act.activation(r[:, 40:44], r[:, 0:4], ACT.Exp, bias=r[:, 37:38],
                                                accum_out=r[:, 44:45]))
                    hear_dve()
                    tell_dve(act.activation(RT[:, :, 98:99], RT[:, :, 97:98], ACT.Exp))
                elif s.name == "post":
                    nacc += 1
                    act.wait_ge(acc_full, nacc)
                    for b in range(4):
                        ins = act.activation(XF[:, 2 * b:2 * b + 2, :].rearrange("p a b -> p (a b)"),
                                             ACC[:, b, :], ACT.Square, accum_out=SS[:, b:b + 1])
                        link(ins)
                    sync()
                    tell_dve(act.copy(SS[:, 8:12], SS[:, 0:4]))
                elif s.name in ("res1", "res2"):
                    nacc += 1
                elif s.name == "sb":
                    h = a
                    if h < SBH:
                        full_wait(act, u)
                        link(act.activation(AB[:, h % 2, :], bank(u)[:, 0:384], ACT.Abs))
                        sync()
                        link(act.activation(AB[:, h % 2, :], AB[:, h % 2, :], ACT.Exp, scale=-1.0))
                        sync()
                        tell_dve(act.activation(LN[:, h % 2, :], AB[:, h % 2, :], ACT.Ln, bias=1.0))
                    if 1 <= h <= SBH:
                        g = (h - 1) % 4
                        done_wait(act, z_prev)
                        act.activation(WX[:, g, :], WX[:, g, :], ACT.Exp).then_inc(weights_ready, 1)
                    if h < SBH:
                        z_prev = u
                    if h >= 2 and h % 2 == 1:
                        w = s.u + s.nu - 1
                        ev_hi(w, OTh[:, (h - 3) // 2, :], bank(w)[:, 0:S])
                elif s.name == "galow":
                    ev(u, ALT[0:16, :], src=bank(u)[0:16, 0:S])
                    for t in range(NT):
                        full_wait(act, u + 1 + t)
                        link(act.activation(GTM[:, t, :], bank(u + 1 + t)[:], ACT.Abs))
                        sync()
                        link(act.activation(GTM[:, t, :], GTM[:, t, :], ACT.Exp, scale=-1.0))
                        sync()
                        tell_dve(act.activation(GTM[:, t, :], GTM[:, t, :], ACT.Ln, bias=1.0))
                elif s.name == "gcum":
                    for q in range(2):
                        ev(u + q, CUM[:, 2 * q:2 * q + 2, :], src=v2(u + q), scale=1.0 / 16)
                    ev(u + 2, ES, ACT.Exp, scale=1.0 / 16)
                    ev(u + 3, KTK)
                    done_wait(act, u)
                    done_wait(act, u + 1)
                    tell_dve(act.activation(QI, CUM[:, :, P:S], ACT.Exp))
                elif s.name == "gscore":
                    hear_dve()
                    tell_dve(act.activation(QGL, QGL, ACT.Exp))
                    for b in range(4):
                        hear_dve()
                        tell_dve(act.activation(KBB[:, b % 2], KBB[:, b % 2], ACT.Exp, scale=-1.0))
                elif s.name == "gout":
                    for q in range(2):
                        ev(u + q, S1G[:, 2 * q:2 * q + 2, :], src=v2(u + q))
                    for q in range(4):
                        ev(u + 2 + q, XS[:, q // 2, 512 * (q % 2):512 * (q % 2) + 512])
                elif s.name == "moe":
                    def silu(ub, extra=0):
                        for t in range(NT):
                            full_wait(act, ub + t, extra)
                            act.activation(SG[:, t, :], bank(ub + t)[:, 0:256], ACT.Silu).then_inc(a2d, 1)

                    def t_hi(ut, extra=0):
                        ev_hi(ut, OTh[:, 0:2, :], v2(ut), extra)

                    def one(e, k, ub, it=None):
                        extra = 0 if it is None else it * MOE_PER["unit"]
                        for kk in (k + 4, k + 5):
                            make_hi(kk, it, MOE_PER)
                        silu(ub, extra)
                        for kk in range(k + 6, k + 10):
                            make_hi(kk, it, MOE_PER)
                        t_hi(ub + 2, extra)

                    split.upto(s.k + 4)
                    silu(u)
                    split.upto(s.k + 8)
                    t_hi(u + 2)
                    for e in range(3):
                        one(e, s.k + 4 + 6 * e, u + 3 * (e + 1))
                    with act.Fori(0, 7) as it:
                        for e in range(3, 7):
                            one(e, s.k + 4 + 6 * e, u + 3 * (e + 1), it)
                    split.next = s.k + s.nk + 2
                    n_a2d += 2 * EXPERTS
                elif s.name == "ffn":
                    def relu(ub, extra=0):
                        for t in range(NT):
                            full_wait(act, ub + t, extra)
                            act.activation(HID[:, t, :], bank(ub + t)[:], ACT.Relu)\
                                .then_inc(done[(ub + t) % WB], 1)

                    def t_hi(ut, extra=0):
                        for t in range(NT):
                            ev_hi(ut + t, OTh[:, 0:4, t * P:t * P + P], v4(ut + t), extra)

                    def one(b, k, ub, it=None):
                        extra = 0 if it is None else it * FFN_PER["unit"]
                        for kk in range(k + 4, k + 8):
                            make_hi(kk, it, FFN_PER)
                        relu(ub, extra)
                        for kk in range(k + 8, k + 12):
                            make_hi(kk, it, FFN_PER)
                        t_hi(ub + 2, extra)

                    split.upto(s.k + 4)
                    relu(u)
                    split.upto(s.k + 8)
                    t_hi(u + 2)
                    one(0, s.k + 4, u + 4)
                    with act.Fori(0, FBLK - 2) as it:
                        one(1, s.k + 12, u + 8, it)
                    split.next = s.k + s.nk

        @block.tensor
        def _(pe):
            nx = n_d2p = nacc = nconv = nhid = 0

            def hear_dve(n=1):
                nonlocal n_d2p
                n_d2p += n
                pe.wait_ge(d2p, n_d2p)

            def begin(u, extra=0):
                if u >= WB:
                    done_wait(pe, u - WB, extra)

            def wait_units(units):
                for x in units:
                    done_wait(pe, x)

            def fin(ins, u):
                ins.then_inc(full[u % WB], 1)

            def mm(o, lhs, rhs, start=True, stop=True, **kw):
                return pe.matmul(o, lhs, rhs, start=start, stop=stop, **kw)

            def mm3(o, lhs, rhs, start, stop):
                mm(o, lhs[0], rhs[0], start, False)
                mm(o, lhs[0], rhs[1], False, False)
                return mm(o, lhs[1], rhs[0], False, stop)

            def tr(o, x):
                return pe.transpose(o, x, IDENT[0:x.shape[0], 0:x.shape[0]])

            def w(k, a, b):
                return whi[:, k % SPL, a:b], wlo[:, k % SPL, a:b]

            def xs_(t, kc, a=None, b=None):
                h, l = t
                if a is None:
                    return h[:, kc, :], l[:, kc, :]
                return h[:, kc, a:b], l[:, kc, a:b]

            XT, OT = (XTh, XTl), (OTh, OTl)

            def tile_ready(k, extra=0):
                pe.wait_ge(lo_made, extra + (k + 1))

            def rows_by_cols(x, k, u, nt=NT, it=None, per=None):
                ek = 0 if it is None else it * per["tiles"]
                eu = 0 if it is None else it * per["unit"]
                for t in range(nt):
                    begin(u + t, eu)
                for j in range(4):
                    tile_ready(k + j, ek)
                    for kc in (2 * j, 2 * j + 1):
                        for t in range(nt):
                            ins = mm3(bank(u + t)[:], xs_(x, kc, t * P, t * P + P),
                                      w(k + j, 512 * (kc % 2), 512 * (kc % 2) + 512), kc == 0, kc == 7)
                            if kc == 7:
                                fin(ins, u + t)
                    if j < 3:
                        ins.then_inc(used, 1)

            def rows_acc(x, kcs, k, first, last, it=None, per=None):
                nonlocal nacc
                ek = 0 if it is None else it * per["tiles"]
                if first:
                    if nacc:
                        pe.wait_ge(acc_free, 4 * nacc)
                    nacc += 1
                for j, kc in enumerate(kcs):
                    tile_ready(k + j, ek)
                    for t in range(NT):
                        for c in range(2):
                            ins = mm3(ACC[:, 2 * t + c, :], xs_(x, kc, t * P, t * P + P),
                                      w(k + j, 512 * c, 512 * c + 512),
                                      first and j == 0, last and j == len(kcs) - 1)
                    ins.then_inc(acc_full if last and j == len(kcs) - 1 else used, 1)

            def masks(h, layer):
                return 2 * SBH * layer + max(2 * h, 1)

            def weights(h, layer):
                return 2 * SBH * layer + min(2 * h + 3, 2 * SBH)

            pe.wait_ge(load_const, 16 * NCONST)
            for s in steps:
                u, a = s.u, s.arg
                if s.name == "params":
                    tr(bank(u)[:, 0:ROWS1], PR[:, 0, :])
                    fin(tr(bank(u)[:, ROWS1:ROWS1 + ROWS2], PR[0:ROWS2, 1, :]), u)
                elif s.name == "cond":
                    nx += 1
                elif s.name == "mod":
                    pe.wait_ge(x_lo, 1)
                    rows_by_cols(OT, s.k, u, nt=1)
                elif s.name == "norm":
                    hear_dve()
                    for q in range(4):
                        begin(u + q)
                        for c in range(2):
                            for t in range(NT):
                                ins = tr(bank(u + q)[:, (2 * c + t) * P:(2 * c + t + 1) * P],
                                         XS[:, t, (2 * q + c) * P:(2 * q + c + 1) * P])
                        fin(ins, u + q)
                    nx += 4
                elif s.name == "bias":
                    hear_dve()
                    for h in range(HA):
                        begin(u + h)
                        fin(mm(bank(u + h)[:], RB[:, h, :], OH[:]), u + h)
                elif s.name == "tblk":
                    pe.wait_ge(x_lo, nx)
                    begin(u)
                    for m in range(2):
                        for kc in range(KC):
                            if m == 0 and kc % 4 == 0:
                                tile_ready(s.k + kc // 4)
                            c0 = (kc % 4) * 256 + m * P
                            ins = mm3(bank(u)[:, m * S:m * S + S], w(s.k + kc // 4, c0, c0 + P),
                                      xs_(XT, kc), kc == 0, kc == 7)
                            if m == 1 and kc == 3:
                                ins.then_inc(used, 1)
                    fin(ins, u)
                elif s.name == "nblk":
                    pe.wait_ge(x_lo, nx)
                    rows_by_cols(XT, s.k, u)
                elif s.name == "ba":
                    pe.wait_ge(x_lo, nx)
                    begin(u)
                    for t in range(NT):
                        for kc in range(KC):
                            ins = mm(bank(u)[:, 8 * t:8 * t + 8], XF[:, kc, t * P:t * P + P],
                                     SMW[:, kc, 0:8], kc == 0, kc == 7)
                    fin(ins, u)
                elif s.name == "dtok":
                    for q in range(6):
                        sec, t = divmod(q, 2)
                        if t == 0:
                            nconv += 1
                            pe.wait_ge(conv_ready, nconv)
                        begin(u + q)
                        for h in range(HB):
                            ins = tr(bank(u + q)[:, h * P:h * P + P],
                                     POST[:, 4 * sec + h, t * P:t * P + P])
                        fin(ins, u + q)
                elif s.name == "decay":
                    hear_dve()
                    begin(u)
                    for q, m in enumerate(("tri", "after", "one")):
                        for t in range(NT):
                            ins = mm(bank(u)[:, 8 * q + 4 * t:8 * q + 4 * t + 4], cst(m),
                                     BT[:, 7, 4 * t:4 * t + 4])
                    fin(ins, u)
                elif s.name == "decay_rows":
                    for t in range(NT):
                        begin(u + t)
                        for h in range(HB):
                            ins = mm(bank(u + t)[:, h * P:h * P + P], NTL[:, 4 * t + h, :], TRI)
                        fin(ins, u + t)
                elif s.name == "dtr":
                    for q in range(6):
                        kind, t = divmod(q, 2)
                        if t == 0:
                            hear_dve()
                        begin(u + q)
                        src = (TOK[:, 1, t, :], KBK[:, t, :], TOK[:, 0, t, :])[kind]
                        for h in range(HB):
                            ins = tr(bank(u + q)[:, h * P:h * P + P], src[:, h * P:h * P + P])
                        fin(ins, u + q)
                elif s.name == "dmat":
                    for q in range(4):
                        kind, t = divmod(q, 2)
                        done_wait(pe, u - 4 + q)
                        if q == 0:
                            done_wait(pe, u - 6)
                            done_wait(pe, u - 5)
                        begin(u + q)
                        for h in range(HB):
                            ins = mm(bank(u + q)[:, h * P:h * P + P], KNT[:, t, h, :],
                                     (QNT if kind else KBT)[:, t, h, :])
                        fin(ins, u + q)
                elif s.name == "inv_y":
                    hear_dve()
                    for q in range(2):
                        begin(u + q)
                        for h in range(4):
                            ins = mm(bank(u + q)[:, h * P:h * P + P], NTL[:, 4 * q + h, :],
                                     XI[:, 4 * q + h, :])
                        fin(ins, u + q)
                    y_units = (u, u + 1)
                elif s.name == "inv_x":
                    x_units = u
                    for q in range(s.nu):
                        if q < 2:
                            done_wait(pe, y_units[q])
                        begin(u + q)
                        m0 = 4 * (q % 2)
                        xy = s.nu == 4 and q < 2
                        for h in range(4):
                            ins = mm(bank(u + q)[:, h * P:h * P + P],
                                     (XTI if xy else YI)[:, m0 + h, :], (YI if xy else XTI)[:, m0 + h, :])
                        fin(ins, u + q)
                elif s.name == "du":
                    for q in range(2):
                        done_wait(pe, x_units + q)
                    for t in range(NT):
                        begin(u + t)
                        for h in range(HB):
                            ins = mm(bank(u + t)[:, h * P:h * P + P], XTI[:, 4 * t + h, :],
                                     TOK[:, 2, t, h * P:h * P + P])
                        fin(ins, u + t)
                    begin(u + 2)
                    for h in range(HB):
                        ins = mm(bank(u + 2)[:, h * P:h * P + P], KBG[:, h * P:h * P + P],
                                 XTI[:, 4 + h, :])
                    fin(ins, u + 2)
                    du = u
                elif s.name == "dstate":
                    done_wait(pe, du)
                    begin(u)
                    for h in range(HB):
                        ins = mm(bank(u)[:, h * P:h * P + P], PTM[:, h, :], UI[:, h, :])
                    fin(ins, u)
                    begin(u + 1)
                    for h in range(HB):
                        ins = mm(bank(u + 1)[:, h * P:h * P + P], KD[:, h * P:h * P + P], UI[:, h, :])
                    fin(ins, u + 1)
                    dst = u + 1
                elif s.name == "dnew":
                    done_wait(pe, dst)
                    done_wait(pe, du + 2)
                    begin(u)
                    for h in range(HB):
                        ins = mm(bank(u)[:, h * P:h * P + P], WT[:, h * P:h * P + P],
                                 S1B[:, h * P:h * P + P])
                    fin(ins, u)
                    dnew = u
                elif s.name == "dout":
                    done_wait(pe, dnew)
                    begin(u)
                    for h in range(HB):
                        o = bank(u)[:, h * P:h * P + P]
                        mm(o, QGT[:, h * P:h * P + P], S1B[:, h * P:h * P + P], True, False)
                        ins = mm(o, PTM[:, 4 + h, :], VNW[:, h * P:h * P + P], False, True)
                    fin(ins, u)
                elif s.name in ("dyt", "gyt"):
                    hear_dve()
                    src = OB if s.name == "dyt" else XS
                    for q in range(s.nu):
                        begin(u + q)
                        for c in range(2):
                            for t in range(NT):
                                ins = tr(bank(u + q)[:, (2 * c + t) * P:(2 * c + t + 1) * P],
                                         src[:, t, (2 * q + c) * P:(2 * q + c + 1) * P])
                        fin(ins, u + q)
                    mixed = [u + q for q in range(s.nu)]
                elif s.name == "moba":
                    n = a
                    v = u
                    if n == 0:
                        for x in steps:
                            if x.name in ("tblk", "nblk") and x.arg[0] in ("qa", "ka", "va"):
                                for q in range(x.nu):
                                    done_wait(pe, x.u + q)
                    if n < 16:
                        h, t = divmod(n, 2)
                        r, c = 64 * (h % 2), h // 2
                        begin(v)
                        fin(mm(bank(v)[:, 0:P * (t + 1)], QAT[r:r + 64, c, t * P:t * P + P],
                               KAT[r:r + 64, c, 0:P * (t + 1)]), v)
                        v += 1
                    if 1 <= n <= 16:
                        t = (n - 1) % 2
                        hear_dve()
                        begin(v)
                        for kt in range(t + 1):
                            ins = tr(bank(v)[:, kt * P:kt * P + P], MP[:, (n - 1) % 2, kt * P:kt * P + P])
                        fin(ins, v)
                        tr_unit = v
                        v += 1
                    if n >= 2 and (n - 2) % 4 == 3:
                        for x in steps:
                            if x.name == "moba" and n - 4 <= x.arg <= n - 1:
                                done_wait(pe, x.u + (x.arg < 16))
                        begin(v)
                        for h in (2 * ((n - 2) // 4), 2 * ((n - 2) // 4) + 1):
                            o = bank(v)[64 * (h % 2):64 * (h % 2) + 64, :]
                            mm(o[:, 0:S], VA[:, 0, 64 * h:64 * h + 64], MPT[:, h % 4, 0, :], True, False)
                            ins = mm(o[:, P:S], VA[:, 1, 64 * h:64 * h + 64], MPT[:, h % 4, 1, P:S],
                                     False, True)
                        fin(ins, v)
                elif s.name == "up":
                    if a == 0:
                        for x in steps:
                            if x.name == "dyt" or (x.name == "moba" and x.arg in (5, 9, 13, 17)):
                                for q in range(x.nu):
                                    done_wait(pe, x.u + q)
                    for q in range(2):
                        tile_ready(s.k + q)
                        begin(u + q)
                        for m in range(2):
                            for kc in range(4):
                                c0 = kc * 256 + m * P
                                ins = mm3(bank(u + q)[:, m * S:m * S + S], w(s.k + q, c0, c0 + P),
                                          xs_(OT, 4 * q + kc), kc == 0, kc == 3)
                        fin(ins, u + q)
                    nx += 1
                elif s.name == "wout":
                    pe.wait_ge(x_lo, nx)
                    if a in (1, 3, 4):
                        wait_units(mixed)
                    rows_acc(XT if a == 0 else OT, range(KC), s.k, True, True)
                elif s.name == "router":
                    pe.wait_ge(x_lo, nx)
                    begin(u)
                    for t in range(NT):
                        for kc in range(KC):
                            ins = mm(bank(u)[:, 64 * t:64 * t + 36], XF[:, kc, t * P:t * P + P],
                                     SMW[:, kc, 8:44], kc == 0, kc == 7)
                    fin(ins, u)
                elif s.name == "moe":
                    def expert_in(k, ub, it=None):
                        rows_by_cols(XT, k, ub, it=it, per=MOE_PER)

                    def expert_tr(ub, it=None):
                        eu = 0 if it is None else it * MOE_PER["unit"]
                        done_wait(pe, ub, eu)
                        done_wait(pe, ub + 1, eu)
                        begin(ub + 2, eu)
                        for c in range(2):
                            for t in range(NT):
                                ins = tr(bank(ub + 2)[:, (2 * c + t) * P:(2 * c + t + 1) * P],
                                         AE[:, t, c * P:c * P + P])
                        fin(ins, ub + 2)

                    def down(ub, k, first, last, it=None):
                        done_wait(pe, ub + 2, 0 if it is None else it * MOE_PER["unit"])
                        rows_acc(OT, range(2), k, first, last, it, MOE_PER)

                    def one(e, it=None):
                        k = s.k + 4 + 6 * e
                        expert_in(k, u + 3 * (e + 1), it)
                        down(u + 3 * e, k + 4, e == 0, False, it)
                        expert_tr(u + 3 * (e + 1), it)

                    pe.wait_ge(x_lo, nx)
                    expert_in(s.k, u)
                    expert_tr(u)
                    for e in range(3):
                        one(e)
                    with pe.Fori(0, 7) as it:
                        for e in range(3, 7):
                            one(e, it)
                    down(u + 3 * (EXPERTS - 1), s.k + s.nk - 2, False, True)
                elif s.name == "sb":
                    h, layer_sb = a, s.sb
                    if h == 0:
                        for x in steps:
                            if x.name in ("tblk", "nblk") and x.arg[0][0] == "s" and x.sb == layer_sb:
                                for q in range(x.nu):
                                    done_wait(pe, x.u + q)
                        mixed = []
                    if h < SBH:
                        r, c = 64 * (h % 2), h // 2
                        begin(u)
                        mm(bank(u)[:, 0:S], KT[r:r + 64, c, 0:P], QT[r:r + 64, c, :], True, True)
                        fin(mm(bank(u)[:, S:S + P], KT[r:r + 64, c, P:S], QT[r:r + 64, c, P:S], False,
                               True, skip_group_check=True), u)
                    if 1 <= h <= SBH:
                        g = (h - 1) % 2
                        pe.wait_ge(pool_masked, masks(h - 1, layer_sb))
                        b = bank(z_prev)
                        mm(b[:, 0:S], cst("neg_ge"), SPM[:, g, 0:S], False, True, skip_group_check=True)
                        mm(b[:, P:S], cst("neg_one"), SPM[:, g, S:S + P], False, True, skip_group_check=True)
                        mm(b[:, S:S + P], cst("neg_ge"), SPM[:, g, S:S + P], False, True,
                           skip_group_check=True).then_inc(z_full, 1)
                    if h < SBH:
                        z_prev = u
                    if h >= 2 and h % 2 == 1:
                        v = s.u + s.nu - 1
                        mixed.append(v)
                        begin(v)
                        for hh in (h - 3, h - 2):
                            pe.wait_ge(pool_masked, weights(hh, layer_sb))
                            o = bank(v)[64 * (hh % 2):64 * (hh % 2) + 64, :]
                            mm(o[:, 0:S], VT[:, 0, 64 * hh:64 * hh + 64], WM[:, hh % 4, 0:S], True, False)
                            ins = mm(o[:, P:S], VT[:, 1, 64 * hh:64 * hh + 64], WM[:, hh % 4, S:S + P],
                                     False, True)
                        fin(ins, v)
                elif s.name == "galow":
                    pe.wait_ge(x_lo, nx)
                    hear_dve()
                    begin(u)
                    for kc in range(KC):
                        ins = mm(bank(u)[0:16, 0:S], SMW[:, kc, 44:60], XF[:, kc, :], kc == 0, kc == 7)
                    fin(ins, u)
                    done_wait(pe, u)
                    for t in range(NT):
                        begin(u + 1 + t)
                        fin(mm(bank(u + 1 + t)[:], ALT[0:17, t * P:t * P + P], GUP[:]), u + 1 + t)
                    galow = u
                elif s.name == "gcum":
                    for t in range(NT):
                        done_wait(pe, galow + 1 + t)
                    for q in range(2):
                        begin(u + q)
                        for h in (2 * q, 2 * q + 1):
                            for t in range(NT):
                                ins = mm(bank(u + q)[:, (h % 2) * S + t * P:(h % 2) * S + t * P + P],
                                         LG[:, t, h * P:h * P + P], TRI)
                        fin(ins, u + q)
                    begin(u + 2)
                    fin(mm(bank(u + 2)[:], cst("after"), LG[:, 0, :]), u + 2)
                    begin(u + 3)
                    for x in steps:
                        if x.name == "tblk" and x.arg[0] == "gk":
                            done_wait(pe, x.u)
                    for h in range(GH):
                        ins = tr(bank(u + 3)[:, h * P:h * P + P], GK[:, h, 0:P])
                    fin(ins, u + 3)
                elif s.name == "gscore":
                    hear_dve()
                    begin(u)
                    begin(u + 1)
                    for b in range(4):
                        hear_dve()
                        for t in range(NT):
                            for h in range(GH):
                                ins = mm(bank(u + t)[:, h * P + GSUB * b:h * P + GSUB * b + GSUB],
                                         KBB[:, b % 2, h, t * P:t * P + P],
                                         QGL[:, h, t * P + GSUB * b:t * P + GSUB * b + GSUB])
                            if b == 3:
                                fin(ins, u + t)
                        if b < 3:
                            ins.then_inc(z_full, 1)
                    gscore = u
                elif s.name == "gout":
                    hear_dve()
                    for x in steps:
                        if x.name == "nblk" and x.arg[0] == "gv":
                            for q in range(2):
                                done_wait(pe, x.u + q)
                    for q in range(2):
                        begin(u + q)
                        for h in (2 * q, 2 * q + 1):
                            ins = mm(bank(u + q)[:, (h % 2) * 256:(h % 2) * 256 + 256],
                                     KDG[:, h * P:h * P + P], GV[:, 0, 256 * h:256 * h + 256])
                        fin(ins, u + q)
                    for q in range(4):
                        t = q // 2
                        if q % 2 == 0:
                            done_wait(pe, gscore + t)
                        if q == 2:
                            done_wait(pe, u)
                            done_wait(pe, u + 1)
                        begin(u + 2 + q)
                        for h in (2 * (q % 2), 2 * (q % 2) + 1):
                            o = bank(u + 2 + q)[:, (h % 2) * 256:(h % 2) * 256 + 256]
                            if t:
                                mm(o, QI[:, h, :], S1G[:, h, :], True, False)
                            ins = mm(o, STT[:, t, h, :], GV[:, t, 256 * h:256 * h + 256], t == 0, True)
                        fin(ins, u + 2 + q)
                elif s.name == "ffn":
                    def up(b, k, ub, it=None):
                        rows_by_cols(XT, k, ub, it=it, per=FFN_PER)

                    def hid_tr(ub, nh, it=None):
                        eu = 0 if it is None else it * FFN_PER["unit"]
                        for t in range(NT):
                            pe.wait_ge(hid_ready, (0 if it is None else it * NT) + (nh + t + 1))
                            begin(ub + 2 + t, eu)
                            for c in range(4):
                                ins = tr(bank(ub + 2 + t)[:, c * P:c * P + P], HID[:, t, c * P:c * P + P])
                            fin(ins, ub + 2 + t)

                    def down(ub, k, first, last, it=None):
                        eu = 0 if it is None else it * FFN_PER["unit"]
                        done_wait(pe, ub + 2, eu)
                        done_wait(pe, ub + 3, eu)
                        rows_acc(OT, range(4), k, first, last, it, FFN_PER)

                    def one(b, it=None):
                        k = s.k + 4 + 8 * b
                        up(b + 1, k, u + 4 * (b + 1), it)
                        down(u + 4 * b, k + 4, b == 0, False, it)
                        hid_tr(u + 4 * (b + 1), nhid + NT * (b + 1), it)

                    pe.wait_ge(x_lo, nx)
                    up(0, s.k, u)
                    hid_tr(u, nhid)
                    one(0)
                    with pe.Fori(0, FBLK - 2) as it:
                        one(1, it)
                    down(u + 4 * (FBLK - 1), s.k + s.nk - 4, False, True)
                    nhid += NT * FBLK
                if s.name == "tblk" and a[0] == "cb":
                    nx += 1

        @block.vector
        def _(dve):
            chain = n_a2d = n_d2a = n_d2p = n_hi = nx = nvar = nacc = ngb = nz = 0
            cu_units, cc_units, delta = {}, {}, {}

            def link(ins):
                nonlocal chain
                chain += 1
                return ins.then_inc(dve_chain, 1)

            def sync():
                dve.wait_ge(dve_chain, chain)

            def tell_act(ins):
                nonlocal n_d2a
                n_d2a += 1
                ins.then_inc(d2a, 1)

            def tell_pe(ins):
                nonlocal n_d2p
                n_d2p += 1
                ins.then_inc(d2p, 1)

            def hear_act(n=1):
                nonlocal n_a2d
                n_a2d += n
                dve.wait_ge(a2d, n_a2d)

            split = Splitter(make_lo)

            def v2(u):
                return bank(u)[:].rearrange("p (a b) -> p a b", a=2)

            def v4(u):
                return bank(u)[:].rearrange("p (a b) -> p a b", a=4)

            def free(ins, u):
                return ins.then_inc(done[u % WB], 1)

            def ev_lo(u, dst, hi, src, extra=0):
                nonlocal n_hi
                n_hi += 1
                dve.wait_ge(hi_out, extra + n_hi)
                free(dve.tensor_tensor(dst, src, hi.bitcast(F32), ALU.subtract), u)

            def x_rest(j, hi, lo):
                nonlocal nx
                nx += 1
                dve.wait_ge(x_hi, nx)
                dve.tensor_tensor(lo[:, 2 * j:2 * j + 2, :], XF[:, 2 * j:2 * j + 2, :],
                                  hi[:, 2 * j:2 * j + 2, :].bitcast(F32), ALU.subtract).then_inc(x_lo, 1)

            def sum_sq(col, x, junk):
                return dve.tensor_tensor_reduce(junk, x, x, 1.0, 0.0, ALU.mult, ALU.add,
                                                accum_out=SS[:, col:col + 1])

            def inv_rms(n, scale):
                nonlocal nvar
                nvar += 1
                dve.tensor_scalar(VAR[:, 0:n], SS[:, 0:n], scale, EPS, ALU.mult, ALU.add)\
                    .then_inc(var_ready, 1)

            def rs_wait():
                dve.wait_ge(rs_ready, nvar)

            def gb_row():
                nonlocal ngb
                dve.wait_ge(gb_loaded[ngb % 2], 16 * (ngb // 2 + 1))
                ngb += 1
                return GB[:, (ngb - 1) % 2, :]

            def col(v, n, w):
                return v.unsqueeze(2).broadcast_to([P, n, w])

            dve.wait_ge(load_const, 16 * NCONST)
            for s in steps:
                u, a = s.u, s.arg
                if s.name in ("tblk", "mod", "nblk", "up", "wout"):
                    split.upto(s.k + s.nk + SPL)
                if s.name == "params":
                    full_wait(dve, u)
                    free(dve.tensor_copy(COLP[:], bank(u)[:, 0:ROWS1 + ROWS2]), u)
                    rel_set = chain + 1
                    link(dve.memset(REL[32:33, :], 1.0))
                    link(dve.memset(VAR[:], 1.0))
                    link(dve.memset(MH[:], -0.5))
                    link(dve.memset(PRE[:, :, 0:3], 0.0))
                elif s.name == "cond":
                    hear_act()
                    tell_act(dve.tensor_copy(XF[:, :, 0:P], col(CC[:, 2, :], KC, P)))
                    nx += 1
                    dve.wait_ge(x_hi, nx)
                    dve.tensor_tensor(OTl[:, :, 0:P], XF[:, :, 0:P], OTh[:, :, 0:P].bitcast(F32),
                                      ALU.subtract).then_inc(x_lo, 1)
                elif s.name == "mod":
                    sec, half = divmod(a, 2)
                    j, kind = divmod(sec, 3)
                    full_wait(dve, u)
                    if kind == 2:
                        dve.wait_ge(gb_loaded[j], 16)
                        g = GB[:, j, 512 * half:512 * half + 512]
                        free(dve.tensor_tensor(g, bank(u)[:], g, ALU.add), u)
                    else:
                        row = 4 if kind else 2 * j
                        mc = MODC[:, row, 4 * half:4 * half + 4]
                        for i in range(4):
                            ins = dve.tensor_tensor_reduce(
                                area(4096, 4, P)[:, i, :], bank(u)[:, i * P:i * P + P], IDENT, 1.0, 0.0,
                                ALU.mult, ALU.add, accum_out=mc[:, i:i + 1])
                        free(ins, u)
                        done_wait(dve, u)
                        bm = COLP[:, R_BM + 8 * sec + 4 * half:][:, 0:4]
                        link(dve.tensor_tensor(mc, mc, bm, ALU.add))
                        if kind == 1:
                            sync()
                            nw = COLP[:, (R_N1, R_N2)[j] + 4 * half:][:, 0:4]
                            ins = dve.scalar_tensor_tensor(MODC[:, 2 * j + 1, 4 * half:4 * half + 4],
                                                           mc, 1.0, nw, ALU.add, ALU.mult)
                            if half:
                                tell_act(ins)
                elif s.name == "norm":
                    for t in range(NT):
                        link(sum_sq(t, H[:, t, :], XS[:, t, :]))
                    sync()
                    inv_rms(2, 1.0 / D)
                    rs_wait()
                    dve.tensor_scalar(XS[:, 0, :], H[:, 0, :], RS[:, 0:1], None, ALU.mult)
                    tell_pe(dve.tensor_scalar(XS[:, 1, :], H[:, 1, :], RS[:, 1:2], None, ALU.mult))
                    for q in range(4):
                        x_rest(q, XTh, XTl)
                elif s.name == "bias":
                    dve.wait_ge(dve_chain, rel_set)
                    tell_pe(dve.tensor_copy(RB[:], REL[:].unsqueeze(2).broadcast_to([33, HA, P])))
                elif s.name == "ba":
                    full_wait(dve, u)
                    ba = bank(u)[:, 0:16].rearrange("p (t k h) -> p t k h", t=2, k=2)
                    dt = over(SROW[:, S_DT:S_DT + 4], 2)
                    link(dve.tensor_copy(BT[:, 0, :].rearrange("p (t h) -> p t h", t=2), ba[:, :, 0, :]))
                    free(dve.tensor_tensor(BT[:, 1, :].rearrange("p (t h) -> p t h", t=2),
                                           ba[:, :, 1, :], dt, ALU.add), u)
                    done_wait(dve, u)
                    tell_act(dve.tensor_scalar(BT[:, 7, :], BT[:, 1, :], 0.0, None, ALU.max))
                    hear_act()
                    link(dve.tensor_scalar(BT[:, 2, :], BT[:, 2, :], 1.0, None, ALU.add))
                    link(dve.tensor_tensor(BT[:, 7, :], BT[:, 7, :], BT[:, 5, :], ALU.add))
                    sync()
                    link(dve.reciprocal(BT[:, 2, :], BT[:, 2, :]))
                    link(dve.scalar_tensor_tensor(
                        BT[:, 7, :].rearrange("p (t h) -> p t h", t=2),
                        BT[:, 7, :].rearrange("p (t h) -> p t h", t=2), -1.0,
                        over(BT[:, 6, 0:4], 2), ALU.mult, ALU.mult))
                elif s.name == "conv_b":
                    for x in steps:
                        if x.name == "tblk" and x.arg[0] == "pre":
                            done_wait(dve, x.u)
                    for q in range(3):
                        for tap in range(4):
                            for ch in range(4 * q, 4 * q + 4):
                                w = COLP[:, R_CW + 12 * tap + ch:][:, 0:1]
                                src = PRE[:, ch, tap:tap + S]
                                if tap == 0:
                                    ins = dve.tensor_scalar(POST[:, ch, :], src, w, None, ALU.mult)
                                else:
                                    ins = dve.scalar_tensor_tensor(POST[:, ch, :], src, w,
                                                                   POST[:, ch, :], ALU.mult, ALU.add)
                            if tap < 3:
                                link(ins)
                                sync()
                            else:
                                tell_act(ins)
                elif s.name == "dtok":
                    for q in range(4):
                        done_wait(dve, u + q)
                        for h in range(HB):
                            link(sum_sq(4 * q + h, TOK[:, q // 2, q % 2, h * P:h * P + P],
                                        area(9252, 16, P)[:, 4 * q + h, :]))
                    sync()
                    inv_rms(16, 1.0)
                    for q in range(4, 6):
                        done_wait(dve, u + q)
                elif s.name == "decay":
                    sync()
                    tell_pe(dve.tensor_copy(NTL[:], col(BT[:, 7, :], 8, P)))
                    rs_wait()
                    link(dve.tensor_scalar(RS[:, 0:8], RS[:, 0:8], float(P) ** -0.5, None, ALU.mult))
                    hear_act()
                    free(dve.tensor_copy(GC[:], bank(u)[:, 0:24]), u)
                    done_wait(dve, u)
                elif s.name == "decay_rows":
                    for t in range(NT):
                        full_wait(dve, u + t)
                        if t == 1:
                            hear_act()
                        for h in range(HB):
                            m = 4 * t + h
                            ins = dve.tensor_scalar(DTI[:, m, :], bank(u + t)[:, h * P:h * P + P],
                                                    GC[:, m:m + 1], 0.0, ALU.subtract, ALU.min)
                        free(ins, u + t)
                elif s.name == "dtr":
                    k8 = TOK[:, 1, :, :].rearrange("p t (h d) -> p (t h) d", h=HB)
                    q8 = TOK[:, 0, :, :].rearrange("p t (h d) -> p (t h) d", h=HB)
                    v8 = TOK[:, 2, :, :].rearrange("p t (h d) -> p (t h) d", h=HB)
                    kb8 = KBK[:].rearrange("p t (h d) -> p (t h) d", h=HB)

                    def heads(v):
                        return v.rearrange("p (h d) -> p h d", h=HB)

                    tell_pe(dve.tensor_tensor(k8, k8, col(RS[:, 8:16], 8, P), ALU.mult))
                    dve.wait_ge(d2p, n_d2p)
                    tell_pe(dve.tensor_tensor(kb8, k8, col(BT[:, 2, :], 8, P), ALU.mult))
                    tell_pe(dve.tensor_tensor(q8, q8, col(RS[:, 0:8], 8, P), ALU.mult))
                    dve.wait_ge(d2p, n_d2p)
                    link(dve.tensor_tensor(heads(KBG), kb8[:, 4:8, :], col(EG[:, 4:8], 4, P), ALU.mult))
                    link(dve.tensor_tensor(heads(KD), k8[:, 0:4, :], col(EG[:, 8:12], 4, P), ALU.mult))
                    link(dve.tensor_tensor(v8, v8, col(BT[:, 2, :], 8, P), ALU.mult))
                    hear_act()
                    link(dve.tensor_tensor(DTI, DTI, over(TRI, 8), ALU.mult))
                    sync()
                    link(dve.tensor_tensor(DTS, DTI, over(cst("strict"), 8), ALU.mult))
                    link(dve.tensor_copy(XI, over(IDENT, 8)))
                    link(dve.tensor_copy(XTI, over(IDENT, 8)))
                    qnt_units = (u + 4, u + 5)
                elif s.name == "dmat":
                    sync()
                    for q in range(4):
                        kind, t = divmod(q, 2)
                        full_wait(dve, u + q)
                        dst, dec = (PTM, DTI) if kind else (NMT, DTS)
                        free(dve.tensor_tensor(dst[:, 4 * t:4 * t + 4, :], v4(u + q),
                                               dec[:, 4 * t:4 * t + 4, :], ALU.mult), u + q)
                    done_wait(dve, qnt_units[1])
                    done_wait(dve, u + 1)
                    link(dve.tensor_tensor(QGT.rearrange("p (h d) -> p h d", h=HB), QNT[:, 1],
                                           ER.rearrange("p (h d) -> p h d", h=HB), ALU.mult))
                elif s.name == "inv_y":
                    sync()
                    tell_pe(dve.tensor_tensor(NTL, NMT, over(cst("levels")[:, P * a:P * a + P], 8), ALU.mult))
                elif s.name == "inv_x":
                    for q in range(s.nu):
                        dst = XI if s.nu == 4 and q < 2 else XTI
                        d = dst[:, 4 * (q % 2):4 * (q % 2) + 4, :]
                        full_wait(dve, u + q)
                        if q % 2 == 0 and q == s.nu - 2:
                            full_wait(dve, u + q + 1)
                        free(dve.tensor_tensor(d, d, v4(u + q), ALU.subtract), u + q)
                    done_wait(dve, u + s.nu - 1)
                elif s.name == "du":
                    delta["du"] = u
                elif s.name == "dnew":
                    full_wait(dve, u)
                    done_wait(dve, delta["du"] + 1)
                    free(dve.tensor_tensor(VNW.rearrange("p (h d) -> p h d", h=HB), UI[:, 4:8, :],
                                           v4(u), ALU.subtract), u)
                    delta["dnew"] = u
                elif s.name == "dyt":
                    for x in steps:
                        if x.name == "nblk" and x.arg[0] == "z":
                            zu = x.u
                        if x.name == "dstate":
                            du0 = x.u
                        if x.name == "dout":
                            do = x.u
                    done_wait(dve, zu)
                    done_wait(dve, zu + 1)
                    z8 = ZS[:].rearrange("p t (h d) -> p (t h) d", h=HB)
                    link(dve.tensor_tensor(z8, z8, over(SROW[:, S_ON:S_ON + P], 8), ALU.mult))
                    done_wait(dve, du0)
                    done_wait(dve, do)
                    sync()
                    for t in range(NT):
                        for h in range(HB):
                            link(sum_sq(4 * t + h, OB[:, t, h * P:h * P + P], YI[:, 4 * t + h, :]))
                    sync()
                    inv_rms(8, 1.0 / P)
                    rs_wait()
                    for t in range(NT):
                        for h in range(HB):
                            o = OB[:, t, h * P:h * P + P]
                            ins = dve.scalar_tensor_tensor(o, o, RS[:, 4 * t + h:4 * t + h + 1],
                                                           ZS[:, t, h * P:h * P + P], ALU.mult, ALU.mult)
                    tell_pe(ins)
                    for q in range(2):
                        ev_lo(u + q, OTl[:, 4 + 2 * q:6 + 2 * q, :], OTh[:, 4 + 2 * q:6 + 2 * q, :], v2(u + q))
                elif s.name == "moba":
                    n = a
                    if n == 0:
                        dve.wait_ge(bias_read, 32)
                    if n < 16:
                        h, t = divmod(n, 2)
                        kk = P * (t + 1)
                        full_wait(dve, u)
                        free(dve.scalar_tensor_tensor(MS_[:, n % 2, 0:kk], bank(u)[:, 0:kk], HDA ** -0.5,
                                                      BIAS[:, h, t, 0:kk], ALU.mult, ALU.add), u)
                        done_wait(dve, u)
                        tell_act(dve.tensor_reduce(SS[:, n % 2:n % 2 + 1], MS_[:, n % 2, 0:kk], AX, ALU.max,
                                                   negate=True))
                    if 1 <= n <= 16:
                        g, kk = (n - 1) % 2, P * ((n - 1) % 2 + 1)
                        hear_act()
                        link(dve.reciprocal(RS2[:, g:g + 1], RS2[:, g:g + 1]))
                        sync()
                        tell_pe(dve.tensor_scalar(MP[:, g, 0:kk], MP[:, g, 0:kk], RS2[:, g:g + 1],
                                                  None, ALU.mult))
                    if n >= 2 and (n - 2) % 4 == 3:
                        v, c = s.u + s.nu - 1, (n - 2) // 4
                        ev_lo(v, OTl[:, c, :], OTh[:, c, :], bank(v)[:, 0:S])
                elif s.name == "up":
                    if a == 0:
                        for x in steps:
                            if x.name == "tblk" and x.arg[0] in ("ga", "gb"):
                                done_wait(dve, x.u)
                    full_wait(dve, u)
                    free(dve.tensor_tensor(MTMP, v2(u), SGA[:, 2 * a:2 * a + 2, :], ALU.mult), u)
                    full_wait(dve, u + 1)
                    xp = XF[:, 2 * a:2 * a + 2, :]
                    free(dve.tensor_tensor(xp, v2(u + 1), SGB[:, 2 * a:2 * a + 2, :], ALU.mult), u + 1)
                    done_wait(dve, u)
                    done_wait(dve, u + 1)
                    dve.tensor_tensor(xp, xp, MTMP, ALU.add).then_inc(xf_ready, 1)
                    x_rest(a, XTh, XTl)
                elif s.name in ("res1", "res2"):
                    nacc += 1
                    dve.wait_ge(acc_full, nacc)
                    row = gb_row()
                    for b in range(4):
                        t, c = divmod(b, 2)
                        dve.tensor_tensor(XS[:, t, 512 * c:512 * c + 512], ACC[:, b, :],
                                          row[:, 512 * c:512 * c + 512], ALU.mult).then_inc(acc_free, 1)
                    for t in range(NT):
                        dve.wait_ge(acc_free, 4 * nacc - 2 + 2 * t)
                        ins = dve.tensor_tensor(H[:, t, :], H[:, t, :], XS[:, t, :], ALU.add)
                        if t == 0:
                            link(ins)
                    ins.then_inc(gb_free, 1)
                    dve.wait_ge(gb_free, ngb)
                    if s.name == "res2":
                        for t in range(NT):
                            link(sum_sq(t, H[:, t, :], XS[:, t, :]))
                        sync()
                        inv_rms(2, 1.0 / D)
                        rs_wait()
                        row = gb_row()
                        for t in range(NT):
                            ins = dve.scalar_tensor_tensor(H[:, t, :], H[:, t, :], RS[:, t:t + 1], row,
                                                           ALU.mult, ALU.mult)
                        ins.then_inc(gb_free, 1)
                        dve.wait_ge(gb_free, ngb)
                elif s.name == "router":
                    def r(c0, c1=None):
                        return RT[:, :, c0:c0 + 1 if c1 is None else c1]

                    def wide(c, w):
                        return r(c).broadcast_to([P, NT, w])

                    def op(o, x, y, f):
                        sync()
                        return link(dve.tensor_tensor(o, x, y, f))

                    def top(values, at_max, idx, onehot, w):
                        iota = over(cst("iota")[:, 0:w], NT)
                        sync()
                        link(dve.tensor_reduce(r(at_max), values, AX, ALU.max))
                        op(r(112, 112 + w), values, wide(at_max, w), ALU.is_lt)
                        sync()
                        link(dve.scalar_tensor_tensor(r(112, 112 + w), r(112, 112 + w), 8.0, iota,
                                                      ALU.mult, ALU.add))
                        sync()
                        link(dve.tensor_reduce(r(idx), r(112, 112 + w), AX, ALU.min))
                        op(onehot, iota, wide(idx, w), ALU.is_equal)

                    full_wait(dve, u)
                    free(dve.tensor_tensor(r(0, 36), bank(u)[:, 0:128].rearrange("p (t w) -> p t w", t=2)[:, :, 0:36],
                                           over(SROW[:, S_BR:S_BR + 36], NT), ALU.add), u)
                    done_wait(dve, u)
                    top(r(0, 4), 36, 52, r(48, 52), 4)
                    tell_act(dve.tensor_scalar(r(37), r(36), -1.0, None, ALU.mult))
                    for g in range(NG):
                        le = r(4 + 8 * g, 12 + 8 * g)
                        if g == 0:
                            op(r(56, 64), le, wide(48, 8), ALU.mult)
                        else:
                            op(r(120, 128), le, wide(48 + g, 8), ALU.mult)
                            op(r(56, 64), r(56, 64), r(120, 128), ALU.add)
                    top(r(56, 64), 64, 66, r(72, 80), 8)
                    sync()
                    link(dve.scalar_tensor_tensor(r(88, 96), r(72, 80), 2 * NEG, r(56, 64), ALU.mult, ALU.add))
                    top(r(88, 96), 65, 67, r(80, 88), 8)
                    sync()
                    tell_act(dve.tensor_tensor(r(97), r(65), r(64), ALU.subtract))
                    hear_act(3)
                    link(dve.reciprocal(r(45), r(44)))
                    sync()
                    link(dve.tensor_scalar(r(99), r(98), 1.0, None, ALU.add))
                    sync()
                    link(dve.reciprocal(r(100), r(99)))
                    op(r(101), r(100), r(45), ALU.mult)
                    op(r(102), r(101), r(98), ALU.mult)
                    op(r(104, 112), r(72, 80), wide(101, 8), ALU.mult)
                    op(r(120, 128), r(80, 88), wide(102, 8), ALU.mult)
                    op(r(104, 112), r(104, 112), r(120, 128), ALU.add)
                    for g in range(NG):
                        op(COMB[:, :, 8 * g:8 * g + 8], r(104, 112), wide(48 + g, 8), ALU.mult)
                    sync()
                elif s.name == "moe":
                    def gated(e, ub, it=None):
                        extra = 0 if it is None else 8 * it
                        for t in range(NT):
                            dve.wait_ge(a2d, extra + (n_a2d + 2 * e + t + 1))
                            if it is None:
                                wt = COMB[:, t, e:e + 1]
                            else:
                                wt = COMB[:, t, bass.ds(4 * it + e, 1)]
                            free(dve.scalar_tensor_tensor(AE[:, t, :], SG[:, t, :], wt,
                                                          bank(ub + t)[:, 256:512], ALU.mult, ALU.mult), ub + t)

                    def t_lo(ut, extra=0):
                        ev_lo(ut, OTl[:, 0:2, :], OTh[:, 0:2, :], v2(ut), extra)

                    def one(e, k, ub, it=None):
                        for kk in (k + 4, k + 5):
                            make_lo(kk, it, MOE_PER)
                        gated(e + 1, ub, it)
                        for kk in range(k + 6, k + 10):
                            make_lo(kk, it, MOE_PER)
                        t_lo(ub + 2, 0 if it is None else 4 * it)

                    split.upto(s.k + 4)
                    gated(0, u)
                    split.upto(s.k + 8)
                    t_lo(u + 2)
                    for e in range(3):
                        one(e, s.k + 4 + 6 * e, u + 3 * (e + 1))
                    with dve.Fori(0, 7) as it:
                        for e in range(3, 7):
                            one(e, s.k + 4 + 6 * e, u + 3 * (e + 1), it)
                    n_hi += 4 * 6
                    split.next = s.k + s.nk + 2
                    n_a2d += 2 * EXPERTS
                elif s.name == "post":
                    nacc += 1
                    hear_act()
                    ss = SS[:, 8:12].rearrange("p (t c) -> p t c", c=2)
                    link(dve.tensor_tensor(SS[:, 0:2].unsqueeze(2), ss[:, :, 0:1], ss[:, :, 1:2], ALU.add))
                    sync()
                    inv_rms(2, 1.0 / D)
                    row = gb_row()
                    rs_wait()
                    for b in range(4):
                        t, c = divmod(b, 2)
                        dve.scalar_tensor_tensor(XS[:, t, 512 * c:512 * c + 512], ACC[:, b, :],
                                                 RS[:, t:t + 1], row[:, 512 * c:512 * c + 512],
                                                 ALU.mult, ALU.mult).then_inc(acc_free, 1)
                    for t in range(NT):
                        dve.wait_ge(acc_free, 4 * nacc - 2 + 2 * t)
                        ins = dve.tensor_tensor(H[:, t, :], H[:, t, :], XS[:, t, :], ALU.add)
                        if t == 0:
                            link(ins)
                    if a == ("ffn", 3):
                        ins.then_inc(h_final, 1)
                    else:
                        ins.then_inc(gb_free, 1)
                        dve.wait_ge(gb_free, ngb)
                elif s.name == "ffn":
                    def square(ub, extra=0):
                        for t in range(NT):
                            done_wait(dve, ub + t, extra)
                            dve.tensor_tensor(HID[:, t, :], HID[:, t, :], HID[:, t, :], ALU.mult)\
                                .then_inc(hid_ready, 1)

                    def t_lo(ut, extra=0):
                        for t in range(NT):
                            tt = slice(t * P, t * P + P)
                            ev_lo(ut + t, OTl[:, 0:4, tt], OTh[:, 0:4, tt], v4(ut + t), extra)

                    def one(b, k, ub, it=None):
                        for kk in range(k + 4, k + 8):
                            make_lo(kk, it, FFN_PER)
                        square(ub, 0 if it is None else it * FFN_PER["unit"])
                        for kk in range(k + 8, k + 12):
                            make_lo(kk, it, FFN_PER)
                        t_lo(ub + 2, 0 if it is None else 2 * it)

                    split.upto(s.k + 4)
                    square(u)
                    split.upto(s.k + 8)
                    t_lo(u + 2)
                    one(0, s.k + 4, u + 4)
                    with dve.Fori(0, FBLK - 2) as it:
                        one(1, s.k + 12, u + 8, it)
                    n_hi += 2 * (FBLK - 3)
                    split.next = s.k + s.nk
                elif s.name == "sb":
                    h = a
                    if h < SBH:
                        hear_act()
                        dve.scalar_tensor_tensor(SPB[:, h % 2, :], bank(u)[:, 0:384], 0.0, LN[:, h % 2, :],
                                                 ALU.max, ALU.add).then_inc(logs_ready, 1)
                    if 1 <= h <= SBH:
                        zu = z_prev
                        nz += 1
                        dve.wait_ge(z_full, nz)
                        free(dve.tensor_scalar(WX[:, (h - 1) % 4, :], bank(zu)[:, 0:384], 0.0, None,
                                               ALU.min), zu)
                    if h < SBH:
                        z_prev = u
                    if h >= 2 and h % 2 == 1:
                        v, c = s.u + s.nu - 1, (h - 3) // 2
                        ev_lo(v, OTl[:, c, :], OTh[:, c, :], bank(v)[:, 0:S])
                elif s.name == "tblk":
                    kind, c = a
                    if kind == "cc":
                        cc_units[c] = u
                        if c == 0:
                            link(dve.memset(HP[:, :, 0:2], 0.0))
                    elif kind == "cu":
                        done_wait(dve, cc_units[c])
                        full_wait(dve, u)
                        free(dve.tensor_tensor(HP[:, 2 * c:2 * c + 2, 2:2 + S], v2(u),
                                               CB[:, 2 * c:2 * c + 2, :], ALU.mult), u)
                        cu_units[c] = u
                    elif kind == "cb":
                        if c == 0:
                            sync()
                        done_wait(dve, cu_units[c])
                        for tap in range(3):
                            for i in range(2):
                                ch = 2 * c + i
                                w = COLP[:, R_CW2 + 8 * tap + ch:][:, 0:1]
                                src = HP[:, ch, tap:tap + S]
                                if tap == 0:
                                    ins = dve.tensor_scalar(CV[:, i, :], src, w, None, ALU.mult)
                                else:
                                    ins = dve.scalar_tensor_tensor(CV[:, i, :], src, w, CV[:, i, :],
                                                                   ALU.mult, ALU.add)
                            link(ins)
                            sync()
                        full_wait(dve, u)
                        free(dve.tensor_tensor(XF[:, 2 * c:2 * c + 2, :], v2(u), CV, ALU.mult), u)
                        x_rest(c, OTh, OTl)
                elif s.name == "galow":
                    tell_pe(dve.memset(ALT[0:17, :], 1.0))
                    for t in range(NT):
                        hear_act()
                        free(dve.scalar_tensor_tensor(LG[:, t, :], bank(u + 1 + t)[:], 0.0, GTM[:, t, :],
                                                      ALU.min, ALU.subtract), u + 1 + t)
                elif s.name == "gcum":
                    link(dve.memset(REF[:, :, 0:1], 0.0))
                    done_wait(dve, u)
                    done_wait(dve, u + 1)
                    cum8 = CUM[:].rearrange("p h (t i) -> p (h t) i", t=NT)
                    link(dve.tensor_copy(REF[:, :, 1:4], cum8[:, :, GSUB - 1:P - 1:GSUB]))
                elif s.name == "gscore":
                    sync()
                    cum32 = CUM[:].rearrange("p h (b i) -> p (h b) i", i=GSUB)
                    ref32 = REF[:].rearrange("p a b -> p (a b)")
                    qgl = QGL[:].rearrange("p h (b i) -> p (h b) i", i=GSUB)
                    tell_act(dve.tensor_tensor(qgl, cum32, col(ref32, 32, GSUB), ALU.subtract))

                    def keys(b):
                        kb = KBB[:, b % 2].rearrange("p h (t i) -> p (h t) i", t=NT)
                        link(dve.tensor_tensor(kb, cum8, REF[:, :, b:b + 1].broadcast_to([P, GH * NT, P]),
                                               ALU.subtract))
                        sync()
                        tell_act(dve.tensor_scalar(kb, kb, -GCLAMP, None, ALU.max))

                    hear_act()
                    link(dve.tensor_tensor(QI, QI, GQ[:, :, P:S], ALU.mult))
                    keys(0)
                    hear_act()
                    tell_pe(dve.tensor_tensor(QGL, QGL, GQ, ALU.mult))
                    keys(1)
                    for b in range(4):
                        hear_act()
                        tell_pe(dve.tensor_tensor(KBB[:, b % 2], KBB[:, b % 2], GK, ALU.mult))
                        if b < 3:
                            nz += 1
                        if b < 2:
                            dve.wait_ge(z_full, nz)
                            keys(b + 2)
                    for x in steps:
                        if x.name == "gcum":
                            done_wait(dve, x.u + 2)
                            done_wait(dve, x.u + 3)
                    tell_pe(dve.tensor_tensor(KDG, KTK, ES, ALU.mult))
                    for t in range(NT):
                        full_wait(dve, u + t)
                        free(dve.tensor_tensor(STT[:, t], v4(u + t), over(TRI, 4), ALU.mult), u + t)
                elif s.name == "gout":
                    gout_units = u
                    row = gb_row()
                    for x in steps:
                        if x.name == "nblk" and x.arg[0] == "gg":
                            done_wait(dve, x.u)
                            done_wait(dve, x.u + 1)
                    for t in range(NT):
                        ins = dve.tensor_tensor(GG[:, t, :], GG[:, t, :], row, ALU.mult)
                    ins.then_inc(gb_free, 1)
                elif s.name == "gyt":
                    for q in range(4):
                        done_wait(dve, gout_units + 2 + q)
                    for t in range(NT):
                        for h in range(GH):
                            link(sum_sq(4 * t + h, XS[:, t, 256 * h:256 * h + 256],
                                        area(0, 8, 256)[:, 4 * t + h, :]))
                    sync()
                    inv_rms(8, 1.0 / 256)
                    rs_wait()
                    dve.wait_ge(gb_free, ngb)
                    for t in range(NT):
                        for h in range(GH):
                            o = XS[:, t, 256 * h:256 * h + 256]
                            ins = dve.scalar_tensor_tensor(o, o, RS[:, 4 * t + h:4 * t + h + 1],
                                                           GG[:, t, 256 * h:256 * h + 256],
                                                           ALU.mult, ALU.mult)
                    tell_pe(ins)
                    for q in range(4):
                        ev_lo(u + q, OTl[:, 2 * q:2 * q + 2, :], OTh[:, 2 * q:2 * q + 2, :], v2(u + q))


def pack(i):
    win = i["w_in"][0]
    gains = i["norm_gains_2"]
    steps = schedule()
    prows = np.concatenate([
        i["norm1_w"].reshape(8, P), i["norm2_w"].reshape(8, P), i["b_mod"].reshape(48, P),
        np.stack([gains[:, 0], gains[:, 2]], axis=1).reshape(64, P),
        i["conv_w"].reshape(48, P), i["conv_w_2"].reshape(24, P)])
    bm = i["b_mod"].reshape(6, D)
    smw = np.concatenate([win[:, C_BA:C_BA + 8], i["w_rg"][0], i["w_re"][0],
                          i["gla_w_in_2"][0][:, 3 * D:3 * D + 16]], axis=1)
    return {k: np.ascontiguousarray(v) for k, v in {
        "x": i["x"], "weights": weight_tiles(i, steps), "cst": constants()[0], "prows": prows,
        "c": i["c"],
        "srow": np.concatenate([i["dt_bias"].ravel(), i["a_log"].ravel(), i["b_rg"].ravel(),
                                i["b_re"].ravel(), i["onorm_w"].ravel()]),
        "smw": smw.reshape(KC, P, 60).transpose(1, 0, 2),
        "gup": np.concatenate([i["gla_w_gate_up_2"][0], i["gla_b_gate_2"]]),
        "rel_bias": i["rel_bias"], "oh": bucket_rows(),
        "brow": np.concatenate([bm[2:3], bm[5:6], i["final_norm_w"].reshape(1, D),
                                np.stack([gains[:, 1], gains[:, 3]], axis=1).reshape(8, D),
                                i["gla_head_norm_2"].reshape(1, D)]),
    }.items()}


def kernel(**inputs):
    import concourse.bacc as _bacc
    from concourse.bass_utils import run_bass_kernel_spmd as _run

    arrays = pack({n: np.asarray(a) for n, a in inputs.items()})
    nc = _bacc.Bacc("TRN2", target_bir_lowering=False, num_devices=1)
    aps = {n: nc.dram_tensor("in_" + n, a.shape, F32, kind="ExternalInput").ap()
           for n, a in arrays.items()}
    aps["out"] = nc.dram_tensor("out", (1, S, D), F32, kind="ExternalOutput").ap()
    build(nc, aps)
    r = _run(nc, [{"in_" + n: a for n, a in arrays.items()}], core_ids=[0])
    return r.results[0]["out"]
```

```python
from contextlib import ExitStack

import numpy as np
import concourse.bass as bass
from concourse import mybir

F32 = mybir.dt.float32
F32R = mybir.dt.float32r
BF16 = mybir.dt.bfloat16
ALU = mybir.AluOpType
ACT = mybir.ActivationFunctionType
AX = mybir.AxisListType.X

P = 128
D = 1024
KC = D // P
S = 256
NT = S // P
EPS = 1e-6
NEG = -1e30

HA, HDA = 8, 64
HB = 4
NG, NE, FE = 4, 8, 256
EXPERTS = NG * NE
FF = 4096
FBLK = FF // 512
SBH = 16
GH = 4
DROPPED = 2.0 ** 100
GSUB = 32
GCLAMP = 60.0
LEVELS = 7

FULL_NORMS = (0, 1, 6)

RAW = 8
SPL = 4
WB = 4

C_QA, C_KA, C_VA, C_QKVB, C_Z, C_BA, C_GA, C_GB = 0, 512, 1024, 1536, 3072, 3584, 3592, 4616


class Step:

    def __init__(self, name, arg, nu, nk):
        self.name, self.arg, self.nu, self.nk = name, arg, nu, nk
        self.u = self.k = 0
        self.sb = 0


def schedule():
    st = []

    def add(name, arg=None, nu=0, nk=0, sb=0):
        st.append(Step(name, arg, nu, nk))
        st[-1].sb = sb

    add("params", None, 1)
    add("cond")
    for n in range(4):
        add("mod", n, 1, 4)
    add("norm", 0, 4)
    add("tblk", ("pre", 0), 1, 2)
    add("bias", None, 1)
    add("tblk", ("pre", 1), 1, 2)
    add("conv", 0)
    add("ba", None, 1)
    for c in range(2, 6):
        add("tblk", ("pre", c), 1, 2)
        add("conv", c - 1)
    mods = [("mod", n, 1, 4) for n in range(4, 12)]
    add("conv", 5)
    add(*mods[0])
    add("dtok", None, 6)
    add("decay", None, 1)
    add("decay_rows", None, 2)
    add("dtr", None, 6)
    add("dmat", None, 4)
    fill = {0: ("nblk", ("z", 0), 2, 4), 1: ("tblk", ("qa", 0), 1, 2), 2: ("tblk", ("qa", 1), 1, 2),
            3: ("tblk", ("ka", 0), 1, 2), 4: ("tblk", ("ka", 1), 1, 2), 5: ("tblk", ("ga", 0), 1, 2)}
    for lev in range(LEVELS):
        add("inv_y", lev, 2)
        add(*mods[1 + lev])
        add("inv_x", lev, 4 if lev < LEVELS - 1 else 2)
        if lev in fill:
            add(*fill[lev])
    add("du", None, 3)
    add("tblk", ("ga", 1), 1, 2)
    add("dstate", None, 2)
    add("nblk", ("va", 0), 2, 4)
    add("dnew", None, 1)
    add("tblk", ("ga", 2), 1, 2)
    add("dout", None, 1)
    add("dnorm")
    add("tblk", ("ga", 3), 1, 2)
    add("dyt", None, 2)
    for g in range(HA + 1):
        if g < HA:
            add("score", g, 1)
        if g > 0:
            add("probs", g - 1, 1)
        if g % 2 and g < HA:
            add("tblk", ("gb", g // 2), 1, 2)
        elif g > 0:
            add("attend", g // 2 - 1, 1)
    for c in range(4):
        add("up", c, 2, 2)
    add("wout", 0, 0, 8)
    add("res1")
    add("norm", 1, 4)
    add("router", None, 1)
    add("moe", None, EXPERTS * 3, EXPERTS * 6)
    add("res2")
    for layer in range(4):
        add("norm", 2 + 2 * layer, 4)
        if layer in (0, 3):
            for d in ("sq", "sk"):
                for c in range(4):
                    add("tblk", (d, c), 1, 2, layer // 3)
            for c in range(2):
                add("nblk", ("sv", c), 2, 4, layer // 3)
            for h in range(SBH + 3):
                add("sb", h, (h < SBH) + (h >= 4 and h % 2 == 0), 0, layer // 3)
        elif layer == 1:
            for d in ("cc", "cu", "cb"):
                for c in range(4):
                    add("tblk", (d, c), 1, 2)
        else:
            add("galow", None, 1)
            add("tblk", ("gq", 0), 1, 2)
            add("gates", None, 2)
            add("tblk", ("gq", 1), 1, 2)
            for c in range(2):
                add("tblk", ("gk", c), 1, 2)
            add("gcum", None, 4)
            for b in range(4):
                add("gkeys", b)
                add("nblk", (("gv", "gg")[b // 2], b % 2), 2, 4)
                add("gscore", b, 1)
            add("gout", None, 6)
            add("gyt", None, 4)
        add("wout", layer + 1, 0, 8)
        add("post", ("mix", layer))
        add("norm", 3 + 2 * layer, 4)
        add("ffn", layer, FBLK * 4, FBLK * 8)
        add("post", ("ffn", layer))
    u = k = 0
    for s in st:
        s.u, s.k = u, k
        u += s.nu
        k += s.nk
    return st


def release_plan(steps):
    rel, used, acc = {}, 0, 0

    def count(k):
        nonlocal used
        used += 1
        rel[k] = ("used", used)

    def unit(k, u):
        rel[k] = ("unit", u)

    for s in steps:
        k = s.k
        if s.name == "up":
            unit(k, s.u)
            unit(k + 1, s.u + 1)
        elif s.name in ("tblk", "mod", "nblk"):
            for j in range(s.nk - 1):
                count(k + j)
            unit(k + s.nk - 1, s.u + s.nu - 1)
        elif s.name == "wout":
            for j in range(7):
                count(k + j)
            acc += 1
            rel[k + 7] = ("acc", 2 * acc)
        elif s.name in ("ffn", "moe"):
            blocks, nd, per = (FBLK, 4, 4) if s.name == "ffn" else (EXPERTS, 2, 3)
            for b in range(blocks + 1):
                if b < blocks:
                    for j in range(3):
                        count(k + j)
                    unit(k + 3, s.u + per * b + 1)
                    k += 4
                if b > 0:
                    for j in range(nd):
                        if b == blocks and j == nd - 1:
                            acc += 1
                            rel[k + j] = ("acc", 2 * acc)
                        else:
                            count(k + j)
                    k += nd
    return rel


def tile_t(w, c):
    b = w[:, c:c + 256].reshape(2, 4, P, 256)
    return [x.transpose(1, 0, 2).reshape(P, 1024) for x in b]


def tile_n(w, c):
    b = w[:, c:c + 512].reshape(4, 2, P, 512)
    return [x.transpose(1, 0, 2).reshape(P, 1024) for x in b]


def tile_rows(w):
    return list(w.reshape(-1, P, 1024))


def weight_tiles(i, steps):
    out = []
    win = i["w_in"][0]
    for s in steps:
        if s.name == "mod":
            out += tile_n(i["w_mod"][0], 512 * s.arg)
        elif s.name in ("tblk", "nblk"):
            kind, c = s.arg
            layer3 = s.sb
            w, c0 = {
                "pre": (win, C_QKVB), "qa": (win, C_QA), "ka": (win, C_KA), "va": (win, C_VA),
                "z": (win, C_Z), "ga": (win, C_GA), "gb": (win, C_GB),
                "sq": (i["sb_w_qkv_2"][layer3], 0), "sk": (i["sb_w_qkv_2"][layer3], D),
                "sv": (i["sb_w_qkv_2"][layer3], 2 * D),
                "cb": (i["conv_w_in_2"][0], 0), "cc": (i["conv_w_in_2"][0], D),
                "cu": (i["conv_w_in_2"][0], 2 * D),
                "gq": (i["gla_w_in_2"][0], 0), "gk": (i["gla_w_in_2"][0], 512),
                "gv": (i["gla_w_in_2"][0], D), "gg": (i["gla_w_in_2"][0], 2 * D),
            }[kind]
            out += tile_t(w, c0 + 256 * c) if s.name == "tblk" else tile_n(w, c0 + 512 * c)
        elif s.name == "up":
            for w in (i["w_up_a"][0], i["w_up_b"][0]):
                b = w[:, 256 * s.arg:256 * s.arg + 256].reshape(4, P, 256)
                out.append(b.transpose(1, 0, 2).reshape(P, 1024))
        elif s.name == "wout":
            w = [i["w_out"][0], i["sb_w_o_2"][0], i["conv_w_out_2"][0], i["gla_w_o_2"][0],
                 i["sb_w_o_2"][1]][s.arg]
            out += tile_rows(w)
        elif s.name == "moe":
            for e in range(EXPERTS + 1):
                if e < EXPERTS:
                    g, x = divmod(e, NE)
                    gu = np.concatenate([i["w_e_gate"][0, g, x], i["w_e_up"][0, g, x]], axis=1)
                    out += tile_n(gu, 0)
                if e > 0:
                    g, x = divmod(e - 1, NE)
                    out += tile_rows(i["w_e_down"][0, g, x])
        elif s.name == "ffn":
            up, down = i["ffn_w_up_2"][s.arg], i["ffn_w_down_2"][s.arg]
            for b in range(FBLK + 1):
                if b < FBLK:
                    out += tile_n(up, 512 * b)
                if b > 0:
                    out += tile_rows(down[512 * (b - 1):512 * b])
    return np.ascontiguousarray(np.stack(out))


def constants():
    j = np.arange(P)[:, None]
    i = np.arange(P)[None, :]
    parts = {
        "ident": (i == j), "tri": (j <= i), "neg_ge": -1.0 * (j >= i), "neg_one": -np.ones((P, P)),
        "after": (j > i), "strict": (i > j), "one": np.ones((P, P)),
        "levels": np.concatenate([((i >> (v + 1)) == (j >> (v + 1))) & ((i >> v) & 1 == 1)
                                  & ((j >> v) & 1 == 0) for v in range(LEVELS)], axis=1),
        "iota": np.broadcast_to(np.arange(NE)[None, :], (P, NE)),
    }
    at, cols = {}, 0
    for n, a in parts.items():
        at[n] = (cols, a.shape[1])
        cols += a.shape[1]
    return np.concatenate([np.asarray(a, np.float32) for a in parts.values()], axis=1), at


def bucket_rows():
    m = np.arange(512)
    n = np.maximum(255 - m, 0)
    nf = np.maximum(n, 1).astype(np.float32)
    large = 16 + (np.log(nf / np.float32(16)) / np.float32(np.log(8.0)) * np.float32(16)).astype(np.int32)
    b = np.where(n < 16, n, np.minimum(large, 31))
    rows = np.zeros((33, 512), np.float32)
    rows[b, m] = 1.0
    rows[:, m > 255] = 0.0
    rows[32, m > 255] = NEG
    return rows


R_N1, R_N2, R_BM, R_PRE, R_CW, R_CW2 = 0, 8, 16, 64, 128, 176
ROWS1, ROWS2 = 128, 72
B_G1, B_G2, B_FINAL, B_POST, B_HEAD = 0, 1, 2, 3, 11
S_DT, S_AL, S_BR, S_ON, S_W = 0, 4, 8, 44, 172


def build(nc, aps, dbg=None):
    steps = schedule()
    rel = release_plan(steps)
    cst_host, cst_at = constants()
    NCST = cst_host.shape[1]
    NTILES = sum(s.nk for s in steps)
    NUNITS = sum(s.nu for s in steps)
    wall, out = aps["weights"], aps["out"]
    bias_rows = nc.dram_tensor("bias_rows", (HA, P, 512), F32, kind="Internal")

    with ExitStack() as ctx:
        def sb(name, shape, dt=F32):
            return ctx.enter_context(nc.sbuf_tensor("s_" + name, shape, dt))

        def sem(name):
            return ctx.enter_context(nc.semaphore(name))

        raw = sb("raw", [P, RAW, 1024])
        whi = sb("whi", [P, SPL, 1024], F32R)
        wlo = sb("wlo", [P, SPL, 1024], F32R)
        H = sb("h", [P, NT, D])
        XS = sb("xs", [P, NT, D])
        XF = sb("xf", [P, KC, S])
        XTh, XTl = sb("xth", [P, KC, S], F32R), sb("xtl", [P, KC, S], F32R)
        OTh, OTl = sb("oth", [P, KC, S], F32R), sb("otl", [P, KC, S], F32R)
        GB = sb("gb", [P, 2, D])
        CST = sb("cst", [P, NCST])
        COLP = sb("colp", [P, ROWS1 + ROWS2])
        SROW = sb("srow", [P, S_W])
        SMW = sb("smw", [P, KC, 60])
        GUP = sb("gup", [17, 512])
        CC = sb("cc", [P, 3, KC])
        MODC = sb("modc", [P, 5, KC])
        SS = sb("ss", [P, 16])
        VAR = sb("var", [P, 2, 16])
        RS = sb("rs", [P, 2, 16])
        MH = sb("mh", [P, 16])
        IDB, DROP = sb("idb", [P, P], BF16), sb("drop", [P, P], BF16)
        BA = sb("ba", [P, 2, 8])
        BT = sb("bt", [P, 8, 8])
        GC = sb("gc", [P, 24])
        EG = sb("eg", [P, 24])
        REL = sb("rel", [33, HA])
        RT = sb("rt", [P, 2, 160])
        COMB = sb("comb", [P, 2, EXPERTS])
        AR = sb("arena", [P, 15648])

        def area(start, *shape):
            n = int(np.prod(shape))
            v = AR[:, start:start + n]
            if len(shape) == 1:
                return v
            names = "abcd"[:len(shape)]
            pat = f"p ({' '.join(names)}) -> p {' '.join(names)}"
            return v.rearrange(pat, **dict(zip(names, shape)))

        def cst(name):
            a, w = cst_at[name]
            return CST[:, a:a + w]

        IDENT, TRI = cst("ident"), cst("tri")

        def over(v, n):
            return v.unsqueeze(1).broadcast_to([P, n, v.shape[1]])

        PRE, POST = area(0, 12, 259), area(3108, 12, S)
        KNT, KBT, QNT = area(0, 2, HB, P), area(1024, 2, HB, P), area(2048, 2, HB, P)
        DTI, DTS, NMT = area(3108, 8, P), area(4132, 8, P), area(5156, 8, P)
        TOK = area(6180, 3, NT, 512)
        KBK = area(9252, NT, 512)
        KBG, KD = area(10276, 512), area(10788, 512)
        ER, WT, S1B, VNW = area(11300, 512), area(11812, 512), area(12324, 512), area(12836, 512)
        PTM = area(13348, 8, P)
        NTL = area(14372, 8, P)
        QGT = area(11300, 512)
        XI = XS[:, 0, :].rearrange("p (a b) -> p a b", a=8)
        XTI = XS[:, 1, :].rearrange("p (a b) -> p a b", a=8)
        YI = XF[:, 0:4, :].rearrange("p a b -> p (a b)").rearrange("p (a b) -> p a b", a=8)
        UI = XF[:, 4:8, :].rearrange("p a b -> p (a b)").rearrange("p (a b) -> p a b", a=8)
        ZS = area(7204, NT, 512)
        OB = area(6180, NT, 512)
        QAT, KAT, VA = area(0, 4, S), area(1024, 4, S), area(2048, NT, 512)
        BIAS = area(9252, HA, 384)
        MS_, MP = area(3108, 2, 384), area(8228, 2, 384)
        MPT = area(13348, 4, 384)
        BST = area(8228, 512)[0:HA]
        PR, OH = area(10276, 2, P), area(10788, 512)[0:33]
        SGA, SGB = area(4132, KC, S), area(6180, KC, S)
        MTMP = area(0, 2, S)
        SG, AE = area(0, NT, 256), area(512, NT, 256)
        HID = area(0, NT, 512)
        QT, KT, VT = area(0, KC, S), area(2048, KC, S), area(4096, NT, D)
        AB, LN, SPB, WX = (area(6144 + 1536 * i, 4, 384) for i in range(4))
        CB, HP, CV = area(0, KC, S), area(2048, KC, 258), area(4112, KC, S)
        GQ, GK, GV, GG = area(0, GH, S), area(1024, GH, S), area(2048, NT, D), area(4096, NT, D)
        ALT = area(6144, S)
        LG, CUM, QGL = area(6400, NT, 512), area(7424, GH, S), area(8448, GH, S)
        KBB = area(9472, 2, GH, S)
        STT = area(11520, NT, GH, P)
        QI, KDG, KTK, ES = area(12544, GH, P), area(13056, 512), area(13568, 512), area(14080, 512)
        S1G = area(14592, GH, 256)
        REF = area(15616, GH * NT, 4)
        GTM = area(14592, NT, 512)

        work = [ctx.enter_context(nc.psum_tensor(f"work{b}", [P, 512], F32)) for b in range(WB)]
        ACC = ctx.enter_context(nc.psum_tensor("acc", [P, 4, 512], F32))

        load_const = sem("load_const")
        loaded = [sem(f"loaded{i}") for i in range(RAW)]
        hi_made, lo_made, used = sem("hi_made"), sem("lo_made"), sem("used")
        full = [sem(f"full{b}") for b in range(WB)]
        done = [sem(f"done{b}") for b in range(WB)]
        acc_full, acc_free = sem("acc_full"), sem("acc_free")
        hi_out = sem("hi_out")
        x_hi, x_lo = sem("x_hi"), sem("x_lo")
        xf_ready = sem("xf_ready")
        var_ready, rs_ready = sem("var_ready"), sem("rs_ready")
        h_ready = sem("h_ready")
        gb_loaded, gb_free = [sem("gb_loaded0"), sem("gb_loaded1")], sem("gb_free")
        act_chain, dve_chain = sem("act_chain"), sem("dve_chain")
        a2d, d2a = sem("act_to_dve"), sem("dve_to_act")
        d2p = sem("dve_to_pe")
        z_full = sem("z_full")
        hid_ready = sem("hid_ready")
        conv_ready = sem("conv_ready")
        RS2 = sb("rs2", [P, 2, 2])
        bias_written = sem("bias_written")
        bias_read = sem("bias_read")
        logs_ready = sem("logs_ready")
        rel_set = sem("rel_set")
        conv_done = sem("conv_done")
        out_sem = sem("out_written")

        def full_wait(eng, u, extra=0):
            eng.wait_ge(full[u % WB], u // WB + 1 + extra)

        def done_wait(eng, u, extra=0):
            eng.wait_ge(done[u % WB], u // WB + 1 + extra)

        def bank(u):
            return work[u % WB]

        block = ctx.enter_context(nc.Block())

        N_UPDATES = sum(1 for s in steps if s.name in ("res1", "post")) + 2 * 1
        NCONST = 10

        @block.sync
        def _(sp):
            for dst, src in (
                (H[:], aps["x"].rearrange("b (t p) d -> p (b t) d", p=P)),
                (CST[:], aps["cst"]), (PR[:, 0, :], aps["prows"][0:ROWS1, :]),
                (PR[0:ROWS2, 1, :], aps["prows"][ROWS1:ROWS1 + ROWS2, :]),
                (CC[:, 0, :], aps["c"].rearrange("b (k p) -> p (b k)", p=P)),
                (SROW[:], aps["srow"].partition_broadcast(P)),
                (SMW[:], aps["smw"]), (GUP[:], aps["gup"]), (REL[0:32, :], aps["rel_bias"]),
                (OH[:], aps["oh"]),
            ):
                with nc.allow_non_contiguous_dma("small parameters"):
                    sp.dma_start(dst, src).then_inc(load_const, 16)
            first = NTILES % RAW + RAW
            for k in range(first):
                if k >= RAW:
                    sp.wait_ge(lo_made, k - RAW + 1)
                sp.dma_start(raw[:, k % RAW, :], wall[k]).then_inc(loaded[k % RAW], 16)
            with sp.Fori(0, (NTILES - first) // RAW) as it:
                for j in range(RAW):
                    k = first + j
                    sp.wait_ge(lo_made, it * RAW + (k - RAW + 1))
                    sp.dma_start(raw[:, k % RAW, :], wall[it * RAW + k]).then_inc(loaded[k % RAW], 16)
            for t in range(NT):
                sp.wait_ge(h_ready, 2 * N_UPDATES - 1 + t)
                sp.dma_start(out[0, t * P:(t + 1) * P, :], H[:, t, :]).then_inc(out_sem, 16)
            sp.wait_ge(out_sem, 16 * NT)

        def tile_wait(eng, k, it=None, per=None):
            kind, v = rel[k]
            extra = 0 if it is None else it * per[kind]
            if kind == "used":
                eng.wait_ge(used, v + extra)
            elif kind == "acc":
                eng.wait_ge(acc_full, v)
            else:
                full_wait(eng, v, extra)

        class Splitter:

            def __init__(self, one):
                self.next, self.one = 0, one

            def upto(self, k):
                while self.next < min(k, NTILES):
                    self.one(self.next)
                    self.next += 1

        def make_hi(k, it=None, per=None):
            act = nc.scalar
            n = 0 if it is None else it * per["tiles"]
            nr = 0 if it is None else it * (16 * per["tiles"] // RAW)
            act.wait_ge(loaded[k % RAW], 16 * (k // RAW + 1) + nr)
            if k >= SPL:
                tile_wait(act, k - SPL, it, per)
            act.copy(whi[:, k % SPL, :], raw[:, k % RAW, :]).then_inc(hi_made, 1)

        def make_lo(k, it=None, per=None):
            dve = nc.vector
            n = 0 if it is None else it * per["tiles"]
            dve.wait_ge(hi_made, n + (k + 1))
            dve.tensor_tensor(wlo[:, k % SPL, :], raw[:, k % RAW, :],
                              whi[:, k % SPL, :].bitcast(F32), ALU.subtract).then_inc(lo_made, 1)

        FFN_PER = {"tiles": 8, "used": 7, "unit": 1}
        MOE_PER = {"tiles": 24, "used": 20, "unit": 3}

        def post_row(which, layer):
            return B_POST + 2 * layer + (which == "ffn")

        gb_rows, gb_freed = [B_G1, B_G2, B_FINAL], [(h_ready, 2), (h_ready, 4), (h_ready, 6)]
        for layer in range(4):
            if layer == 2:
                gb_rows.append(B_HEAD)
                gb_freed.append((gb_free, 1))
            gb_rows += [post_row("mix", layer), post_row("ffn", layer)]
            gb_freed += [(h_ready, 8 + 4 * layer), (h_ready, 10 + 4 * layer)]

        @block.gpsimd
        def _(pool):
            asked = uses = loads = 0

            def load_rows():
                nonlocal loads
                while loads < min(uses + 2, len(gb_rows)):
                    if loads >= 2:
                        pool.wait_ge(*gb_freed[loads - 2])
                    pool.dma_start(GB[:, loads % 2, :], aps["brow"][gb_rows[loads]].partition_broadcast(P))\
                        .then_inc(gb_loaded[loads % 2], 16)
                    loads += 1

            def inv_sqrt(w):
                nonlocal asked
                asked += 1
                pool.wait_ge(var_ready, asked)
                i = (asked - 1) % 2
                pool.tensor_tensor(RS[:, i, 0:w], VAR[:, i, 0:w], MH[:, 0:w], ALU.pow).then_inc(rs_ready, 1)

            load_rows()
            roots = {"dtok": 1, "dnorm": 1, "gyt": 1, "res1": 2, "res2": 4}
            for s in steps:
                n = roots.get(s.name, 0)
                if s.name == "post":
                    n = 2 if s.arg == ("ffn", 3) else 4
                elif s.name == "norm" and s.arg == 0:
                    n = 2
                for _ in range(n):
                    inv_sqrt({"dtok": 16, "dnorm": 8, "gyt": 8}.get(s.name, 1))
                if s.name == "norm":
                    load_rows()
                if s.name == "bias":
                    done_wait(pool, s.u)
                    with nc.allow_non_contiguous_dma("rows"):
                        pool.dma_start(bias_rows.ap(), BST.unsqueeze(1).broadcast_to([HA, P, 512]))\
                            .then_inc(bias_written, 16)
                elif s.name == "dyt":
                    pool.wait_ge(bias_written, 16)
                    done_wait(pool, s.u + 1)
                    for t in range(NT):
                        src = bass.AP(tensor=bias_rows, offset=255 - P * t,
                                      ap=[[511, P], [P * 512, HA], [1, P * (t + 1)]])
                        pool.dma_start(BIAS[:, :, P * t:P * t + P * (t + 1)], src).then_inc(bias_read, 16)
                if s.name in ("res1", "gyt"):
                    uses += 1
                elif s.name == "post":
                    uses += 1
                elif s.name == "res2":
                    uses += 2

        @block.scalar
        def _(act):
            chain = n_a2d = n_d2a = n_hi = nx = nacc = nxf = nh = nz = 0
            z_units = {}

            def link(ins):
                nonlocal chain
                chain += 1
                ins.then_inc(act_chain, 1)

            def sync():
                act.wait_ge(act_chain, chain)

            def tell_dve(ins):
                nonlocal n_a2d
                n_a2d += 1
                ins.then_inc(a2d, 1)

            def hear_dve():
                nonlocal n_d2a
                n_d2a += 1
                act.wait_ge(d2a, n_d2a)

            split = Splitter(make_hi)

            def ev_hi(u, dst, src=None, extra=0):
                full_wait(act, u, extra)
                src = bank(u)[:] if src is None else src
                act.copy(dst, src).then_inc(hi_out, 1)

            def ev(u, dst, func=ACT.Copy, src=None, scale=1.0):
                full_wait(act, u)
                act.activation(dst, bank(u)[:] if src is None else src, func, scale=scale)\
                    .then_inc(done[u % WB], 1)

            def x_split(j, dst):
                nonlocal nx
                act.copy(dst[:, 2 * j:2 * j + 2, :], XF[:, 2 * j:2 * j + 2, :]).then_inc(x_hi, 1)
                nx += 1

            def sum_sq(dst, src, t):
                junk = XF[:, 4 * t:4 * t + 4, :].rearrange("p a b -> p (a b)")
                tell_dve(act.activation(junk, src, ACT.Square, accum_out=dst))

            def sum_sq_h(t, col):
                nonlocal nh
                nh += 1
                act.wait_ge(h_ready, nh)
                sum_sq(SS[:, col + t:col + t + 1], H[:, t, :], t)

            def v2(u):
                return bank(u)[:].rearrange("p (a b) -> p a b", a=2)

            def v4(u):
                return bank(u)[:].rearrange("p (a b) -> p a b", a=4)

            act.wait_ge(load_const, 16 * NCONST)
            for s in steps:
                u, a = s.u, s.arg
                if s.name in ("tblk", "mod", "nblk", "up"):
                    split.upto(s.k + s.nk + SPL)
                elif s.name == "wout":
                    split.upto(s.k + s.nk)
                if s.name == "mod" and a in (3, 9):
                    hear_dve()
                elif s.name == "cond":
                    link(act.activation(CC[:, 1, :], CC[:, 0, :], ACT.Silu))
                    sync()
                    tell_dve(act.copy(CC[:, 2, :], CC[:, 1, :]))
                    hear_dve()
                    act.copy(OTh[:, :, 0:P], XF[:, :, 0:P]).then_inc(x_hi, 1)
                    nx += 1
                elif s.name == "norm":
                    j = a
                    if j == 0:
                        for t in range(NT):
                            sum_sq(SS[:, t:t + 1], H[:, t, :], t)
                    for q in range(4):
                        full_wait(act, u + q)
                        for c in range(2):
                            ch = 2 * q + c
                            if j < 2:
                                sc, bi = MODC[:, 2 * j + 1, ch:ch + 1], MODC[:, 2 * j, ch:ch + 1]
                            else:
                                sc, bi = COLP[:, R_PRE + 8 * (j - 2) + ch:][:, 0:1], 0.0
                            dst = XF if j in FULL_NORMS else XTh
                            ins = act.activation(dst[:, ch, :], v2(u + q)[:, c, :], ACT.Identity,
                                                 bias=bi, scale=sc)
                        if j in FULL_NORMS:
                            ins.then_inc(done[(u + q) % WB], 1)
                            done_wait(act, u + q)
                            x_split(q, XTh)
                        else:
                            ins.then_inc(x_hi, 1)
                            nx += 1
                elif s.name == "bias":
                    ev(u, BST, src=bank(u)[0:HA, :])
                elif s.name == "tblk":
                    kind, c = a
                    if kind == "pre":
                        ev(u, PRE[:, 2 * c:2 * c + 2, 3:259], src=v2(u))
                    elif kind in ("qa", "ka"):
                        ev(u, (QAT if kind == "qa" else KAT)[:, 2 * c:2 * c + 2, :], src=v2(u))
                    elif kind in ("ga", "gb"):
                        ev(u, (SGA if kind == "ga" else SGB)[:, 2 * c:2 * c + 2, :], ACT.Sigmoid, v2(u))
                    elif kind in ("sq", "gq"):
                        ev(u, (QT if kind == "sq" else GQ)[:, 2 * c:2 * c + 2, :], src=v2(u),
                           scale=0.125 if kind == "sq" else float(P) ** -0.5)
                    elif kind in ("sk", "gk"):
                        ev(u, (KT if kind == "sk" else GK)[:, 2 * c:2 * c + 2, :], src=v2(u))
                    elif kind == "cc":
                        ev(u, CB[:, 2 * c:2 * c + 2, :], src=v2(u))
                    elif kind == "cb":
                        done_wait(act, u)
                        x_split(c, OTh)
                elif s.name == "nblk":
                    kind, c = a
                    for t in range(NT):
                        dst = {"z": ZS, "va": VA}[kind][:, t, :] if kind in ("z", "va") else \
                            {"sv": VT, "gv": GV, "gg": GG}[kind][:, t, 512 * c:512 * c + 512]
                        ev(u + t, dst, ACT.Silu if kind in ("z", "gg") else ACT.Copy)
                elif s.name == "ba":
                    hear_dve()
                    act.preload_act_table_set("natural_log_exp_and_others")
                    link(act.activation(BT[:, 2, :], BT[:, 0, :], ACT.Exp, scale=-1.0))
                    link(act.activation(BT[:, 3, :], BT[:, 1, :], ACT.Abs))
                    link(act.activation(BT[:, 6, 0:4], SROW[:, S_AL:S_AL + 4], ACT.Exp))
                    sync()
                    link(act.activation(BT[:, 4, :], BT[:, 3, :], ACT.Exp, scale=-1.0))
                    sync()
                    tell_dve(act.activation(BT[:, 5, :], BT[:, 4, :], ACT.Ln, bias=1.0))
                elif s.name == "conv":
                    act.wait_ge(conv_done, a + 1)
                    act.activation(POST[:, 2 * a:2 * a + 2, :], POST[:, 2 * a:2 * a + 2, :],
                                   ACT.Silu).then_inc(conv_ready, 1)
                elif s.name == "dtok":
                    act.wait_ge(bias_written, 16)
                    for q in range(6):
                        ev(u + q, TOK[:, q // 2, q % 2, :])
                elif s.name == "decay":
                    full_wait(act, u)
                    act.activation(EG[:], bank(u)[:, 0:24], ACT.Exp).then_inc(a2d, 1)
                    n_a2d += 1
                elif s.name == "decay_rows":
                    full_wait(act, u + 1)
                    tell_dve(act.activation(ER, bank(u + 1)[:], ACT.Exp))
                    done_wait(act, u)
                    done_wait(act, u + 1)
                    tell_dve(act.activation(DTI, DTI, ACT.Exp))
                elif s.name == "dtr":
                    for q in range(6):
                        ev(u + q, (KNT, KBT, QNT)[q // 2][:, q % 2], src=v4(u + q))
                elif s.name == "inv_y":
                    for q in range(2):
                        ev(u + q, YI[:, 4 * q:4 * q + 4, :], src=v4(u + q))
                elif s.name == "du":
                    for q in range(2):
                        ev(u + q, UI[:, 4 * q:4 * q + 4, :], src=v4(u + q))
                    ev(u + 2, WT)
                elif s.name == "dstate":
                    ev(u, OB[:, 0, :])
                    ev(u + 1, S1B)
                elif s.name == "dout":
                    ev(u, OB[:, 1, :])
                elif s.name in ("dyt", "gyt"):
                    for q in range(s.nu):
                        c0 = 4 + 2 * q if s.name == "dyt" else 2 * q
                        ev_hi(u + q, OTh[:, c0:c0 + 2, :], v2(u + q))
                elif s.name == "score":
                    g = a % 2
                    hear_dve()
                    act.activation(MP[:, g, 0:P], MS_[:, g, 0:P], ACT.Exp, bias=SS[:, 2 * g:2 * g + 1],
                                   accum_out=RS2[:, g, 0:1])
                    tell_dve(act.activation(MP[:, g, P:384], MS_[:, g, P:384], ACT.Exp,
                                            bias=SS[:, 2 * g + 1:2 * g + 2], accum_out=RS2[:, g, 1:2]))
                elif s.name == "probs":
                    ev(u, MPT[:, a % 4, :], src=bank(u)[:, 0:384])
                elif s.name == "attend":
                    ev_hi(u, OTh[:, a, :], bank(u)[:, 0:S])
                elif s.name == "up":
                    nxf += 1
                    act.wait_ge(xf_ready, nxf)
                    x_split(a, XTh)
                elif s.name == "router":
                    hear_dve()
                    for t in range(NT):
                        r = RT[:, t, :]
                        tell_dve(act.activation(r[:, 40:44], r[:, 0:4], ACT.Exp, bias=r[:, 37:38],
                                                accum_out=r[:, 44:45]))
                    hear_dve()
                    tell_dve(act.activation(RT[:, :, 98:99], RT[:, :, 97:98], ACT.Exp))
                elif s.name == "post":
                    for t in range(NT):
                        act.wait_ge(acc_full, 2 * nacc + 1 + t)
                        sum_sq(SS[:, 4 + t:5 + t], ACC[:, 2 * t:2 * t + 2, :].rearrange("p a b -> p (a b)"), t)
                        if t == 0:
                            split.upto(s.k + 2)
                        if a != ("ffn", 3):
                            sum_sq_h(t, 0)
                            split.upto(s.k + 3 + t)
                    nacc += 1
                elif s.name == "res1":
                    nacc += 1
                    for t in range(NT):
                        sum_sq_h(t, 0)
                        split.upto(s.k + 2 + 2 * t)
                elif s.name == "res2":
                    nacc += 1
                    for col, t in ((4, 0), (4, 1), (0, 0), (0, 1)):
                        sum_sq_h(t, col)
                    split.upto(s.k + 4)
                elif s.name == "sb":
                    h = a
                    if h < SBH:
                        if h == 0:
                            act.preload_act_table_set("natural_log_exp_and_others")
                        b = h % 4
                        full_wait(act, u)
                        link(act.activation(AB[:, b, :], bank(u)[:, 0:384], ACT.Abs))
                        sync()
                        link(act.activation(AB[:, b, :], AB[:, b, :], ACT.Exp, scale=-1.0))
                        sync()
                        tell_dve(act.activation(LN[:, b, :], AB[:, b, :], ACT.Ln, bias=1.0))
                        z_units[h] = u
                    if 2 <= h < SBH + 2:
                        nz += 1
                        act.wait_ge(z_full, nz)
                        w = z_units[h - 2]
                        act.activation(WX[:, (h - 2) % 4, :], bank(w)[:, 0:384], ACT.Exp)\
                            .then_inc(done[w % WB], 1)
                    if h >= 4 and h % 2 == 0:
                        w = s.u + s.nu - 1
                        ev_hi(w, OTh[:, (h - 4) // 2, :], bank(w)[:, 0:S])
                elif s.name == "galow":
                    ev(u, ALT[0:16, :], src=bank(u)[0:16, 0:S])
                elif s.name == "gates":
                    act.preload_act_table_set("natural_log_exp_and_others")
                    for t in range(NT):
                        full_wait(act, u + t)
                        link(act.activation(GTM[:, t, :], bank(u + t)[:], ACT.Abs))
                        sync()
                        link(act.activation(GTM[:, t, :], GTM[:, t, :], ACT.Exp, scale=-1.0))
                        sync()
                        tell_dve(act.activation(GTM[:, t, :], GTM[:, t, :], ACT.Ln, bias=1.0))
                elif s.name == "gcum":
                    for q in range(2):
                        ev(u + q, CUM[:, 2 * q:2 * q + 2, :], src=v2(u + q), scale=1.0 / 16)
                    ev(u + 2, ES, ACT.Exp, scale=1.0 / 16)
                    ev(u + 3, KTK)
                    done_wait(act, u)
                    done_wait(act, u + 1)
                    tell_dve(act.activation(QI, CUM[:, :, P:S], ACT.Exp))
                elif s.name == "gkeys":
                    if a == 0:
                        hear_dve()
                        tell_dve(act.activation(QGL, QGL, ACT.Exp))
                    hear_dve()
                    tell_dve(act.activation(KBB[:, a % 2], KBB[:, a % 2], ACT.Exp, scale=-1.0))
                elif s.name == "gout":
                    for q in range(2):
                        ev(u + q, S1G[:, 2 * q:2 * q + 2, :], src=v2(u + q))
                    for q in range(4):
                        ev(u + 2 + q, XS[:, q // 2, 512 * (q % 2):512 * (q % 2) + 512])
                elif s.name == "moe":
                    def silu(ub, extra=0):
                        for t in range(NT):
                            full_wait(act, ub + t, extra)
                            act.activation(SG[:, t, :], bank(ub + t)[:, 0:256], ACT.Silu).then_inc(a2d, 1)

                    def t_hi(ut, extra=0):
                        ev_hi(ut, OTh[:, 0:2, :], v2(ut), extra)

                    def one(e, k, ub, it=None):
                        extra = 0 if it is None else it * MOE_PER["unit"]
                        for kk in (k + 4, k + 5):
                            make_hi(kk, it, MOE_PER)
                        silu(ub, extra)
                        for kk in range(k + 6, k + 10):
                            make_hi(kk, it, MOE_PER)
                        t_hi(ub + 2, extra)

                    split.upto(s.k + 4)
                    silu(u)
                    split.upto(s.k + 8)
                    t_hi(u + 2)
                    for e in range(3):
                        one(e, s.k + 4 + 6 * e, u + 3 * (e + 1))
                    with act.Fori(0, 7) as it:
                        for e in range(3, 7):
                            one(e, s.k + 4 + 6 * e, u + 3 * (e + 1), it)
                    split.next = s.k + s.nk + 2
                    n_a2d += 2 * EXPERTS
                elif s.name == "ffn":
                    def relu(ub, extra=0):
                        for t in range(NT):
                            full_wait(act, ub + t, extra)
                            act.activation(HID[:, t, :], bank(ub + t)[:], ACT.Relu)\
                                .then_inc(done[(ub + t) % WB], 1)

                    def t_hi(ut, extra=0):
                        for t in range(NT):
                            ev_hi(ut + t, OTh[:, 0:4, t * P:t * P + P], v4(ut + t), extra)

                    def one(b, k, ub, it=None):
                        extra = 0 if it is None else it * FFN_PER["unit"]
                        for kk in range(k + 4, k + 8):
                            make_hi(kk, it, FFN_PER)
                        relu(ub, extra)
                        for kk in range(k + 8, k + 12):
                            make_hi(kk, it, FFN_PER)
                        t_hi(ub + 2, extra)

                    split.upto(s.k + 4)
                    relu(u)
                    split.upto(s.k + 8)
                    t_hi(u + 2)
                    one(0, s.k + 4, u + 4)
                    with act.Fori(0, FBLK - 2) as it:
                        one(1, s.k + 12, u + 8, it)
                    split.next = s.k + s.nk

        @block.tensor
        def _(pe):
            nx = n_d2p = nacc = nhid = 0
            nlogs, norm_u, z_units = 0, None, {}

            def hear_dve(n=1):
                nonlocal n_d2p
                n_d2p += n
                pe.wait_ge(d2p, n_d2p)

            def begin(u, extra=0):
                if u >= WB:
                    done_wait(pe, u - WB, extra)

            def x_wait(j):
                if norm_u is None:
                    pe.wait_ge(x_lo, nx - 3 + j)
                else:
                    done_wait(pe, norm_u + j)

            def wait_units(units):
                for x in units:
                    done_wait(pe, x)

            def fin(ins, u):
                ins.then_inc(full[u % WB], 1)

            def mm(o, lhs, rhs, start=True, stop=True, **kw):
                return pe.matmul(o, lhs, rhs, start=start, stop=stop, **kw)

            def mm3(o, lhs, rhs, start, stop):
                mm(o, lhs[0], rhs[0], start, False)
                mm(o, lhs[0], rhs[1], False, False)
                return mm(o, lhs[1], rhs[0], False, stop)

            def tr(o, x):
                return pe.transpose(o, x, IDENT[0:x.shape[0], 0:x.shape[0]])

            def w(k, a, b):
                return whi[:, k % SPL, a:b], wlo[:, k % SPL, a:b]

            def xs_(t, kc, a=None, b=None):
                h, l = t
                if a is None:
                    return h[:, kc, :], l[:, kc, :]
                return h[:, kc, a:b], l[:, kc, a:b]

            XT, OT = (XTh, XTl), (OTh, OTl)

            def tile_ready(k, extra=0):
                pe.wait_ge(lo_made, extra + (k + 1))

            def rows_by_cols(x, k, u, nt=NT, it=None, per=None, x_waits=False):
                ek = 0 if it is None else it * per["tiles"]
                eu = 0 if it is None else it * per["unit"]
                for t in range(nt):
                    begin(u + t, eu)
                for j in range(4):
                    tile_ready(k + j, ek)
                    if x_waits:
                        x_wait(j)
                    for kc in (2 * j, 2 * j + 1):
                        for t in range(nt):
                            ins = mm3(bank(u + t)[:], xs_(x, kc, t * P, t * P + P),
                                      w(k + j, 512 * (kc % 2), 512 * (kc % 2) + 512), kc == 0, kc == 7)
                            if kc == 7:
                                fin(ins, u + t)
                    if j < 3:
                        ins.then_inc(used, 1)

            def rows_acc(x, kcs, k, first, last, it=None, per=None, x_waits=False):
                nonlocal nacc
                ek = 0 if it is None else it * per["tiles"]
                if first:
                    if nacc:
                        pe.wait_ge(acc_free, 2 * nacc)
                    nacc += 1
                n, kcs = len(kcs), list(kcs)

                def product(j, t):
                    for c in range(2):
                        ins = mm3(ACC[:, 2 * t + c, :], xs_(x, kcs[j], t * P, t * P + P),
                                  w(k + j, 512 * c, 512 * c + 512),
                                  first and j == 0, last and j == n - 1)
                    return ins

                tail = min(n, SPL) if last else 0
                for j in range(n - tail):
                    tile_ready(k + j, ek)
                    if x_waits:
                        x_wait(j // 2)
                    for t in range(NT):
                        ins = product(j, t)
                    ins.then_inc(used, 1)
                for t in range(NT if tail else 0):
                    for j in range(n - tail, n):
                        tile_ready(k + j, ek)
                        if x_waits:
                            x_wait(j // 2)
                        ins = product(j, t)
                        if j == n - 1:
                            ins.then_inc(acc_full, 1)
                        elif t == NT - 1:
                            ins.then_inc(used, 1)

            pe.wait_ge(load_const, 16 * NCONST)
            for s in steps:
                u, a = s.u, s.arg
                if s.name == "params":
                    tr(bank(u)[:, 0:ROWS1], PR[:, 0, :])
                    fin(tr(bank(u)[:, ROWS1:ROWS1 + ROWS2], PR[0:ROWS2, 1, :]), u)
                elif s.name == "cond":
                    nx += 1
                elif s.name == "mod":
                    pe.wait_ge(x_lo, 1)
                    rows_by_cols(OT, s.k, u, nt=1)
                elif s.name == "norm":
                    for t in range(NT):
                        hear_dve()
                        for q in range(4):
                            if t == 0:
                                begin(u + q)
                            for c in range(2):
                                ins = tr(bank(u + q)[:, (2 * c + t) * P:(2 * c + t + 1) * P],
                                         XS[:, t, (2 * q + c) * P:(2 * q + c + 1) * P])
                            if t == NT - 1:
                                fin(ins, u + q)
                    norm_u = None if a in FULL_NORMS else u
                    if a in FULL_NORMS:
                        nx += 4
                elif s.name == "bias":
                    pe.wait_ge(rel_set, 1)
                    begin(u)
                    fin(mm(bank(u)[0:HA, :], REL[:], OH[:]), u)
                elif s.name == "tblk":
                    begin(u)
                    for m in range(2):
                        for kc in range(KC):
                            if m == 0 and kc % 2 == 0:
                                x_wait(kc // 2)
                            if m == 0 and kc % 4 == 0:
                                tile_ready(s.k + kc // 4)
                            c0 = (kc % 4) * 256 + m * P
                            ins = mm3(bank(u)[:, m * S:m * S + S], w(s.k + kc // 4, c0, c0 + P),
                                      xs_(XT, kc), kc == 0, kc == 7)
                            if m == 1 and kc == 3:
                                ins.then_inc(used, 1)
                    fin(ins, u)
                elif s.name == "nblk":
                    rows_by_cols(XT, s.k, u, x_waits=True)
                elif s.name == "ba":
                    pe.wait_ge(x_lo, nx)
                    begin(u)
                    for t in range(NT):
                        for kc in range(KC):
                            ins = mm(bank(u)[:, 8 * t:8 * t + 8], XF[:, kc, t * P:t * P + P],
                                     SMW[:, kc, 0:8], kc == 0, kc == 7)
                    fin(ins, u)
                elif s.name == "dtok":
                    for q in range(6):
                        sec, t = divmod(q, 2)
                        pe.wait_ge(conv_ready, 2 * sec + 2)
                        begin(u + q)
                        for h in range(HB):
                            ins = tr(bank(u + q)[:, h * P:h * P + P],
                                     POST[:, 4 * sec + h, t * P:t * P + P])
                        fin(ins, u + q)
                elif s.name == "decay":
                    hear_dve()
                    begin(u)
                    for q, m in enumerate(("tri", "after", "one")):
                        for t in range(NT):
                            ins = mm(bank(u)[:, 8 * q + 4 * t:8 * q + 4 * t + 4], cst(m),
                                     BT[:, 7, 4 * t:4 * t + 4])
                    fin(ins, u)
                elif s.name == "decay_rows":
                    for t in range(NT):
                        begin(u + t)
                        for h in range(HB):
                            ins = mm(bank(u + t)[:, h * P:h * P + P], NTL[:, 4 * t + h, :], TRI)
                        fin(ins, u + t)
                elif s.name == "dtr":
                    for q in range(6):
                        kind, t = divmod(q, 2)
                        if t == 0:
                            hear_dve()
                        begin(u + q)
                        src = (TOK[:, 1, t, :], KBK[:, t, :], TOK[:, 0, t, :])[kind]
                        for h in range(HB):
                            ins = tr(bank(u + q)[:, h * P:h * P + P], src[:, h * P:h * P + P])
                        fin(ins, u + q)
                elif s.name == "dmat":
                    for q in range(4):
                        kind, t = divmod(q, 2)
                        done_wait(pe, u - 4 + q)
                        if q == 0:
                            done_wait(pe, u - 6)
                            done_wait(pe, u - 5)
                        begin(u + q)
                        for h in range(HB):
                            ins = mm(bank(u + q)[:, h * P:h * P + P], KNT[:, t, h, :],
                                     (QNT if kind else KBT)[:, t, h, :])
                        fin(ins, u + q)
                elif s.name == "inv_y":
                    hear_dve()
                    for q in range(2):
                        begin(u + q)
                        for h in range(4):
                            ins = mm(bank(u + q)[:, h * P:h * P + P], NTL[:, 4 * q + h, :],
                                     XI[:, 4 * q + h, :])
                        fin(ins, u + q)
                    y_units = (u, u + 1)
                elif s.name == "inv_x":
                    x_units = u
                    for q in range(s.nu):
                        if q < 2:
                            done_wait(pe, y_units[q])
                        begin(u + q)
                        m0 = 4 * (q % 2)
                        xy = s.nu == 4 and q < 2
                        for h in range(4):
                            ins = mm(bank(u + q)[:, h * P:h * P + P],
                                     (XTI if xy else YI)[:, m0 + h, :], (YI if xy else XTI)[:, m0 + h, :])
                        fin(ins, u + q)
                elif s.name == "du":
                    for q in range(2):
                        done_wait(pe, x_units + q)
                    for t in range(NT):
                        begin(u + t)
                        for h in range(HB):
                            ins = mm(bank(u + t)[:, h * P:h * P + P], XTI[:, 4 * t + h, :],
                                     TOK[:, 2, t, h * P:h * P + P])
                        fin(ins, u + t)
                    begin(u + 2)
                    for h in range(HB):
                        ins = mm(bank(u + 2)[:, h * P:h * P + P], KBG[:, h * P:h * P + P],
                                 XTI[:, 4 + h, :])
                    fin(ins, u + 2)
                    du = u
                elif s.name == "dstate":
                    done_wait(pe, du)
                    begin(u)
                    for h in range(HB):
                        ins = mm(bank(u)[:, h * P:h * P + P], PTM[:, h, :], UI[:, h, :])
                    fin(ins, u)
                    begin(u + 1)
                    for h in range(HB):
                        ins = mm(bank(u + 1)[:, h * P:h * P + P], KD[:, h * P:h * P + P], UI[:, h, :])
                    fin(ins, u + 1)
                    dst = u + 1
                elif s.name == "dnew":
                    done_wait(pe, dst)
                    done_wait(pe, du + 2)
                    begin(u)
                    for h in range(HB):
                        ins = mm(bank(u)[:, h * P:h * P + P], WT[:, h * P:h * P + P],
                                 S1B[:, h * P:h * P + P])
                    fin(ins, u)
                    dnew = u
                elif s.name == "dout":
                    done_wait(pe, dnew)
                    begin(u)
                    for h in range(HB):
                        o = bank(u)[:, h * P:h * P + P]
                        mm(o, QGT[:, h * P:h * P + P], S1B[:, h * P:h * P + P], True, False)
                        ins = mm(o, PTM[:, 4 + h, :], VNW[:, h * P:h * P + P], False, True)
                    fin(ins, u)
                elif s.name in ("dyt", "gyt"):
                    hear_dve()
                    src = OB if s.name == "dyt" else XS
                    for q in range(s.nu):
                        begin(u + q)
                        for c in range(2):
                            for t in range(NT):
                                ins = tr(bank(u + q)[:, (2 * c + t) * P:(2 * c + t + 1) * P],
                                         src[:, t, (2 * q + c) * P:(2 * q + c + 1) * P])
                        fin(ins, u + q)
                    mixed = [u + q for q in range(s.nu)]
                elif s.name == "score":
                    if a == 0:
                        for x in steps:
                            if x.name in ("tblk", "nblk") and x.arg[0] in ("qa", "ka", "va"):
                                for q in range(x.nu):
                                    done_wait(pe, x.u + q)
                        probs_units = {}
                    r, c = 64 * (a % 2), a // 2
                    begin(u)
                    mm(bank(u)[:, 0:P], QAT[r:r + 64, c, 0:P], KAT[r:r + 64, c, 0:P])
                    fin(mm(bank(u)[:, P:384], QAT[r:r + 64, c, P:S], KAT[r:r + 64, c, :]), u)
                elif s.name == "probs":
                    hear_dve()
                    begin(u)
                    for c in range(3):
                        ins = tr(bank(u)[:, c * P:c * P + P], MP[:, a % 2, c * P:c * P + P])
                    fin(ins, u)
                    probs_units[a] = u
                elif s.name == "attend":
                    begin(u)
                    for h in (2 * a, 2 * a + 1):
                        done_wait(pe, probs_units[h])
                        o = bank(u)[64 * (h % 2):64 * (h % 2) + 64, :]
                        mm(o[:, 0:S], VA[:, 0, 64 * h:64 * h + 64], MPT[:, h % 4, 0:S], True, False)
                        ins = mm(o[:, P:S], VA[:, 1, 64 * h:64 * h + 64], MPT[:, h % 4, S:384],
                                 False, True)
                    fin(ins, u)
                elif s.name == "up":
                    if a == 0:
                        for x in steps:
                            if x.name in ("dyt", "attend"):
                                for q in range(x.nu):
                                    done_wait(pe, x.u + q)
                    for q in range(2):
                        tile_ready(s.k + q)
                        begin(u + q)
                        for m in range(2):
                            for kc in range(4):
                                c0 = kc * 256 + m * P
                                ins = mm3(bank(u + q)[:, m * S:m * S + S], w(s.k + q, c0, c0 + P),
                                          xs_(OT, 4 * q + kc), kc == 0, kc == 3)
                        fin(ins, u + q)
                    nx += 1
                elif s.name == "wout":
                    if a in (1, 3, 4):
                        wait_units(mixed)
                    rows_acc(XT if a == 0 else OT, range(KC), s.k, True, True, x_waits=a in (0, 2))
                elif s.name == "router":
                    pe.wait_ge(x_lo, nx)
                    begin(u)
                    for t in range(NT):
                        for kc in range(KC):
                            ins = mm(bank(u)[:, 64 * t:64 * t + 36], XF[:, kc, t * P:t * P + P],
                                     SMW[:, kc, 8:44], kc == 0, kc == 7)
                    fin(ins, u)
                elif s.name == "moe":
                    def expert_in(k, ub, it=None, x_waits=False):
                        rows_by_cols(XT, k, ub, it=it, per=MOE_PER, x_waits=x_waits)

                    def expert_tr(ub, it=None):
                        eu = 0 if it is None else it * MOE_PER["unit"]
                        done_wait(pe, ub, eu)
                        done_wait(pe, ub + 1, eu)
                        begin(ub + 2, eu)
                        for c in range(2):
                            for t in range(NT):
                                ins = tr(bank(ub + 2)[:, (2 * c + t) * P:(2 * c + t + 1) * P],
                                         AE[:, t, c * P:c * P + P])
                        fin(ins, ub + 2)

                    def down(ub, k, first, last, it=None):
                        done_wait(pe, ub + 2, 0 if it is None else it * MOE_PER["unit"])
                        rows_acc(OT, range(2), k, first, last, it, MOE_PER)

                    def one(e, it=None):
                        k = s.k + 4 + 6 * e
                        expert_in(k, u + 3 * (e + 1), it)
                        down(u + 3 * e, k + 4, e == 0, False, it)
                        expert_tr(u + 3 * (e + 1), it)

                    expert_in(s.k, u, x_waits=True)
                    expert_tr(u)
                    for e in range(3):
                        one(e)
                    with pe.Fori(0, 7) as it:
                        for e in range(3, 7):
                            one(e, it)
                    down(u + 3 * (EXPERTS - 1), s.k + s.nk - 2, False, True)
                elif s.name == "sb":
                    h, layer_sb = a, s.sb
                    if h == 0:
                        for x in steps:
                            if x.name in ("tblk", "nblk") and x.arg[0][0] == "s" and x.sb == layer_sb:
                                for q in range(x.nu):
                                    done_wait(pe, x.u + q)
                        mixed = []
                    if h < SBH:
                        r, c = 64 * (h % 2), h // 2
                        begin(u)
                        b = bank(u)
                        mm(b[:, 0:S], KT[r:r + 64, c, 0:P], QT[r:r + 64, c, :], True, True)
                        mm(b[:, S:S + P], KT[r:r + 64, c, P:S], QT[r:r + 64, c, P:S], False, True,
                           skip_group_check=True)
                        mm(b[:, 0:P], IDB[:], DROP[:], False, True, skip_group_check=True)
                        fin(mm(b[:, S:S + P], IDB[:], DROP[:], False, True, skip_group_check=True), u)
                        z_units[h] = u
                    if 2 <= h < SBH + 2:
                        nlogs += 1
                        pe.wait_ge(logs_ready, nlogs)
                        b, sp = bank(z_units[h - 2]), SPB[:, (h - 2) % 4, :]
                        mm(b[:, 0:S], cst("neg_ge"), sp[:, 0:S], False, True, skip_group_check=True)
                        mm(b[:, P:S], cst("neg_one"), sp[:, S:S + P], False, True, skip_group_check=True)
                        mm(b[:, S:S + P], cst("neg_ge"), sp[:, S:S + P], False, True,
                           skip_group_check=True).then_inc(z_full, 1)
                    if h >= 4 and h % 2 == 0:
                        v = s.u + s.nu - 1
                        mixed.append(v)
                        begin(v)
                        for hh in (h - 4, h - 3):
                            done_wait(pe, z_units[hh])
                            o = bank(v)[64 * (hh % 2):64 * (hh % 2) + 64, :]
                            mm(o[:, 0:S], VT[:, 0, 64 * hh:64 * hh + 64], WX[:, hh % 4, 0:S], True, False)
                            ins = mm(o[:, P:S], VT[:, 1, 64 * hh:64 * hh + 64], WX[:, hh % 4, S:S + P],
                                     False, True)
                        fin(ins, v)
                elif s.name == "galow":
                    pe.wait_ge(x_lo, nx)
                    hear_dve()
                    begin(u)
                    for kc in range(KC):
                        ins = mm(bank(u)[0:16, 0:S], SMW[:, kc, 44:60], XF[:, kc, :], kc == 0, kc == 7)
                    fin(ins, u)
                    galow = u
                elif s.name == "gates":
                    done_wait(pe, galow)
                    for t in range(NT):
                        begin(u + t)
                        fin(mm(bank(u + t)[:], ALT[0:17, t * P:t * P + P], GUP[:]), u + t)
                    gates = u
                elif s.name == "gcum":
                    for t in range(NT):
                        done_wait(pe, gates + t)
                    for q in range(2):
                        begin(u + q)
                        for h in (2 * q, 2 * q + 1):
                            for t in range(NT):
                                ins = mm(bank(u + q)[:, (h % 2) * S + t * P:(h % 2) * S + t * P + P],
                                         LG[:, t, h * P:h * P + P], TRI)
                        fin(ins, u + q)
                    begin(u + 2)
                    fin(mm(bank(u + 2)[:], cst("after"), LG[:, 0, :]), u + 2)
                    begin(u + 3)
                    for x in steps:
                        if x.name == "tblk" and x.arg[0] == "gk":
                            done_wait(pe, x.u)
                    for h in range(GH):
                        ins = tr(bank(u + 3)[:, h * P:h * P + P], GK[:, h, 0:P])
                    fin(ins, u + 3)
                elif s.name == "gscore":
                    hear_dve(3 if a == 0 else 1)
                    begin(u)
                    for t in range(NT):
                        for h in range(GH):
                            m = GSUB * (GH * t + h)
                            ins = mm(bank(u)[:, m:m + GSUB], KBB[:, a % 2, h, t * P:t * P + P],
                                     QGL[:, h, t * P + GSUB * a:t * P + GSUB * a + GSUB])
                    fin(ins, u)
                    gscores = gscores + [u] if a else [u]
                elif s.name == "gout":
                    wait_units(gscores)
                    for x in steps:
                        if x.name == "nblk" and x.arg[0] == "gv":
                            for q in range(2):
                                done_wait(pe, x.u + q)
                    for q in range(2):
                        begin(u + q)
                        for h in (2 * q, 2 * q + 1):
                            ins = mm(bank(u + q)[:, (h % 2) * 256:(h % 2) * 256 + 256],
                                     KDG[:, h * P:h * P + P], GV[:, 0, 256 * h:256 * h + 256])
                        fin(ins, u + q)
                    for q in range(4):
                        t = q // 2
                        if q == 2:
                            done_wait(pe, u)
                            done_wait(pe, u + 1)
                        begin(u + 2 + q)
                        for h in (2 * (q % 2), 2 * (q % 2) + 1):
                            o = bank(u + 2 + q)[:, (h % 2) * 256:(h % 2) * 256 + 256]
                            if t:
                                mm(o, QI[:, h, :], S1G[:, h, :], True, False)
                            ins = mm(o, STT[:, t, h, :], GV[:, t, 256 * h:256 * h + 256], t == 0, True)
                        fin(ins, u + 2 + q)
                elif s.name == "ffn":
                    def up(b, k, ub, it=None, x_waits=False):
                        rows_by_cols(XT, k, ub, it=it, per=FFN_PER, x_waits=x_waits)

                    def hid_tr(ub, nh, it=None):
                        eu = 0 if it is None else it * FFN_PER["unit"]
                        for t in range(NT):
                            pe.wait_ge(hid_ready, (0 if it is None else it * NT) + (nh + t + 1))
                            begin(ub + 2 + t, eu)
                            for c in range(4):
                                ins = tr(bank(ub + 2 + t)[:, c * P:c * P + P], HID[:, t, c * P:c * P + P])
                            fin(ins, ub + 2 + t)

                    def down(ub, k, first, last, it=None):
                        eu = 0 if it is None else it * FFN_PER["unit"]
                        done_wait(pe, ub + 2, eu)
                        done_wait(pe, ub + 3, eu)
                        rows_acc(OT, range(4), k, first, last, it, FFN_PER)

                    def one(b, it=None):
                        k = s.k + 4 + 8 * b
                        up(b + 1, k, u + 4 * (b + 1), it)
                        down(u + 4 * b, k + 4, b == 0, False, it)
                        hid_tr(u + 4 * (b + 1), nhid + NT * (b + 1), it)

                    up(0, s.k, u, x_waits=True)
                    hid_tr(u, nhid)
                    one(0)
                    with pe.Fori(0, FBLK - 2) as it:
                        one(1, it)
                    down(u + 4 * (FBLK - 1), s.k + s.nk - 4, False, True)
                    nhid += NT * FBLK
                if s.name == "tblk" and a[0] == "cb":
                    nx += 1
                    if a[1] == 3:
                        norm_u = None

        @block.vector
        def _(dve):
            chain = n_a2d = n_d2a = n_d2p = n_hi = nx = nvar = nacc = ngb = nz = nh = 0
            cc_units, pre_units, delta = {}, {}, {}

            def link(ins):
                nonlocal chain
                chain += 1
                return ins.then_inc(dve_chain, 1)

            def sync():
                dve.wait_ge(dve_chain, chain)

            def tell_act(ins):
                nonlocal n_d2a
                n_d2a += 1
                ins.then_inc(d2a, 1)

            def tell_pe(ins):
                nonlocal n_d2p
                n_d2p += 1
                ins.then_inc(d2p, 1)

            def hear_act(n=1):
                nonlocal n_a2d
                n_a2d += n
                dve.wait_ge(a2d, n_a2d)

            split = Splitter(make_lo)

            def v2(u):
                return bank(u)[:].rearrange("p (a b) -> p a b", a=2)

            def v4(u):
                return bank(u)[:].rearrange("p (a b) -> p a b", a=4)

            def free(ins, u):
                return ins.then_inc(done[u % WB], 1)

            def ev_lo(u, dst, hi, src, extra=0):
                nonlocal n_hi
                n_hi += 1
                dve.wait_ge(hi_out, extra + n_hi)
                free(dve.tensor_tensor(dst, src, hi.bitcast(F32), ALU.subtract), u)

            def x_rest(j, hi, lo):
                nonlocal nx
                nx += 1
                dve.wait_ge(x_hi, nx)
                dve.tensor_tensor(lo[:, 2 * j:2 * j + 2, :], XF[:, 2 * j:2 * j + 2, :],
                                  hi[:, 2 * j:2 * j + 2, :].bitcast(F32), ALU.subtract).then_inc(x_lo, 1)

            def sum_sq(col, x, junk):
                return dve.tensor_tensor_reduce(junk, x, x, 1.0, 0.0, ALU.mult, ALU.add,
                                                accum_out=SS[:, col:col + 1])

            def inv_rms(c0, n, scale):
                nonlocal nvar
                nvar += 1
                dve.tensor_scalar(VAR[:, (nvar - 1) % 2, 0:n], SS[:, c0:c0 + n], scale, EPS,
                                  ALU.mult, ALU.add).then_inc(var_ready, 1)
                return nvar

            def roots(req):
                dve.wait_ge(rs_ready, req)
                return RS[:, (req - 1) % 2, :]

            def ask(t, c0):
                hear_act()
                return inv_rms(c0 + t, 1, 1.0 / D)

            def update(t, row, req=None):
                nonlocal nh
                acc = ACC[:, 2 * t:2 * t + 2, :].rearrange("p a b -> p (a b)")
                dve.wait_ge(acc_full, 2 * nacc + 1 + t)
                if req is None:
                    ins = dve.tensor_tensor(XS[:, t, :], acc, row, ALU.mult)
                else:
                    ins = dve.scalar_tensor_tensor(XS[:, t, :], acc, roots(req)[:, 0:1], row,
                                                   ALU.mult, ALU.mult)
                ins.then_inc(acc_free, 1)
                dve.wait_ge(acc_free, 2 * nacc + 1 + t)
                dve.tensor_tensor(H[:, t, :], H[:, t, :], XS[:, t, :], ALU.add).then_inc(h_ready, 1)
                nh += 1

            def scale(t, req):
                tell_pe(dve.tensor_scalar(XS[:, t, :], H[:, t, :], roots(req)[:, 0:1], None, ALU.mult))

            def gb_row():
                nonlocal ngb
                dve.wait_ge(gb_loaded[ngb % 2], 16 * (ngb // 2 + 1))
                ngb += 1
                return GB[:, (ngb - 1) % 2, :]

            def col(v, n, w):
                return v.unsqueeze(2).broadcast_to([P, n, w])

            def level(lev):
                mask = cst("levels")[:, P * lev:P * lev + P]
                tell_pe(dve.tensor_tensor(NTL, NMT, over(mask, 8), ALU.mult))

            dve.wait_ge(load_const, 16 * NCONST)
            for s in steps:
                u, a = s.u, s.arg
                if s.name in ("tblk", "mod", "nblk", "up"):
                    split.upto(s.k + s.nk + SPL)
                elif s.name == "wout":
                    split.upto(s.k + s.nk)
                if s.name == "params":
                    full_wait(dve, u)
                    free(dve.tensor_copy(COLP[:], bank(u)[:, 0:ROWS1 + ROWS2]), u)
                    dve.memset(REL[32:33, :], 1.0).then_inc(rel_set, 1)
                    link(dve.memset(VAR[:], 1.0))
                    link(dve.memset(MH[:], -0.5))
                    link(dve.tensor_copy(IDB[:], IDENT))
                    link(dve.tensor_scalar(DROP[:], cst("strict"), 1.0, DROPPED, ALU.subtract, ALU.mult))
                    link(dve.memset(PRE[:, :, 0:3], 0.0))
                elif s.name == "cond":
                    hear_act()
                    tell_act(dve.tensor_copy(XF[:, :, 0:P], col(CC[:, 2, :], KC, P)))
                    nx += 1
                    dve.wait_ge(x_hi, nx)
                    dve.tensor_tensor(OTl[:, :, 0:P], XF[:, :, 0:P], OTh[:, :, 0:P].bitcast(F32),
                                      ALU.subtract).then_inc(x_lo, 1)
                elif s.name == "mod":
                    sec, half = divmod(a, 2)
                    j, kind = divmod(sec, 3)
                    full_wait(dve, u)
                    if kind == 2:
                        dve.wait_ge(gb_loaded[j], 16)
                        g = GB[:, j, 512 * half:512 * half + 512]
                        free(dve.tensor_tensor(g, bank(u)[:], g, ALU.add), u)
                    else:
                        row = 4 if kind else 2 * j
                        mc = MODC[:, row, 4 * half:4 * half + 4]
                        for i in range(4):
                            ins = dve.tensor_tensor_reduce(
                                area(4096, 4, P)[:, i, :], bank(u)[:, i * P:i * P + P], IDENT, 1.0, 0.0,
                                ALU.mult, ALU.add, accum_out=mc[:, i:i + 1])
                        free(ins, u)
                        done_wait(dve, u)
                        bm = COLP[:, R_BM + 8 * sec + 4 * half:][:, 0:4]
                        link(dve.tensor_tensor(mc, mc, bm, ALU.add))
                        if kind == 1:
                            sync()
                            nw = COLP[:, (R_N1, R_N2)[j] + 4 * half:][:, 0:4]
                            ins = dve.scalar_tensor_tensor(MODC[:, 2 * j + 1, 4 * half:4 * half + 4],
                                                           mc, 1.0, nw, ALU.add, ALU.mult)
                            if half:
                                tell_act(ins)
                elif s.name == "norm":
                    if a == 0:
                        req = [ask(t, 0) for t in range(NT)]
                        for t in range(NT):
                            scale(t, req[t])
                    if a in FULL_NORMS:
                        for q in range(4):
                            x_rest(q, XTh, XTl)
                    else:
                        for q in range(4):
                            nx += 1
                            dve.wait_ge(x_hi, nx)
                            for c in range(2):
                                ch = 2 * q + c
                                gain = COLP[:, R_PRE + 8 * (a - 2) + ch:][:, 0:1]
                                ins = dve.scalar_tensor_tensor(XTl[:, ch, :], v2(u + q)[:, c, :], gain,
                                                               XTh[:, ch, :].bitcast(F32),
                                                               ALU.mult, ALU.subtract)
                            free(ins, u + q)
                elif s.name == "ba":
                    full_wait(dve, u)
                    ba = bank(u)[:, 0:16].rearrange("p (t k h) -> p t k h", t=2, k=2)
                    dt = over(SROW[:, S_DT:S_DT + 4], 2)
                    link(dve.tensor_copy(BT[:, 0, :].rearrange("p (t h) -> p t h", t=2), ba[:, :, 0, :]))
                    free(dve.tensor_tensor(BT[:, 1, :].rearrange("p (t h) -> p t h", t=2),
                                           ba[:, :, 1, :], dt, ALU.add), u)
                    done_wait(dve, u)
                    tell_act(dve.tensor_scalar(BT[:, 7, :], BT[:, 1, :], 0.0, None, ALU.max))
                    hear_act()
                    link(dve.tensor_scalar(BT[:, 2, :], BT[:, 2, :], 1.0, None, ALU.add))
                    link(dve.tensor_tensor(BT[:, 7, :], BT[:, 7, :], BT[:, 5, :], ALU.add))
                    sync()
                    link(dve.reciprocal(BT[:, 2, :], BT[:, 2, :]))
                    link(dve.scalar_tensor_tensor(
                        BT[:, 7, :].rearrange("p (t h) -> p t h", t=2),
                        BT[:, 7, :].rearrange("p (t h) -> p t h", t=2), -1.0,
                        over(BT[:, 6, 0:4], 2), ALU.mult, ALU.mult))
                elif s.name == "conv":
                    done_wait(dve, pre_units[a])
                    for tap in range(4):
                        for ch in (2 * a, 2 * a + 1):
                            w = COLP[:, R_CW + 12 * tap + ch:][:, 0:1]
                            src = PRE[:, ch, tap:tap + S]
                            if tap == 0:
                                ins = dve.tensor_scalar(POST[:, ch, :], src, w, None, ALU.mult)
                            else:
                                ins = dve.scalar_tensor_tensor(POST[:, ch, :], src, w,
                                                               POST[:, ch, :], ALU.mult, ALU.add)
                        if tap < 3:
                            link(ins)
                            sync()
                        else:
                            ins.then_inc(conv_done, 1)
                elif s.name == "dtok":
                    for q in range(4):
                        done_wait(dve, u + q)
                        for h in range(HB):
                            link(sum_sq(4 * q + h, TOK[:, q // 2, q % 2, h * P:h * P + P],
                                        area(9252, 16, P)[:, 4 * q + h, :]))
                    sync()
                    norm_req = inv_rms(0, 16, 1.0)
                    for q in range(4, 6):
                        done_wait(dve, u + q)
                elif s.name == "decay":
                    sync()
                    tell_pe(dve.tensor_copy(NTL[:], col(BT[:, 7, :], 8, P)))
                    rqk = roots(norm_req)
                    link(dve.tensor_scalar(rqk[:, 0:8], rqk[:, 0:8], float(P) ** -0.5, None, ALU.mult))
                    hear_act()
                    free(dve.tensor_copy(GC[:], bank(u)[:, 0:24]), u)
                    done_wait(dve, u)
                elif s.name == "decay_rows":
                    for t in range(NT):
                        full_wait(dve, u + t)
                        if t == 1:
                            hear_act()
                        for h in range(HB):
                            m = 4 * t + h
                            ins = dve.tensor_scalar(DTI[:, m, :], bank(u + t)[:, h * P:h * P + P],
                                                    GC[:, m:m + 1], 0.0, ALU.subtract, ALU.min)
                        free(ins, u + t)
                elif s.name == "dtr":
                    k8 = TOK[:, 1, :, :].rearrange("p t (h d) -> p (t h) d", h=HB)
                    q8 = TOK[:, 0, :, :].rearrange("p t (h d) -> p (t h) d", h=HB)
                    v8 = TOK[:, 2, :, :].rearrange("p t (h d) -> p (t h) d", h=HB)
                    kb8 = KBK[:].rearrange("p t (h d) -> p (t h) d", h=HB)

                    def heads(v):
                        return v.rearrange("p (h d) -> p h d", h=HB)

                    tell_pe(dve.tensor_tensor(k8, k8, col(rqk[:, 8:16], 8, P), ALU.mult))
                    dve.wait_ge(d2p, n_d2p)
                    tell_pe(dve.tensor_tensor(kb8, k8, col(BT[:, 2, :], 8, P), ALU.mult))
                    tell_pe(dve.tensor_tensor(q8, q8, col(rqk[:, 0:8], 8, P), ALU.mult))
                    dve.wait_ge(d2p, n_d2p)
                    link(dve.tensor_tensor(heads(KBG), kb8[:, 4:8, :], col(EG[:, 4:8], 4, P), ALU.mult))
                    link(dve.tensor_tensor(heads(KD), k8[:, 0:4, :], col(EG[:, 8:12], 4, P), ALU.mult))
                    link(dve.tensor_tensor(v8, v8, col(BT[:, 2, :], 8, P), ALU.mult))
                    hear_act()
                    link(dve.tensor_tensor(DTI, DTI, over(TRI, 8), ALU.mult))
                    sync()
                    link(dve.tensor_tensor(DTS, DTI, over(cst("strict"), 8), ALU.mult))
                    link(dve.tensor_copy(XI, over(IDENT, 8)))
                    link(dve.tensor_copy(XTI, over(IDENT, 8)))
                    qnt_units = (u + 4, u + 5)
                elif s.name == "dmat":
                    sync()
                    for q in range(4):
                        kind, t = divmod(q, 2)
                        full_wait(dve, u + q)
                        dst, dec = (PTM, DTI) if kind else (NMT, DTS)
                        free(dve.tensor_tensor(dst[:, 4 * t:4 * t + 4, :], v4(u + q),
                                               dec[:, 4 * t:4 * t + 4, :], ALU.mult), u + q)
                    done_wait(dve, qnt_units[1])
                    done_wait(dve, u + 1)
                    link(dve.tensor_tensor(QGT.rearrange("p (h d) -> p h d", h=HB), QNT[:, 1],
                                           ER.rearrange("p (h d) -> p h d", h=HB), ALU.mult))
                    sync()
                    level(0)
                elif s.name == "inv_x":
                    for q in range(s.nu):
                        dst = XI if s.nu == 4 and q < 2 else XTI
                        d = dst[:, 4 * (q % 2):4 * (q % 2) + 4, :]
                        full_wait(dve, u + q)
                        if q % 2 == 0 and q == s.nu - 2:
                            full_wait(dve, u + q + 1)
                        free(dve.tensor_tensor(d, d, v4(u + q), ALU.subtract), u + q)
                    done_wait(dve, u + s.nu - 1)
                    if a < LEVELS - 1:
                        level(a + 1)
                elif s.name == "du":
                    delta["du"] = u
                elif s.name == "dnew":
                    full_wait(dve, u)
                    done_wait(dve, delta["du"] + 1)
                    free(dve.tensor_tensor(VNW.rearrange("p (h d) -> p h d", h=HB), UI[:, 4:8, :],
                                           v4(u), ALU.subtract), u)
                    delta["dnew"] = u
                elif s.name == "dnorm":
                    for x in steps:
                        if x.name == "nblk" and x.arg[0] == "z":
                            zu = x.u
                        if x.name == "dstate":
                            du0 = x.u
                        if x.name == "dout":
                            do = x.u
                    done_wait(dve, zu)
                    done_wait(dve, zu + 1)
                    z8 = ZS[:].rearrange("p t (h d) -> p (t h) d", h=HB)
                    link(dve.tensor_tensor(z8, z8, over(SROW[:, S_ON:S_ON + P], 8), ALU.mult))
                    done_wait(dve, du0)
                    done_wait(dve, do)
                    sync()
                    for t in range(NT):
                        for h in range(HB):
                            link(sum_sq(4 * t + h, OB[:, t, h * P:h * P + P], YI[:, 4 * t + h, :]))
                    sync()
                    rs = roots(inv_rms(0, 8, 1.0 / P))
                    for t in range(NT):
                        for h in range(HB):
                            o = OB[:, t, h * P:h * P + P]
                            ins = dve.scalar_tensor_tensor(o, o, rs[:, 4 * t + h:4 * t + h + 1],
                                                           ZS[:, t, h * P:h * P + P], ALU.mult, ALU.mult)
                    tell_pe(ins)
                elif s.name == "dyt":
                    for q in range(2):
                        ev_lo(u + q, OTl[:, 4 + 2 * q:6 + 2 * q, :], OTh[:, 4 + 2 * q:6 + 2 * q, :], v2(u + q))
                elif s.name == "score":
                    if a == 0:
                        dve.wait_ge(bias_read, 32)
                    g = a % 2
                    full_wait(dve, u)
                    free(dve.scalar_tensor_tensor(MS_[:, g, :], bank(u)[:, 0:384], HDA ** -0.5,
                                                  BIAS[:, a, :], ALU.mult, ALU.add), u)
                    done_wait(dve, u)
                    dve.tensor_reduce(SS[:, 2 * g:2 * g + 1], MS_[:, g, 0:P], AX, ALU.max, negate=True)
                    tell_act(dve.tensor_reduce(SS[:, 2 * g + 1:2 * g + 2], MS_[:, g, P:384], AX, ALU.max,
                                               negate=True))
                elif s.name == "probs":
                    g = a % 2
                    hear_act()
                    link(dve.reciprocal(RS2[:, g, :], RS2[:, g, :]))
                    sync()
                    dve.tensor_scalar(MP[:, g, 0:P], MP[:, g, 0:P], RS2[:, g, 0:1], None, ALU.mult)
                    tell_pe(dve.tensor_scalar(MP[:, g, P:384], MP[:, g, P:384], RS2[:, g, 1:2], None,
                                              ALU.mult))
                elif s.name == "attend":
                    ev_lo(u, OTl[:, a, :], OTh[:, a, :], bank(u)[:, 0:S])
                elif s.name == "up":
                    if a == 0:
                        for x in steps:
                            if x.name == "tblk" and x.arg[0] in ("ga", "gb"):
                                done_wait(dve, x.u)
                    full_wait(dve, u)
                    free(dve.tensor_tensor(MTMP, v2(u), SGA[:, 2 * a:2 * a + 2, :], ALU.mult), u)
                    full_wait(dve, u + 1)
                    xp = XF[:, 2 * a:2 * a + 2, :]
                    free(dve.tensor_tensor(xp, v2(u + 1), SGB[:, 2 * a:2 * a + 2, :], ALU.mult), u + 1)
                    done_wait(dve, u)
                    done_wait(dve, u + 1)
                    dve.tensor_tensor(xp, xp, MTMP, ALU.add).then_inc(xf_ready, 1)
                    x_rest(a, XTh, XTl)
                elif s.name == "res1":
                    row = gb_row()
                    update(0, row)
                    split.upto(s.k + 1)
                    r0 = ask(0, 0)
                    update(1, row)
                    scale(0, r0)
                    split.upto(s.k + 2)
                    r1 = ask(1, 0)
                    scale(1, r1)
                    split.upto(s.k + 4)
                    nacc += 1
                elif s.name == "res2":
                    def final(t, req):
                        nonlocal nh
                        dve.scalar_tensor_tensor(H[:, t, :], H[:, t, :], roots(req)[:, 0:1], frow,
                                                 ALU.mult, ALU.mult).then_inc(h_ready, 1)
                        nh += 1

                    row = gb_row()
                    update(0, row)
                    update(1, row)
                    frow = gb_row()
                    f0 = ask(0, 4)
                    final(0, f0)
                    f1 = ask(1, 4)
                    final(1, f1)
                    r0 = ask(0, 0)
                    scale(0, r0)
                    r1 = ask(1, 0)
                    scale(1, r1)
                    split.upto(s.k + 4)
                    nacc += 1
                elif s.name == "router":
                    def r(c0, c1=None):
                        return RT[:, :, c0:c0 + 1 if c1 is None else c1]

                    def wide(c, w):
                        return r(c).broadcast_to([P, NT, w])

                    def op(o, x, y, f):
                        sync()
                        return link(dve.tensor_tensor(o, x, y, f))

                    def top(values, at_max, idx, onehot, w):
                        iota = over(cst("iota")[:, 0:w], NT)
                        sync()
                        link(dve.tensor_reduce(r(at_max), values, AX, ALU.max))
                        op(r(112, 112 + w), values, wide(at_max, w), ALU.is_lt)
                        sync()
                        link(dve.scalar_tensor_tensor(r(112, 112 + w), r(112, 112 + w), 8.0, iota,
                                                      ALU.mult, ALU.add))
                        sync()
                        link(dve.tensor_reduce(r(idx), r(112, 112 + w), AX, ALU.min))
                        op(onehot, iota, wide(idx, w), ALU.is_equal)

                    full_wait(dve, u)
                    free(dve.tensor_tensor(r(0, 36), bank(u)[:, 0:128].rearrange("p (t w) -> p t w", t=2)[:, :, 0:36],
                                           over(SROW[:, S_BR:S_BR + 36], NT), ALU.add), u)
                    done_wait(dve, u)
                    top(r(0, 4), 36, 52, r(48, 52), 4)
                    tell_act(dve.tensor_scalar(r(37), r(36), -1.0, None, ALU.mult))
                    for g in range(NG):
                        le = r(4 + 8 * g, 12 + 8 * g)
                        if g == 0:
                            op(r(56, 64), le, wide(48, 8), ALU.mult)
                        else:
                            op(r(120, 128), le, wide(48 + g, 8), ALU.mult)
                            op(r(56, 64), r(56, 64), r(120, 128), ALU.add)
                    top(r(56, 64), 64, 66, r(72, 80), 8)
                    sync()
                    link(dve.scalar_tensor_tensor(r(88, 96), r(72, 80), 2 * NEG, r(56, 64), ALU.mult, ALU.add))
                    top(r(88, 96), 65, 67, r(80, 88), 8)
                    sync()
                    tell_act(dve.tensor_tensor(r(97), r(65), r(64), ALU.subtract))
                    hear_act(3)
                    link(dve.reciprocal(r(45), r(44)))
                    sync()
                    link(dve.tensor_scalar(r(99), r(98), 1.0, None, ALU.add))
                    sync()
                    link(dve.reciprocal(r(100), r(99)))
                    op(r(101), r(100), r(45), ALU.mult)
                    op(r(102), r(101), r(98), ALU.mult)
                    op(r(104, 112), r(72, 80), wide(101, 8), ALU.mult)
                    op(r(120, 128), r(80, 88), wide(102, 8), ALU.mult)
                    op(r(104, 112), r(104, 112), r(120, 128), ALU.add)
                    for g in range(NG):
                        op(COMB[:, :, 8 * g:8 * g + 8], r(104, 112), wide(48 + g, 8), ALU.mult)
                    sync()
                elif s.name == "moe":
                    def gated(e, ub, it=None):
                        extra = 0 if it is None else 8 * it
                        for t in range(NT):
                            dve.wait_ge(a2d, extra + (n_a2d + 2 * e + t + 1))
                            if it is None:
                                wt = COMB[:, t, e:e + 1]
                            else:
                                wt = COMB[:, t, bass.ds(4 * it + e, 1)]
                            free(dve.scalar_tensor_tensor(AE[:, t, :], SG[:, t, :], wt,
                                                          bank(ub + t)[:, 256:512], ALU.mult, ALU.mult), ub + t)

                    def t_lo(ut, extra=0):
                        ev_lo(ut, OTl[:, 0:2, :], OTh[:, 0:2, :], v2(ut), extra)

                    def one(e, k, ub, it=None):
                        for kk in (k + 4, k + 5):
                            make_lo(kk, it, MOE_PER)
                        gated(e + 1, ub, it)
                        for kk in range(k + 6, k + 10):
                            make_lo(kk, it, MOE_PER)
                        t_lo(ub + 2, 0 if it is None else 4 * it)

                    split.upto(s.k + 4)
                    gated(0, u)
                    split.upto(s.k + 8)
                    t_lo(u + 2)
                    for e in range(3):
                        one(e, s.k + 4 + 6 * e, u + 3 * (e + 1))
                    with dve.Fori(0, 7) as it:
                        for e in range(3, 7):
                            one(e, s.k + 4 + 6 * e, u + 3 * (e + 1), it)
                    n_hi += 4 * 6
                    split.next = s.k + s.nk + 2
                    n_a2d += 2 * EXPERTS
                elif s.name == "post":
                    row = gb_row()
                    p0 = ask(0, 4)
                    update(0, row, p0)
                    split.upto(s.k + 2)
                    if a == ("ffn", 3):
                        p1 = ask(1, 4)
                        update(1, row, p1)
                    else:
                        r0 = ask(0, 0)
                        p1 = ask(1, 4)
                        scale(0, r0)
                        update(1, row, p1)
                        split.upto(s.k + 3)
                        r1 = ask(1, 0)
                        scale(1, r1)
                        split.upto(s.k + 4)
                    nacc += 1
                elif s.name == "ffn":
                    def square(ub, extra=0):
                        for t in range(NT):
                            done_wait(dve, ub + t, extra)
                            dve.tensor_tensor(HID[:, t, :], HID[:, t, :], HID[:, t, :], ALU.mult)\
                                .then_inc(hid_ready, 1)

                    def t_lo(ut, extra=0):
                        for t in range(NT):
                            tt = slice(t * P, t * P + P)
                            ev_lo(ut + t, OTl[:, 0:4, tt], OTh[:, 0:4, tt], v4(ut + t), extra)

                    def one(b, k, ub, it=None):
                        for kk in range(k + 4, k + 8):
                            make_lo(kk, it, FFN_PER)
                        square(ub, 0 if it is None else it * FFN_PER["unit"])
                        for kk in range(k + 8, k + 12):
                            make_lo(kk, it, FFN_PER)
                        t_lo(ub + 2, 0 if it is None else 2 * it)

                    split.upto(s.k + 4)
                    square(u)
                    split.upto(s.k + 8)
                    t_lo(u + 2)
                    one(0, s.k + 4, u + 4)
                    with dve.Fori(0, FBLK - 2) as it:
                        one(1, s.k + 12, u + 8, it)
                    n_hi += 2 * (FBLK - 3)
                    split.next = s.k + s.nk
                elif s.name == "sb":
                    h = a
                    if h < SBH:
                        hear_act()
                        b = h % 4
                        dve.scalar_tensor_tensor(SPB[:, b, :], bank(u)[:, 0:384], 0.0, LN[:, b, :],
                                                 ALU.max, ALU.add).then_inc(logs_ready, 1)
                    if h >= 4 and h % 2 == 0:
                        v, c = s.u + s.nu - 1, (h - 4) // 2
                        ev_lo(v, OTl[:, c, :], OTh[:, c, :], bank(v)[:, 0:S])
                elif s.name == "tblk":
                    kind, c = a
                    if kind == "pre":
                        pre_units[c] = u
                    elif kind == "cc":
                        cc_units[c] = u
                        if c == 0:
                            link(dve.memset(HP[:, :, 0:2], 0.0))
                    elif kind == "cu":
                        done_wait(dve, cc_units[c])
                        full_wait(dve, u)
                        free(dve.tensor_tensor(HP[:, 2 * c:2 * c + 2, 2:2 + S], v2(u),
                                               CB[:, 2 * c:2 * c + 2, :], ALU.mult), u)
                        if c == 0:
                            sync()
                        done_wait(dve, u)
                        for tap in range(3):
                            for ch in (2 * c, 2 * c + 1):
                                w = COLP[:, R_CW2 + 8 * tap + ch:][:, 0:1]
                                src = HP[:, ch, tap:tap + S]
                                if tap == 0:
                                    ins = dve.tensor_scalar(CV[:, ch, :], src, w, None, ALU.mult)
                                else:
                                    ins = dve.scalar_tensor_tensor(CV[:, ch, :], src, w, CV[:, ch, :],
                                                                   ALU.mult, ALU.add)
                            link(ins)
                            if tap < 2:
                                sync()
                    elif kind == "cb":
                        sync()
                        full_wait(dve, u)
                        free(dve.tensor_tensor(XF[:, 2 * c:2 * c + 2, :], v2(u), CV[:, 2 * c:2 * c + 2, :], ALU.mult), u)
                        x_rest(c, OTh, OTl)
                elif s.name == "galow":
                    tell_pe(dve.memset(ALT[0:17, :], 1.0))
                elif s.name == "gates":
                    for t in range(NT):
                        hear_act()
                        free(dve.scalar_tensor_tensor(LG[:, t, :], bank(u + t)[:], 0.0, GTM[:, t, :],
                                                      ALU.min, ALU.subtract), u + t)
                elif s.name == "gcum":
                    gcum, score_units = u, {}
                    link(dve.memset(REF[:, :, 0:1], 0.0))
                    done_wait(dve, u)
                    done_wait(dve, u + 1)
                    cum8 = CUM[:].rearrange("p h (t i) -> p (h t) i", t=NT)
                    link(dve.tensor_copy(REF[:, :, 1:4], cum8[:, :, GSUB - 1:P - 1:GSUB]))
                elif s.name == "gkeys":
                    if a == 0:
                        sync()
                        cum32 = CUM[:].rearrange("p h (b i) -> p (h b) i", i=GSUB)
                        ref32 = REF[:].rearrange("p a b -> p (a b)")
                        qgl = QGL[:].rearrange("p h (b i) -> p (h b) i", i=GSUB)
                        tell_act(dve.tensor_tensor(qgl, cum32, col(ref32, 32, GSUB), ALU.subtract))
                    if a >= 2:
                        dve.wait_ge(full[score_units[a - 2] % WB], score_units[a - 2] // WB + 1)
                    kb = KBB[:, a % 2].rearrange("p h (t i) -> p (h t) i", t=NT)
                    link(dve.tensor_tensor(kb, cum8, REF[:, :, a:a + 1].broadcast_to([P, GH * NT, P]),
                                           ALU.subtract))
                    sync()
                    tell_act(dve.tensor_scalar(kb, kb, -GCLAMP, None, ALU.max))
                    if a == 0:
                        hear_act()
                        link(dve.tensor_tensor(QI, QI, GQ[:, :, P:S], ALU.mult))
                        hear_act()
                        tell_pe(dve.tensor_tensor(QGL, QGL, GQ, ALU.mult))
                        done_wait(dve, gcum + 2)
                        done_wait(dve, gcum + 3)
                        tell_pe(dve.tensor_tensor(KDG, KTK, ES, ALU.mult))
                    hear_act()
                    tell_pe(dve.tensor_tensor(KBB[:, a % 2], KBB[:, a % 2], GK, ALU.mult))
                elif s.name == "gscore":
                    score_units[a] = u
                    full_wait(dve, u)
                    i = slice(GSUB * a, GSUB * a + GSUB)
                    free(dve.tensor_tensor(STT[:].rearrange("p t h i -> p (t h) i")[:, :, i],
                                           bank(u)[:, 0:S].rearrange("p (m i) -> p m i", i=GSUB),
                                           over(TRI[:, i], 8), ALU.mult), u)
                elif s.name == "gout":
                    gout_units = u
                    row = gb_row()
                    for x in steps:
                        if x.name == "nblk" and x.arg[0] == "gg":
                            done_wait(dve, x.u)
                            done_wait(dve, x.u + 1)
                    for t in range(NT):
                        ins = dve.tensor_tensor(GG[:, t, :], GG[:, t, :], row, ALU.mult)
                    ins.then_inc(gb_free, 1)
                elif s.name == "gyt":
                    for q in range(4):
                        done_wait(dve, gout_units + 2 + q)
                    for t in range(NT):
                        for h in range(GH):
                            link(sum_sq(4 * t + h, XS[:, t, 256 * h:256 * h + 256],
                                        area(0, 8, 256)[:, 4 * t + h, :]))
                    sync()
                    rs = roots(inv_rms(0, 8, 1.0 / 256))
                    dve.wait_ge(gb_free, 1)
                    for t in range(NT):
                        for h in range(GH):
                            o = XS[:, t, 256 * h:256 * h + 256]
                            ins = dve.scalar_tensor_tensor(o, o, rs[:, 4 * t + h:4 * t + h + 1],
                                                           GG[:, t, 256 * h:256 * h + 256],
                                                           ALU.mult, ALU.mult)
                    tell_pe(ins)
                    for q in range(4):
                        ev_lo(u + q, OTl[:, 2 * q:2 * q + 2, :], OTh[:, 2 * q:2 * q + 2, :], v2(u + q))


def pack(i):
    win = i["w_in"][0]
    gains = i["norm_gains_2"]
    steps = schedule()
    prows = np.concatenate([
        i["norm1_w"].reshape(8, P), i["norm2_w"].reshape(8, P), i["b_mod"].reshape(48, P),
        np.stack([gains[:, 0], gains[:, 2]], axis=1).reshape(64, P),
        i["conv_w"].reshape(48, P), i["conv_w_2"].reshape(24, P)])
    bm = i["b_mod"].reshape(6, D)
    smw = np.concatenate([win[:, C_BA:C_BA + 8], i["w_rg"][0], i["w_re"][0],
                          i["gla_w_in_2"][0][:, 3 * D:3 * D + 16]], axis=1)
    return {k: np.ascontiguousarray(v) for k, v in {
        "x": i["x"], "weights": weight_tiles(i, steps), "cst": constants()[0], "prows": prows,
        "c": i["c"],
        "srow": np.concatenate([i["dt_bias"].ravel(), i["a_log"].ravel(), i["b_rg"].ravel(),
                                i["b_re"].ravel(), i["onorm_w"].ravel()]),
        "smw": smw.reshape(KC, P, 60).transpose(1, 0, 2),
        "gup": np.concatenate([i["gla_w_gate_up_2"][0], i["gla_b_gate_2"]]),
        "rel_bias": i["rel_bias"], "oh": bucket_rows(),
        "brow": np.concatenate([bm[2:3], bm[5:6], i["final_norm_w"].reshape(1, D),
                                np.stack([gains[:, 1], gains[:, 3]], axis=1).reshape(8, D),
                                i["gla_head_norm_2"].reshape(1, D)]),
    }.items()}


def kernel(**inputs):
    import concourse.bacc as _bacc
    from concourse.bass_utils import run_bass_kernel_spmd as _run

    arrays = pack({n: np.asarray(a) for n, a in inputs.items()})
    nc = _bacc.Bacc("TRN2", target_bir_lowering=False, num_devices=1)
    aps = {n: nc.dram_tensor("in_" + n, a.shape, F32, kind="ExternalInput").ap()
           for n, a in arrays.items()}
    aps["out"] = nc.dram_tensor("out", (1, S, D), F32, kind="ExternalOutput").ap()
    build(nc, aps)
    r = _run(nc, [{"in_" + n: a for n, a in arrays.items()}], core_ids=[0])
    return r.results[0]["out"]
```

```python
from contextlib import ExitStack

import numpy as np
import concourse.bass as bass
from concourse import mybir

F32 = mybir.dt.float32
F32R = mybir.dt.float32r
BF16 = mybir.dt.bfloat16
ALU = mybir.AluOpType
ACT = mybir.ActivationFunctionType
AX = mybir.AxisListType.X

P = 128
D = 1024
KC = D // P
S = 256
NT = S // P
EPS = 1e-6
NEG = -1e30

HA, HDA = 8, 64
HB = 4
NG, NE, FE = 4, 8, 256
EXPERTS = NG * NE
FF = 4096
FBLK = FF // 512
SBH = 16
GH = 4
DROPPED = 2.0 ** 100
GSUB = 32
GCLAMP = 60.0
LEVELS = 7

FULL_NORMS = (0, 1, 6)

RAW = 8
SPL = 4
WB = 4

C_QA, C_KA, C_VA, C_QKVB, C_Z, C_BA, C_GA, C_GB = 0, 512, 1024, 1536, 3072, 3584, 3592, 4616


class Step:

    def __init__(self, name, arg, nu, nk):
        self.name, self.arg, self.nu, self.nk = name, arg, nu, nk
        self.u = self.k = 0
        self.sb = 0


def schedule():
    st = []

    def add(name, arg=None, nu=0, nk=0, sb=0):
        st.append(Step(name, arg, nu, nk))
        st[-1].sb = sb

    def mod(n):
        add("mod", n, 1, 4)
        add("modcols", n)

    add("cond")
    add("mod", 0, 1, 4)
    add("params", None, 1)
    add("modcols", 0)
    for n in range(1, 4):
        add("mod", n, 1, 4)
        add("modcols", n)
    add("norm", 0, 4)
    add("tblk", ("pre", 0), 1, 2)
    add("bias", None, 1)
    add("tblk", ("pre", 1), 1, 2)
    add("conv", 0)
    add("ba", None, 1)
    for c in range(2, 6):
        add("tblk", ("pre", c), 1, 2)
        add("conv", c - 1)
    add("conv", 5)
    mod(4)
    add("dtok", None, 6)
    add("decay", None, 1)
    add("decay_rows", None, 2)
    add("dtr", None, 6)
    add("dmat", None, 4)
    fill = {0: ("nblk", ("z", 0), 2, 4), 1: ("tblk", ("qa", 0), 1, 2), 2: ("tblk", ("qa", 1), 1, 2),
            3: ("tblk", ("ka", 0), 1, 2), 4: ("tblk", ("ka", 1), 1, 2), 5: ("tblk", ("ga", 0), 1, 2)}
    for lev in range(LEVELS):
        add("inv_y", lev, 2)
        mod(5 + lev)
        add("inv_x", lev, 4 if lev < LEVELS - 1 else 2)
        if lev in fill:
            add(*fill[lev])
    add("du", None, 3)
    add("tblk", ("ga", 1), 1, 2)
    add("dstate", None, 2)
    add("nblk", ("va", 0), 2, 4)
    add("dnew", None, 1)
    add("tblk", ("ga", 2), 1, 2)
    add("dout", None, 1)
    add("dnorm")
    add("tblk", ("ga", 3), 1, 2)
    add("dyt", None, 2)
    for g in range(HA + 1):
        if g < HA:
            add("score", g, 1)
        if g > 0:
            add("probs", g - 1, 1)
        if g % 2 and g < HA:
            add("tblk", ("gb", g // 2), 1, 2)
        elif g > 0:
            add("up", ("b", g // 2 - 1), 1, 1)
            add("attend", g // 2 - 1, 1)
    for c in range(4):
        add("up", ("a", c), 1, 1)
    add("wout", 0, 0, 8)
    add("res1")
    add("norm", 1, 4)
    add("router", None, 2)
    add("gather", 0, 4)
    add("shares", None, 1)
    add("ein", 0, 1, 4)
    add("selt", None, 3)
    add("etr", 0, 1)
    for e in range(1, EXPERTS):
        if e == EXPERTS // 2:
            add("gather", 1, 4)
            add("edown", e - 1, 0, 2)
            add("yout", e // NE - 1)
            add("ein", e, 1, 4)
        else:
            add("ein", e, 1, 4)
            add("edown", e - 1, 0, 2)
            if e % NE == 0:
                add("yout", e // NE - 1)
        add("etr", e, 1)
    add("edown", EXPERTS - 1, 0, 2)
    add("yout", NG - 1)
    add("overflow")
    add("scatter")
    add("res2")
    for layer in range(4):
        add("norm", 2 + 2 * layer, 4)
        if layer in (0, 3):
            for d in ("sq", "sk"):
                for c in range(4):
                    add("tblk", (d, c), 1, 2, layer // 3)
            for c in range(2):
                add("nblk", ("sv", c), 2, 4, layer // 3)
            for h in range(SBH + 3):
                add("sb", h, h < SBH, 0, layer // 3)
        elif layer == 1:
            for d in ("cc", "cu", "cb"):
                for c in range(4):
                    add("tblk", (d, c), 1, 2)
        else:
            add("galow", None, 1)
            add("tblk", ("gq", 0), 1, 2)
            add("gates", None, 2)
            add("tblk", ("gq", 1), 1, 2)
            for c in range(2):
                add("tblk", ("gk", c), 1, 2)
            add("gcum", None, 4)
            for b in range(4):
                add("gkeys", b)
                add("nblk", (("gv", "gg")[b // 2], b % 2), 2, 4)
                add("gscore", b, 1)
            add("gout", None, 6)
            add("gyt", None, 4)
        add("wout", layer + 1, 0, 8)
        add("post", ("mix", layer))
        add("norm", 3 + 2 * layer, 4)
        add("ffn", layer, FBLK * 4, FBLK * 8)
        add("post", ("ffn", layer))
    u = k = 0
    for s in st:
        s.u, s.k = u, k
        u += s.nu
        k += s.nk
    return st


def release_plan(steps):
    rel, used, acc = {}, 0, 0

    def count(k):
        nonlocal used
        used += 1
        rel[k] = ("used", used)

    def unit(k, u):
        rel[k] = ("unit", u)

    for s in steps:
        k = s.k
        if s.name == "up":
            unit(k, s.u)
        elif s.name in ("tblk", "mod", "nblk"):
            for j in range(s.nk - 1):
                count(k + j)
            unit(k + s.nk - 1, s.u + s.nu - 1)
        elif s.name == "wout":
            for j in range(7):
                count(k + j)
            acc += 1
            rel[k + 7] = ("acc", 2 * acc)
        elif s.name == "ein":
            for j in range(3):
                count(k + j)
            unit(k + 3, s.u)
        elif s.name == "edown":
            count(k)
            if s.arg % NE == NE - 1:
                rel[k + 1] = ("y", s.arg // NE + 1)
            else:
                count(k + 1)
        elif s.name == "scatter":
            acc += 1
        elif s.name == "ffn":
            blocks, nd, per = FBLK, 4, 4
            for b in range(blocks + 1):
                if b < blocks:
                    for j in range(3):
                        count(k + j)
                    unit(k + 3, s.u + per * b + 1)
                    k += 4
                if b > 0:
                    for j in range(nd):
                        if b == blocks and j == nd - 1:
                            acc += 1
                            rel[k + j] = ("acc", 2 * acc)
                        else:
                            count(k + j)
                    k += nd
    return rel


def tile_t(w, c):
    b = w[:, c:c + 256].reshape(2, 4, P, 256)
    return [x.transpose(1, 0, 2).reshape(P, 1024) for x in b]


def tile_n(w, c):
    b = w[:, c:c + 512].reshape(4, 2, P, 512)
    return [x.transpose(1, 0, 2).reshape(P, 1024) for x in b]


def tile_rows(w):
    return list(w.reshape(-1, P, 1024))


def weight_tiles(i, steps):
    out = []
    win = i["w_in"][0]
    for s in steps:
        if s.name == "mod":
            out += tile_n(i["w_mod"][0], 512 * s.arg)
        elif s.name in ("tblk", "nblk"):
            kind, c = s.arg
            layer3 = s.sb
            w, c0 = {
                "pre": (win, C_QKVB), "qa": (win, C_QA), "ka": (win, C_KA), "va": (win, C_VA),
                "z": (win, C_Z), "ga": (win, C_GA), "gb": (win, C_GB),
                "sq": (i["sb_w_qkv_2"][layer3], 0), "sk": (i["sb_w_qkv_2"][layer3], D),
                "sv": (i["sb_w_qkv_2"][layer3], 2 * D),
                "cb": (i["conv_w_in_2"][0], 0), "cc": (i["conv_w_in_2"][0], D),
                "cu": (i["conv_w_in_2"][0], 2 * D),
                "gq": (i["gla_w_in_2"][0], 0), "gk": (i["gla_w_in_2"][0], 512),
                "gv": (i["gla_w_in_2"][0], D), "gg": (i["gla_w_in_2"][0], 2 * D),
            }[kind]
            out += tile_t(w, c0 + 256 * c) if s.name == "tblk" else tile_n(w, c0 + 512 * c)
        elif s.name == "up":
            kind, c = s.arg
            b = i["w_up_" + kind][0][:, 256 * c:256 * c + 256].reshape(4, P, 256)
            out.append(b.transpose(1, 0, 2).reshape(P, 1024))
        elif s.name == "wout":
            w = [i["w_out"][0], i["sb_w_o_2"][0], i["conv_w_out_2"][0], i["gla_w_o_2"][0],
                 i["sb_w_o_2"][1]][s.arg]
            out += tile_rows(w)
        elif s.name == "ein":
            g, x = divmod(s.arg, NE)
            out += tile_n(np.concatenate([i["w_e_gate"][0, g, x], i["w_e_up"][0, g, x]], axis=1), 0)
        elif s.name == "edown":
            g, x = divmod(s.arg, NE)
            out += tile_rows(i["w_e_down"][0, g, x])
        elif s.name == "ffn":
            up, down = i["ffn_w_up_2"][s.arg], i["ffn_w_down_2"][s.arg]
            for b in range(FBLK + 1):
                if b < FBLK:
                    out += tile_n(up, 512 * b)
                if b > 0:
                    out += tile_rows(down[512 * (b - 1):512 * b])
    return np.ascontiguousarray(np.stack(out))


def constants():
    j = np.arange(P)[:, None]
    i = np.arange(P)[None, :]
    parts = {
        "ident": (i == j), "tri": (j <= i), "neg_ge": -1.0 * (j >= i), "neg_one": -np.ones((P, P)),
        "after": (j > i), "strict": (i > j), "one": np.ones((P, P)),
        "levels": np.concatenate([((i >> (v + 1)) == (j >> (v + 1))) & ((i >> v) & 1 == 1)
                                  & ((j >> v) & 1 == 0) for v in range(LEVELS)], axis=1),
        "cols": np.broadcast_to(i, (P, P)),
        "iota": np.broadcast_to(np.arange(NE)[None, :], (P, NE)),
    }
    at, cols = {}, 0
    for n, a in parts.items():
        at[n] = (cols, a.shape[1])
        cols += a.shape[1]
    return np.concatenate([np.asarray(a, np.float32) for a in parts.values()], axis=1), at


def bucket_rows():
    m = np.arange(512)
    n = np.maximum(255 - m, 0)
    nf = np.maximum(n, 1).astype(np.float32)
    large = 16 + (np.log(nf / np.float32(16)) / np.float32(np.log(8.0)) * np.float32(16)).astype(np.int32)
    b = np.where(n < 16, n, np.minimum(large, 31))
    rows = np.zeros((33, 512), np.float32)
    rows[b, m] = 1.0
    rows[:, m > 255] = 0.0
    rows[32, m > 255] = NEG
    return rows


R_N1, R_N2, R_BM, R_PRE, R_CW, R_CW2 = 0, 8, 16, 64, 128, 176
ROWS1, ROWS2 = 128, 72
B_G1, B_G2, B_FINAL, B_POST, B_HEAD = 0, 1, 2, 3, 11
S_DT, S_AL, S_BR, S_ON, S_W = 0, 4, 8, 44, 172


def build(nc, aps, dbg=None):
    steps = schedule()
    rel = release_plan(steps)
    cst_host, cst_at = constants()
    NCST = cst_host.shape[1]
    NTILES = sum(s.nk for s in steps)
    NUNITS = sum(s.nu for s in steps)
    wall, out = aps["weights"], aps["out"]
    bias_rows = nc.dram_tensor("bias_rows", (HA, P, 512), F32, kind="Internal")

    with ExitStack() as ctx:
        def sb(name, shape, dt=F32):
            return ctx.enter_context(nc.sbuf_tensor("s_" + name, shape, dt))

        def sem(name):
            return ctx.enter_context(nc.semaphore(name))

        raw = sb("raw", [P, RAW, 1024])
        whi = sb("whi", [P, SPL, 1024], F32R)
        wlo = sb("wlo", [P, SPL, 1024], F32R)
        H = sb("h", [P, NT, D])
        XS = sb("xs", [P, NT, D])
        XF = sb("xf", [P, KC, S])
        XTh, XTl = sb("xth", [P, KC, S], F32R), sb("xtl", [P, KC, S], F32R)
        OTh, OTl = sb("oth", [P, KC, S], F32R), sb("otl", [P, KC, S], F32R)
        GB = sb("gb", [P, 2, D])
        CST = sb("cst", [P, NCST])
        COLP = sb("colp", [P, ROWS1 + ROWS2])
        SROW = sb("srow", [P, S_W])
        SMW = sb("smw", [P, KC, 60])
        GUP = sb("gup", [17, 512])
        CC = sb("cc", [P, 3, KC])
        MODC = sb("modc", [P, 5, KC])
        SS = sb("ss", [P, 16])
        VAR = sb("var", [P, 2, 16])
        RS = sb("rs", [P, 2, 16])
        MH = sb("mh", [P, 16])
        IDB, DROP = sb("idb", [P, P], BF16), sb("drop", [P, P], BF16)
        BA = sb("ba", [P, 2, 8])
        BT = sb("bt", [P, 8, 8])
        GC = sb("gc", [P, 24])
        EG = sb("eg", [P, 24])
        REL = sb("rel", [33, HA])
        RT = sb("rt", [P, 2, 160])
        JUNK = sb("junk", [P, 4, P])
        OVX = sb("ovx", [P, 2])
        OVF, OVI = sb("ovf", [P, 4]), sb("ovi", [P, 2], mybir.dt.int32)
        AR = sb("arena", [P, 15648])

        def area(start, *shape):
            n = int(np.prod(shape))
            v = AR[:, start:start + n]
            if len(shape) == 1:
                return v
            names = "abcd"[:len(shape)]
            pat = f"p ({' '.join(names)}) -> p {' '.join(names)}"
            return v.rearrange(pat, **dict(zip(names, shape)))

        def cst(name):
            a, w = cst_at[name]
            return CST[:, a:a + w]

        IDENT, TRI = cst("ident"), cst("tri")

        def over(v, n):
            return v.unsqueeze(1).broadcast_to([P, n, v.shape[1]])

        PRE, POST = area(0, 12, 259), area(3108, 12, S)
        KNT, KBT, QNT = area(0, 2, HB, P), area(1024, 2, HB, P), area(2048, 2, HB, P)
        DTI, DTS, NMT = area(3108, 8, P), area(4132, 8, P), area(5156, 8, P)
        TOK = area(6180, 3, NT, 512)
        KBK = area(9252, NT, 512)
        KBG, KD = area(10276, 512), area(10788, 512)
        ER, WT, S1B, VNW = area(11300, 512), area(11812, 512), area(12324, 512), area(12836, 512)
        PTM = area(13348, 8, P)
        NTL = area(14372, 8, P)
        QGT = area(11300, 512)
        XI = XS[:, 0, :].rearrange("p (a b) -> p a b", a=8)
        XTI = XS[:, 1, :].rearrange("p (a b) -> p a b", a=8)
        YI = XF[:, 0:4, :].rearrange("p a b -> p (a b)").rearrange("p (a b) -> p a b", a=8)
        UI = XF[:, 4:8, :].rearrange("p a b -> p (a b)").rearrange("p (a b) -> p a b", a=8)
        ZS = area(7204, NT, 512)
        OB = area(6180, NT, 512)
        QAT, KAT, VA = area(0, 4, S), area(1024, 4, S), area(2048, NT, 512)
        BIAS = area(9252, HA, 384)
        MS_, MP = area(3108, 2, 384), area(8228, 2, 384)
        MPT = area(13348, 4, 384)
        BST = area(8228, 512)[0:HA]
        PR, OH = area(10276, 2, P), area(10788, 512)[0:33]
        SGA, SGB = area(4132, KC, S), area(6180, KC, S)
        MTMP = area(0, 2, 2, S)
        SEL, SELT = area(0, NT, NG + 1, P), area(1280, NG + 1, S)
        YG = area(2560, NG + 1, D)
        SG, AE = area(7680, 256), area(7936, 256)
        OVW, OVT = area(8192, 6, D), area(14336, 2, P)
        CG = area(14592, (NG + 1) * NE)
        HID = area(0, NT, 512)
        QT, KT, VT = area(0, KC, S), area(2048, KC, S), area(4096, NT, D)
        AB, LN, SPB, WX = (area(6144 + 1536 * i, 4, 384) for i in range(4))
        CB, HP, CV = area(0, KC, S), area(2048, KC, 258), area(4112, KC, S)
        GQ, GK, GV, GG = area(0, GH, S), area(1024, GH, S), area(2048, NT, D), area(4096, NT, D)
        ALT = area(6144, S)
        LG, CUM, QGL = area(6400, NT, 512), area(7424, GH, S), area(8448, GH, S)
        KBB = area(9472, 2, GH, S)
        STT = area(11520, NT, GH, P)
        QI, KDG, KTK, ES = area(12544, GH, P), area(13056, 512), area(13568, 512), area(14080, 512)
        S1G = area(14592, GH, 256)
        REF = area(15616, GH * NT, 4)
        GTM = area(14592, NT, 512)

        work = [ctx.enter_context(nc.psum_tensor(f"work{b}", [P, 512], F32)) for b in range(WB)]
        ACC = ctx.enter_context(nc.psum_tensor("acc", [P, 4, 512], F32))

        load_c, load_const, load_rest = sem("load_c"), sem("load_const"), sem("load_rest")
        loaded = [sem(f"loaded{i}") for i in range(RAW)]
        hi_made, lo_made, used = sem("hi_made"), sem("lo_made"), sem("used")
        full = [sem(f"full{b}") for b in range(WB)]
        done = [sem(f"done{b}") for b in range(WB)]
        acc_full, acc_free = sem("acc_full"), sem("acc_free")
        hi_out = sem("hi_out")
        x_hi, x_lo = sem("x_hi"), sem("x_lo")
        xf_ready = sem("xf_ready")
        var_ready, rs_ready = sem("var_ready"), sem("rs_ready")
        h_ready = sem("h_ready")
        gb_loaded, gb_free = [sem("gb_loaded0"), sem("gb_loaded1")], sem("gb_free")
        act_chain, dve_chain = sem("act_chain"), sem("dve_chain")
        a2d, d2a = sem("act_to_dve"), sem("dve_to_act")
        d2p = sem("dve_to_pe")
        z_full = sem("z_full")
        hid_ready = sem("hid_ready")
        conv_ready = sem("conv_ready")
        RS2 = sb("rs2", [P, 2, 2])
        bias_written = sem("bias_written")
        bias_read = [sem("bias_read0"), sem("bias_read1")]
        logs_ready = sem("logs_ready")
        sums_full, sums_free = sem("sums_full"), sem("sums_free")
        y_full, y_free = sem("y_full"), sem("y_free")
        y_zero = sem("y_zero")
        ov_known, ov, ov_loaded = sem("ov_known"), sem("ov"), sem("ov_loaded")
        rel_set = sem("rel_set")
        conv_done = sem("conv_done")
        out_sem = sem("out_written")

        def full_wait(eng, u, extra=0):
            eng.wait_ge(full[u % WB], u // WB + 1 + extra)

        def done_wait(eng, u, extra=0):
            eng.wait_ge(done[u % WB], u // WB + 1 + extra)

        def bank(u):
            return work[u % WB]

        block = ctx.enter_context(nc.Block())

        N_UPDATES = sum({"res1": 1, "post": 1, "res2": 2}.get(s.name, 0) for s in steps)
        NCONST, NREST = 3, 6

        @block.sync
        def _(sp):
            def load(dst, src, signal):
                with nc.allow_non_contiguous_dma("small parameters"):
                    sp.dma_start(dst, src).then_inc(signal, 16)

            def load_tile(k):
                if k >= RAW:
                    sp.wait_ge(lo_made, k - RAW + 1)
                sp.dma_start(raw[:, k % RAW, :], wall[k]).then_inc(loaded[k % RAW], 16)

            load(CC[:, 0, :], aps["c"].rearrange("b (k p) -> p (b k)", p=P), load_c)
            for k in range(4):
                load_tile(k)
            load(PR[:, 0, :], aps["prows"][0:ROWS1, :], load_const)
            load(PR[0:ROWS2, 1, :], aps["prows"][ROWS1:ROWS1 + ROWS2, :], load_const)
            load(CST[:], aps["cst"], load_const)
            for k in range(4, 12):
                load_tile(k)
            for dst, src in (
                (H[:], aps["x"].rearrange("b (t p) d -> p (b t) d", p=P)),
                (SROW[:], aps["srow"].partition_broadcast(P)),
                (SMW[:], aps["smw"]), (GUP[:], aps["gup"]), (REL[0:32, :], aps["rel_bias"]),
                (OH[:], aps["oh"]),
            ):
                load(dst, src, load_rest)
            first = NTILES % RAW + 2 * RAW
            for k in range(12, first):
                load_tile(k)
            with sp.Fori(0, (NTILES - first) // RAW) as it:
                for j in range(RAW):
                    k = first + j
                    sp.wait_ge(lo_made, it * RAW + (k - RAW + 1))
                    sp.dma_start(raw[:, k % RAW, :], wall[it * RAW + k]).then_inc(loaded[k % RAW], 16)
            for t in range(NT):
                sp.wait_ge(h_ready, 2 * N_UPDATES - 1 + t)
                sp.dma_start(out[0, t * P:(t + 1) * P, :], H[:, t, :]).then_inc(out_sem, 16)
            sp.wait_ge(out_sem, 16 * NT)

        def tile_wait(eng, k, it=None, per=None):
            kind, v = rel[k]
            extra = 0 if it is None else it * per[kind]
            if kind == "used":
                eng.wait_ge(used, v + extra)
            elif kind == "acc":
                eng.wait_ge(acc_full, v)
            elif kind == "y":
                eng.wait_ge(y_full, v)
            else:
                full_wait(eng, v, extra)

        class Splitter:

            def __init__(self, one):
                self.next, self.one = 0, one

            def upto(self, k):
                while self.next < min(k, NTILES):
                    self.one(self.next)
                    self.next += 1

        def make_hi(k, it=None, per=None):
            act = nc.scalar
            nr = 0 if it is None else it * (16 * per["tiles"] // RAW)
            act.wait_ge(loaded[k % RAW], 16 * (k // RAW + 1) + nr)
            if k >= SPL:
                tile_wait(act, k - SPL, it, per)
            act.copy(whi[:, k % SPL, :], raw[:, k % RAW, :]).then_inc(hi_made, 1)

        def make_lo(k, it=None, per=None):
            dve = nc.vector
            n = 0 if it is None else it * per["tiles"]
            dve.wait_ge(hi_made, n + (k + 1))
            dve.tensor_tensor(wlo[:, k % SPL, :], raw[:, k % RAW, :],
                              whi[:, k % SPL, :].bitcast(F32), ALU.subtract).then_inc(lo_made, 1)

        FFN_PER = {"tiles": 8, "used": 7, "unit": 1}

        def post_row(which, layer):
            return B_POST + 2 * layer + (which == "ffn")

        gb_rows, gb_freed = [B_G1, B_G2, B_FINAL], [(h_ready, 2), (h_ready, 4), (h_ready, 6)]
        for layer in range(4):
            if layer == 2:
                gb_rows.append(B_HEAD)
                gb_freed.append((gb_free, 1))
            gb_rows += [post_row("mix", layer), post_row("ffn", layer)]
            gb_freed += [(h_ready, 8 + 4 * layer), (h_ready, 10 + 4 * layer)]

        @block.gpsimd
        def _(pool):
            asked = uses = loads = 0

            def load_rows():
                nonlocal loads
                while loads < min(uses + 2, len(gb_rows)):
                    if loads >= 2:
                        pool.wait_ge(*gb_freed[loads - 2])
                    pool.dma_start(GB[:, loads % 2, :], aps["brow"][gb_rows[loads]].partition_broadcast(P))\
                        .then_inc(gb_loaded[loads % 2], 16)
                    loads += 1

            def inv_sqrt(w):
                nonlocal asked
                asked += 1
                pool.wait_ge(var_ready, asked)
                i = (asked - 1) % 2
                pool.tensor_tensor(RS[:, i, 0:w], VAR[:, i, 0:w], MH[:, 0:w], ALU.pow).then_inc(rs_ready, 1)

            load_rows()
            roots = {"dtok": 1, "dnorm": 1, "gyt": 1, "res1": 2, "res2": 4}
            for s in steps:
                n = roots.get(s.name, 0)
                if s.name == "post":
                    n = 2 if s.arg == ("ffn", 3) else 4
                elif s.name == "norm" and s.arg == 0:
                    n = 2
                for _ in range(n):
                    inv_sqrt({"dtok": 16, "dnorm": 8, "gyt": 8}.get(s.name, 1))
                if s.name == "norm":
                    load_rows()
                if s.name == "bias":
                    done_wait(pool, s.u)
                    with nc.allow_non_contiguous_dma("rows"):
                        pool.dma_start(bias_rows.ap(), BST.unsqueeze(1).broadcast_to([HA, P, 512]))\
                            .then_inc(bias_written, 16)
                if s.name == "overflow":
                    pool.wait_ge(ov_known, 1)
                    flag = pool.value_load(OVI[0:1, 0:1], min_val=0, max_val=1)
                    group = pool.value_load(OVI[0:1, 1:2], min_val=0, max_val=NG - 1)
                    with pool.If(flag > 0):
                        with pool.Fori(0, NE) as e:
                            pool.wait_ge(ov, e * 7 + 2)
                            pool.dma_start(OVW, aps["experts"][group * NE + e]).then_inc(ov_loaded, 16)
                if s.name == "du":
                    inv_done = s.u
                if s.name in ("dnew", "dyt"):
                    pool.wait_ge(bias_written, 16)
                    half = s.name == "dyt"
                    if half:
                        done_wait(pool, s.u + 1)
                    else:
                        done_wait(pool, inv_done + 2)
                    for t in range(NT):
                        src = bass.AP(tensor=bias_rows, offset=255 - P * t + half * 4 * P * 512,
                                      ap=[[511, P], [P * 512, 4], [1, P * (t + 1)]])
                        pool.dma_start(BIAS[:, 4 * half:4 * half + 4, P * t:P * t + P * (t + 1)], src)\
                            .then_inc(bias_read[half], 16)
                if s.name in ("res1", "gyt"):
                    uses += 1
                elif s.name == "post":
                    uses += 1
                elif s.name == "res2":
                    uses += 2

        @block.scalar
        def _(act):
            chain = n_a2d = n_d2a = n_hi = nx = nacc = nxf = nh = nz = 0
            z_units = {}

            def link(ins):
                nonlocal chain
                chain += 1
                ins.then_inc(act_chain, 1)

            def sync():
                act.wait_ge(act_chain, chain)

            def tell_dve(ins):
                nonlocal n_a2d
                n_a2d += 1
                ins.then_inc(a2d, 1)

            def hear_dve():
                nonlocal n_d2a
                n_d2a += 1
                act.wait_ge(d2a, n_d2a)

            split = Splitter(make_hi)

            def ev_hi(u, dst, src=None, extra=0):
                full_wait(act, u, extra)
                src = bank(u)[:] if src is None else src
                act.copy(dst, src).then_inc(hi_out, 1)

            def ev(u, dst, func=ACT.Copy, src=None, scale=1.0):
                full_wait(act, u)
                act.activation(dst, bank(u)[:] if src is None else src, func, scale=scale)\
                    .then_inc(done[u % WB], 1)

            def x_split(j, dst):
                nonlocal nx
                act.copy(dst[:, 2 * j:2 * j + 2, :], XF[:, 2 * j:2 * j + 2, :]).then_inc(x_hi, 1)
                nx += 1

            def sum_sq(dst, src, t):
                junk = XF[:, 4 * t:4 * t + 4, :].rearrange("p a b -> p (a b)")
                tell_dve(act.activation(junk, src, ACT.Square, accum_out=dst))

            def sum_sq_h(t, col):
                nonlocal nh
                nh += 1
                act.wait_ge(h_ready, nh)
                sum_sq(SS[:, col + t:col + t + 1], H[:, t, :], t)

            def v2(u):
                return bank(u)[:].rearrange("p (a b) -> p a b", a=2)

            def v4(u):
                return bank(u)[:].rearrange("p (a b) -> p a b", a=4)

            for s in steps:
                u, a = s.u, s.arg
                if s.name in ("tblk", "mod", "nblk", "up"):
                    split.upto(s.k + s.nk + SPL)
                elif s.name == "wout":
                    split.upto(s.k + s.nk)
                if s.name == "modcols" and a in (3, 9):
                    hear_dve()
                elif s.name == "cond":
                    act.wait_ge(load_c, 16)
                    link(act.activation(CC[:, 1, :], CC[:, 0, :], ACT.Silu))
                    sync()
                    tell_dve(act.copy(CC[:, 2, :], CC[:, 1, :]))
                    hear_dve()
                    act.copy(OTh[:, :, 0:P], XF[:, :, 0:P]).then_inc(x_hi, 1)
                    nx += 1
                elif s.name in ("norm", "gather"):
                    j = 1 if s.name == "gather" else a
                    if j == 0:
                        act.wait_ge(load_rest, 16 * NREST)
                        for t in range(NT):
                            sum_sq(SS[:, t:t + 1], H[:, t, :], t)
                    for q in range(4):
                        full_wait(act, u + q)
                        for c in range(2):
                            ch = 2 * q + c
                            if j < 2:
                                sc, bi = MODC[:, 2 * j + 1, ch:ch + 1], MODC[:, 2 * j, ch:ch + 1]
                            else:
                                sc, bi = COLP[:, R_PRE + 8 * (j - 2) + ch:][:, 0:1], 0.0
                            dst = XF if j in FULL_NORMS else XTh
                            keep = s.name == "norm" and j == 1
                            ins = act.activation(dst[:, ch, :], v2(u + q)[:, c, :], ACT.Identity,
                                                 bias=bi, scale=sc)
                        if j in FULL_NORMS:
                            ins.then_inc(done[(u + q) % WB], 1)
                            if not keep:
                                done_wait(act, u + q)
                                x_split(q, XTh)
                        else:
                            ins.then_inc(x_hi, 1)
                            nx += 1
                elif s.name == "bias":
                    ev(u, BST, src=bank(u)[0:HA, :])
                elif s.name == "tblk":
                    kind, c = a
                    if kind == "pre":
                        ev(u, PRE[:, 2 * c:2 * c + 2, 3:259], src=v2(u))
                    elif kind in ("qa", "ka"):
                        ev(u, (QAT if kind == "qa" else KAT)[:, 2 * c:2 * c + 2, :], src=v2(u))
                    elif kind in ("ga", "gb"):
                        ev(u, (SGA if kind == "ga" else SGB)[:, 2 * c:2 * c + 2, :], ACT.Sigmoid, v2(u))
                    elif kind in ("sq", "gq"):
                        ev(u, (QT if kind == "sq" else GQ)[:, 2 * c:2 * c + 2, :], src=v2(u),
                           scale=0.125 if kind == "sq" else float(P) ** -0.5)
                    elif kind in ("sk", "gk"):
                        ev(u, (KT if kind == "sk" else GK)[:, 2 * c:2 * c + 2, :], src=v2(u))
                    elif kind == "cc":
                        ev(u, CB[:, 2 * c:2 * c + 2, :], src=v2(u))
                    elif kind == "cb":
                        done_wait(act, u)
                        x_split(c, OTh)
                elif s.name == "nblk":
                    kind, c = a
                    for t in range(NT):
                        dst = {"z": ZS, "va": VA}[kind][:, t, :] if kind in ("z", "va") else \
                            {"sv": VT, "gv": GV, "gg": GG}[kind][:, t, 512 * c:512 * c + 512]
                        ev(u + t, dst, ACT.Silu if kind in ("z", "gg") else ACT.Copy)
                elif s.name == "ba":
                    hear_dve()
                    act.preload_act_table_set("natural_log_exp_and_others")
                    link(act.activation(BT[:, 2, :], BT[:, 0, :], ACT.Exp, scale=-1.0))
                    link(act.activation(BT[:, 3, :], BT[:, 1, :], ACT.Abs))
                    link(act.activation(BT[:, 6, 0:4], SROW[:, S_AL:S_AL + 4], ACT.Exp))
                    sync()
                    link(act.activation(BT[:, 4, :], BT[:, 3, :], ACT.Exp, scale=-1.0))
                    sync()
                    tell_dve(act.activation(BT[:, 5, :], BT[:, 4, :], ACT.Ln, bias=1.0))
                elif s.name == "conv":
                    act.wait_ge(conv_done, a + 1)
                    act.activation(POST[:, 2 * a:2 * a + 2, :], POST[:, 2 * a:2 * a + 2, :],
                                   ACT.Silu).then_inc(conv_ready, 1)
                elif s.name == "dtok":
                    act.wait_ge(bias_written, 16)
                    for q in range(6):
                        ev(u + q, TOK[:, q // 2, q % 2, :])
                elif s.name == "decay":
                    full_wait(act, u)
                    act.activation(EG[:], bank(u)[:, 0:24], ACT.Exp).then_inc(a2d, 1)
                    n_a2d += 1
                elif s.name == "decay_rows":
                    full_wait(act, u + 1)
                    tell_dve(act.activation(ER, bank(u + 1)[:], ACT.Exp))
                    done_wait(act, u)
                    done_wait(act, u + 1)
                    tell_dve(act.activation(DTI, DTI, ACT.Exp))
                elif s.name == "dtr":
                    for q in range(6):
                        ev(u + q, (KNT, KBT, QNT)[q // 2][:, q % 2], src=v4(u + q))
                elif s.name == "inv_y":
                    for q in range(2):
                        ev(u + q, YI[:, 4 * q:4 * q + 4, :], src=v4(u + q))
                elif s.name == "du":
                    for q in range(2):
                        ev(u + q, UI[:, 4 * q:4 * q + 4, :], src=v4(u + q))
                    ev(u + 2, WT)
                elif s.name == "dstate":
                    ev(u, OB[:, 0, :])
                    ev(u + 1, S1B)
                elif s.name == "dout":
                    ev(u, OB[:, 1, :])
                elif s.name in ("dyt", "gyt"):
                    for q in range(s.nu):
                        c0 = 4 + 2 * q if s.name == "dyt" else 2 * q
                        ev_hi(u + q, OTh[:, c0:c0 + 2, :], v2(u + q))
                elif s.name == "score":
                    g = a % 2
                    hear_dve()
                    act.activation(MP[:, g, 0:P], MS_[:, g, 0:P], ACT.Exp, bias=SS[:, 2 * g:2 * g + 1],
                                   accum_out=RS2[:, g, 0:1])
                    tell_dve(act.activation(MP[:, g, P:384], MS_[:, g, P:384], ACT.Exp,
                                            bias=SS[:, 2 * g + 1:2 * g + 2], accum_out=RS2[:, g, 1:2]))
                elif s.name == "probs":
                    ev(u, MPT[:, a % 4, :], src=bank(u)[:, 0:384])
                elif s.name == "attend":
                    ev_hi(u, OTh[:, a, :], bank(u)[:, 0:S])
                elif s.name == "up" and a[0] == "a":
                    nxf += 1
                    act.wait_ge(xf_ready, nxf)
                    x_split(a[1], XTh)
                elif s.name == "router":
                    hear_dve()
                    for t in range(NT):
                        r = RT[:, t, :]
                        tell_dve(act.activation(r[:, 40:44], r[:, 0:4], ACT.Exp, bias=r[:, 37:38],
                                                accum_out=r[:, 44:45]))
                    hear_dve()
                    tell_dve(act.activation(RT[:, :, 98:99], RT[:, :, 97:98], ACT.Exp))
                elif s.name == "post":
                    for t in range(NT):
                        act.wait_ge(acc_full, 2 * nacc + 1 + t)
                        sum_sq(SS[:, 4 + t:5 + t], ACC[:, 2 * t:2 * t + 2, :].rearrange("p a b -> p (a b)"), t)
                        if t == 0:
                            split.upto(s.k + 2)
                        if a != ("ffn", 3):
                            sum_sq_h(t, 0)
                            split.upto(s.k + 3 + t)
                    nacc += 1
                elif s.name == "res1":
                    nacc += 1
                    for t in range(NT):
                        sum_sq_h(t, 0)
                        split.upto(s.k + 2 + 2 * t)
                elif s.name == "res2":
                    nacc += 1
                    for col, t in ((4, 0), (4, 1), (0, 0), (0, 1)):
                        sum_sq_h(t, col)
                    split.upto(s.k + 4)
                elif s.name == "sb":
                    h = a
                    if h < SBH:
                        if h == 0:
                            act.preload_act_table_set("natural_log_exp_and_others")
                        b = h % 4
                        full_wait(act, u)
                        link(act.activation(AB[:, b, :], bank(u)[:, 0:384], ACT.Abs))
                        sync()
                        link(act.activation(AB[:, b, :], AB[:, b, :], ACT.Exp, scale=-1.0))
                        sync()
                        tell_dve(act.activation(LN[:, b, :], AB[:, b, :], ACT.Ln, bias=1.0))
                        z_units[h] = u
                    if 2 <= h < SBH + 2:
                        nz += 1
                        act.wait_ge(z_full, nz)
                        w = z_units[h - 2]
                        act.activation(WX[:, (h - 2) % 4, :], bank(w)[:, 0:384], ACT.Exp)\
                            .then_inc(done[w % WB], 1)
                    if h >= 4 and h % 2 == 0:
                        c = (h - 4) // 2
                        act.wait_ge(sums_full, 8 * s.sb + c + 1)
                        act.copy(OTh[:, c, :], ACC[:, c % 4, 0:S]).then_inc(hi_out, 1)
                elif s.name == "galow":
                    ev(u, ALT[0:16, :], src=bank(u)[0:16, 0:S])
                elif s.name == "gates":
                    act.preload_act_table_set("natural_log_exp_and_others")
                    for t in range(NT):
                        full_wait(act, u + t)
                        link(act.activation(GTM[:, t, :], bank(u + t)[:], ACT.Abs))
                        sync()
                        link(act.activation(GTM[:, t, :], GTM[:, t, :], ACT.Exp, scale=-1.0))
                        sync()
                        tell_dve(act.activation(GTM[:, t, :], GTM[:, t, :], ACT.Ln, bias=1.0))
                elif s.name == "gcum":
                    for q in range(2):
                        ev(u + q, CUM[:, 2 * q:2 * q + 2, :], src=v2(u + q), scale=1.0 / 16)
                    ev(u + 2, ES, ACT.Exp, scale=1.0 / 16)
                    ev(u + 3, KTK)
                    done_wait(act, u)
                    done_wait(act, u + 1)
                    tell_dve(act.activation(QI, CUM[:, :, P:S], ACT.Exp))
                elif s.name == "gkeys":
                    if a == 0:
                        hear_dve()
                        tell_dve(act.activation(QGL, QGL, ACT.Exp))
                    hear_dve()
                    tell_dve(act.activation(KBB[:, a % 2], KBB[:, a % 2], ACT.Exp, scale=-1.0))
                elif s.name == "gout":
                    for q in range(2):
                        ev(u + q, S1G[:, 2 * q:2 * q + 2, :], src=v2(u + q))
                    for q in range(4):
                        ev(u + 2 + q, XS[:, q // 2, 512 * (q % 2):512 * (q % 2) + 512])
                elif s.name == "ein":
                    split.upto(s.k + 6)
                    full_wait(act, u)
                    tell_dve(act.activation(SG, bank(u)[:, 0:256], ACT.Silu))
                elif s.name == "edown":
                    split.upto(s.k + 6)
                elif s.name == "etr":
                    ev_hi(u, OTh[:, 0:2, 0:P], bank(u)[:, 0:256].rearrange("p (a b) -> p a b", a=2))
                elif s.name == "selt":
                    for q in range(3):
                        n = min(2, NG + 1 - 2 * q)
                        ev(u + q, SELT[:, 2 * q:2 * q + n, :],
                           src=bank(u + q)[:, 0:S * n].rearrange("p (a b) -> p a b", a=n))
                elif s.name == "yout":
                    act.wait_ge(y_full, a + 1)
                    b = 2 * (a % 2)
                    act.copy(YG[:, a, :], ACC[:, b:b + 2, :].rearrange("p a b -> p (a b)")).then_inc(y_free, 1)
                elif s.name == "overflow":
                    act.wait_ge(ov_known, 1)
                    flag = act.value_load(OVI[0:1, 0:1], min_val=0, max_val=1)
                    with act.If(flag > 0):
                        act.wait_ge(ov, 1)
                        for q in range(2):
                            for c in range(4):
                                ch = 4 * q + c
                                ins = act.activation(XF[:, ch, 0:P], work[q][:, c * P:c * P + P], ACT.Identity,
                                                     bias=MODC[:, 2, ch:ch + 1], scale=MODC[:, 3, ch:ch + 1])
                        ins.then_inc(ov, 1)
                        with act.Fori(0, NE) as e:
                            act.wait_ge(ov, e * 7 + 3)
                            act.activation(SG, work[0][:, 0:256], ACT.Silu).then_inc(ov, 1)
                            act.wait_ge(ov, e * 7 + 6)
                            act.copy(OVT, work[1][:, 0:256].rearrange("p (a b) -> p a b", a=2)).then_inc(ov, 1)
                elif s.name == "ffn":
                    def relu(ub, extra=0):
                        for t in range(NT):
                            full_wait(act, ub + t, extra)
                            act.activation(HID[:, t, :], bank(ub + t)[:], ACT.Relu)\
                                .then_inc(done[(ub + t) % WB], 1)

                    def t_hi(ut, extra=0):
                        for t in range(NT):
                            ev_hi(ut + t, OTh[:, 0:4, t * P:t * P + P], v4(ut + t), extra)

                    def one(b, k, ub, it=None):
                        extra = 0 if it is None else it * FFN_PER["unit"]
                        for kk in range(k + 4, k + 8):
                            make_hi(kk, it, FFN_PER)
                        relu(ub, extra)
                        for kk in range(k + 8, k + 12):
                            make_hi(kk, it, FFN_PER)
                        t_hi(ub + 2, extra)

                    split.upto(s.k + 4)
                    relu(u)
                    split.upto(s.k + 8)
                    t_hi(u + 2)
                    one(0, s.k + 4, u + 4)
                    with act.Fori(0, FBLK - 2) as it:
                        one(1, s.k + 12, u + 8, it)
                    split.next = s.k + s.nk

        @block.tensor
        def _(pe):
            nx = n_d2p = nacc = nhid = 0
            nlogs, norm_u, z_units = 0, None, {}

            def hear_dve(n=1):
                nonlocal n_d2p
                n_d2p += n
                pe.wait_ge(d2p, n_d2p)

            def begin(u, extra=0):
                if u >= WB:
                    done_wait(pe, u - WB, extra)

            def x_wait(j):
                if norm_u is None:
                    pe.wait_ge(x_lo, nx - 3 + j)
                else:
                    done_wait(pe, norm_u + j)

            def wait_units(units):
                for x in units:
                    done_wait(pe, x)

            def fin(ins, u):
                ins.then_inc(full[u % WB], 1)

            def mm(o, lhs, rhs, start=True, stop=True, **kw):
                return pe.matmul(o, lhs, rhs, start=start, stop=stop, **kw)

            def mm3(o, lhs, rhs, start, stop):
                mm(o, lhs[0], rhs[0], start, False)
                mm(o, lhs[0], rhs[1], False, False)
                return mm(o, lhs[1], rhs[0], False, stop)

            def tr(o, x):
                return pe.transpose(o, x, IDENT[0:x.shape[0], 0:x.shape[0]])

            def w(k, a, b):
                return whi[:, k % SPL, a:b], wlo[:, k % SPL, a:b]

            def xs_(t, kc, a=None, b=None):
                h, l = t
                if a is None:
                    return h[:, kc, :], l[:, kc, :]
                return h[:, kc, a:b], l[:, kc, a:b]

            XT, OT = (XTh, XTl), (OTh, OTl)

            def tile_ready(k, extra=0):
                pe.wait_ge(lo_made, extra + (k + 1))

            def rows_by_cols(x, k, u, nt=NT, it=None, per=None, x_waits=False, c0=0):
                ek = 0 if it is None else it * per["tiles"]
                eu = 0 if it is None else it * per["unit"]
                for t in range(nt):
                    begin(u + t, eu)
                for j in range(4):
                    tile_ready(k + j, ek)
                    if x_waits:
                        x_wait(j)
                    for kc in (2 * j, 2 * j + 1):
                        for t in range(nt):
                            ins = mm3(bank(u + t)[:], xs_(x, kc, c0 + t * P, c0 + t * P + P),
                                      w(k + j, 512 * (kc % 2), 512 * (kc % 2) + 512), kc == 0, kc == 7)
                            if kc == 7:
                                fin(ins, u + t)
                    if j < 3:
                        ins.then_inc(used, 1)

            def rows_acc(x, kcs, k, first, last, it=None, per=None, x_waits=False):
                nonlocal nacc
                ek = 0 if it is None else it * per["tiles"]
                if first:
                    if nacc:
                        pe.wait_ge(acc_free, 2 * nacc)
                    nacc += 1
                n, kcs = len(kcs), list(kcs)

                def product(j, t):
                    for c in range(2):
                        ins = mm3(ACC[:, 2 * t + c, :], xs_(x, kcs[j], t * P, t * P + P),
                                  w(k + j, 512 * c, 512 * c + 512),
                                  first and j == 0, last and j == n - 1)
                    return ins

                tail = min(n, SPL) if last else 0
                for j in range(n - tail):
                    tile_ready(k + j, ek)
                    if x_waits:
                        x_wait(j // 2)
                    for t in range(NT):
                        ins = product(j, t)
                    ins.then_inc(used, 1)
                for t in range(NT if tail else 0):
                    for j in range(n - tail, n):
                        tile_ready(k + j, ek)
                        if x_waits:
                            x_wait(j // 2)
                        ins = product(j, t)
                        if j == n - 1:
                            ins.then_inc(acc_full, 1)
                        elif t == NT - 1:
                            ins.then_inc(used, 1)

            for s in steps:
                u, a = s.u, s.arg
                if s.name == "params":
                    pe.wait_ge(load_const, 16 * NCONST)
                    tr(bank(u)[:, 0:ROWS1], PR[:, 0, :])
                    fin(tr(bank(u)[:, ROWS1:ROWS1 + ROWS2], PR[0:ROWS2, 1, :]), u)
                elif s.name == "cond":
                    nx += 1
                elif s.name == "mod":
                    pe.wait_ge(x_lo, 1)
                    rows_by_cols(OT, s.k, u, nt=1)
                elif s.name == "norm":
                    for t in range(NT):
                        hear_dve()
                        for q in range(4):
                            if t == 0:
                                begin(u + q)
                            for c in range(2):
                                ins = tr(bank(u + q)[:, (2 * c + t) * P:(2 * c + t + 1) * P],
                                         XS[:, t, (2 * q + c) * P:(2 * q + c + 1) * P])
                            if t == NT - 1:
                                fin(ins, u + q)
                    norm_u = None if a in FULL_NORMS and a != 1 else u
                    if norm_u is None:
                        nx += 4
                elif s.name == "bias":
                    pe.wait_ge(load_rest, 16 * NREST)
                    pe.wait_ge(rel_set, 1)
                    begin(u)
                    fin(mm(bank(u)[0:HA, :], REL[:], OH[:]), u)
                elif s.name == "tblk":
                    begin(u)
                    for m in range(2):
                        for kc in range(KC):
                            if m == 0 and kc % 2 == 0:
                                x_wait(kc // 2)
                            if m == 0 and kc % 4 == 0:
                                tile_ready(s.k + kc // 4)
                            c0 = (kc % 4) * 256 + m * P
                            ins = mm3(bank(u)[:, m * S:m * S + S], w(s.k + kc // 4, c0, c0 + P),
                                      xs_(XT, kc), kc == 0, kc == 7)
                            if m == 1 and kc == 3:
                                ins.then_inc(used, 1)
                    fin(ins, u)
                elif s.name == "nblk":
                    rows_by_cols(XT, s.k, u, x_waits=True)
                elif s.name == "ba":
                    pe.wait_ge(x_lo, nx)
                    begin(u)
                    for t in range(NT):
                        for kc in range(KC):
                            ins = mm(bank(u)[:, 8 * t:8 * t + 8], XF[:, kc, t * P:t * P + P],
                                     SMW[:, kc, 0:8], kc == 0, kc == 7)
                    fin(ins, u)
                elif s.name == "dtok":
                    for q in range(6):
                        sec, t = divmod(q, 2)
                        pe.wait_ge(conv_ready, 2 * sec + 2)
                        begin(u + q)
                        for h in range(HB):
                            ins = tr(bank(u + q)[:, h * P:h * P + P],
                                     POST[:, 4 * sec + h, t * P:t * P + P])
                        fin(ins, u + q)
                elif s.name == "decay":
                    hear_dve()
                    begin(u)
                    for q, m in enumerate(("tri", "after", "one")):
                        for t in range(NT):
                            ins = mm(bank(u)[:, 8 * q + 4 * t:8 * q + 4 * t + 4], cst(m),
                                     BT[:, 7, 4 * t:4 * t + 4])
                    fin(ins, u)
                elif s.name == "decay_rows":
                    for t in range(NT):
                        begin(u + t)
                        for h in range(HB):
                            ins = mm(bank(u + t)[:, h * P:h * P + P], NTL[:, 4 * t + h, :], TRI)
                        fin(ins, u + t)
                elif s.name == "dtr":
                    for q in range(6):
                        kind, t = divmod(q, 2)
                        if t == 0:
                            hear_dve()
                        begin(u + q)
                        src = (TOK[:, 1, t, :], KBK[:, t, :], TOK[:, 0, t, :])[kind]
                        for h in range(HB):
                            ins = tr(bank(u + q)[:, h * P:h * P + P], src[:, h * P:h * P + P])
                        fin(ins, u + q)
                elif s.name == "dmat":
                    for q in range(4):
                        kind, t = divmod(q, 2)
                        done_wait(pe, u - 4 + q)
                        if q == 0:
                            done_wait(pe, u - 6)
                            done_wait(pe, u - 5)
                        begin(u + q)
                        for h in range(HB):
                            ins = mm(bank(u + q)[:, h * P:h * P + P], KNT[:, t, h, :],
                                     (QNT if kind else KBT)[:, t, h, :])
                        fin(ins, u + q)
                elif s.name == "inv_y":
                    hear_dve()
                    for q in range(2):
                        begin(u + q)
                        for h in range(4):
                            ins = mm(bank(u + q)[:, h * P:h * P + P], NTL[:, 4 * q + h, :],
                                     XI[:, 4 * q + h, :])
                        fin(ins, u + q)
                    y_units = (u, u + 1)
                elif s.name == "inv_x":
                    x_units = u
                    for q in range(s.nu):
                        if q < 2:
                            done_wait(pe, y_units[q])
                        begin(u + q)
                        m0 = 4 * (q % 2)
                        xy = s.nu == 4 and q < 2
                        for h in range(4):
                            ins = mm(bank(u + q)[:, h * P:h * P + P],
                                     (XTI if xy else YI)[:, m0 + h, :], (YI if xy else XTI)[:, m0 + h, :])
                        fin(ins, u + q)
                elif s.name == "du":
                    for q in range(2):
                        done_wait(pe, x_units + q)
                    for t in range(NT):
                        begin(u + t)
                        for h in range(HB):
                            ins = mm(bank(u + t)[:, h * P:h * P + P], XTI[:, 4 * t + h, :],
                                     TOK[:, 2, t, h * P:h * P + P])
                        fin(ins, u + t)
                    begin(u + 2)
                    for h in range(HB):
                        ins = mm(bank(u + 2)[:, h * P:h * P + P], KBG[:, h * P:h * P + P],
                                 XTI[:, 4 + h, :])
                    fin(ins, u + 2)
                    du = u
                elif s.name == "dstate":
                    done_wait(pe, du)
                    begin(u)
                    for h in range(HB):
                        ins = mm(bank(u)[:, h * P:h * P + P], PTM[:, h, :], UI[:, h, :])
                    fin(ins, u)
                    begin(u + 1)
                    for h in range(HB):
                        ins = mm(bank(u + 1)[:, h * P:h * P + P], KD[:, h * P:h * P + P], UI[:, h, :])
                    fin(ins, u + 1)
                    dst = u + 1
                elif s.name == "dnew":
                    done_wait(pe, dst)
                    done_wait(pe, du + 2)
                    begin(u)
                    for h in range(HB):
                        ins = mm(bank(u)[:, h * P:h * P + P], WT[:, h * P:h * P + P],
                                 S1B[:, h * P:h * P + P])
                    fin(ins, u)
                    dnew = u
                elif s.name == "dout":
                    done_wait(pe, dnew)
                    begin(u)
                    for h in range(HB):
                        o = bank(u)[:, h * P:h * P + P]
                        mm(o, QGT[:, h * P:h * P + P], S1B[:, h * P:h * P + P], True, False)
                        ins = mm(o, PTM[:, 4 + h, :], VNW[:, h * P:h * P + P], False, True)
                    fin(ins, u)
                elif s.name in ("dyt", "gyt"):
                    hear_dve()
                    src = OB if s.name == "dyt" else XS
                    for q in range(s.nu):
                        begin(u + q)
                        for c in range(2):
                            for t in range(NT):
                                ins = tr(bank(u + q)[:, (2 * c + t) * P:(2 * c + t + 1) * P],
                                         src[:, t, (2 * q + c) * P:(2 * q + c + 1) * P])
                        fin(ins, u + q)
                    mixed = [u + q for q in range(s.nu)]
                elif s.name == "score":
                    if a == 0:
                        for x in steps:
                            if x.name in ("tblk", "nblk") and x.arg[0] in ("qa", "ka", "va"):
                                for q in range(x.nu):
                                    done_wait(pe, x.u + q)
                        probs_units = {}
                    r, c = 64 * (a % 2), a // 2
                    begin(u)
                    mm(bank(u)[:, 0:P], QAT[r:r + 64, c, 0:P], KAT[r:r + 64, c, 0:P])
                    fin(mm(bank(u)[:, P:384], QAT[r:r + 64, c, P:S], KAT[r:r + 64, c, :]), u)
                elif s.name == "probs":
                    hear_dve()
                    begin(u)
                    for c in range(3):
                        ins = tr(bank(u)[:, c * P:c * P + P], MP[:, a % 2, c * P:c * P + P])
                    fin(ins, u)
                    probs_units[a] = u
                elif s.name == "attend":
                    begin(u)
                    for h in (2 * a, 2 * a + 1):
                        done_wait(pe, probs_units[h])
                        o = bank(u)[64 * (h % 2):64 * (h % 2) + 64, :]
                        mm(o[:, 0:S], VA[:, 0, 64 * h:64 * h + 64], MPT[:, h % 4, 0:S], True, False)
                        ins = mm(o[:, P:S], VA[:, 1, 64 * h:64 * h + 64], MPT[:, h % 4, S:384],
                                 False, True)
                    fin(ins, u)
                elif s.name == "up":
                    kind, c = a
                    if c == 0:
                        for x in steps:
                            if x.name == ("dyt" if kind == "b" else "attend"):
                                for q in range(x.nu):
                                    done_wait(pe, x.u + q)
                    tile_ready(s.k)
                    begin(u)
                    for m in range(2):
                        for kc in range(4):
                            c0 = kc * 256 + m * P
                            ins = mm3(bank(u)[:, m * S:m * S + S], w(s.k, c0, c0 + P),
                                      xs_(OT, 4 * (kind == "b") + kc), kc == 0, kc == 3)
                    fin(ins, u)
                    nx += kind == "a"
                elif s.name == "wout":
                    if a in (1, 4):
                        pe.wait_ge(sums_free, 8 * (1 + a // 4))
                    elif a == 3:
                        wait_units(mixed)
                    rows_acc(XT if a == 0 else OT, range(KC), s.k, True, True, x_waits=a in (0, 2))
                elif s.name == "router":
                    for q in range(4):
                        x_wait(q)
                    begin(u)
                    for t in range(NT):
                        for kc in range(KC):
                            ins = mm(bank(u)[:, 64 * t:64 * t + 36], XF[:, kc, t * P:t * P + P],
                                     SMW[:, kc, 8:44], kc == 0, kc == 7)
                    fin(ins, u)
                    hear_dve()
                    b = bank(u + 1)
                    begin(u + 1)
                    oh = [RT[:, t, 48:52] for t in range(NT)]
                    mm(b[:, 0:4], cst("strict"), oh[0])
                    mm(b[:, 4:8], cst("one"), oh[0], True, False)
                    mm(b[:, 4:8], cst("strict"), oh[1], False, True)
                    mm(b[:, 8:12], cst("one"), oh[0], True, False)
                    fin(mm(b[:, 8:12], cst("one"), oh[1], False, True), u + 1)
                    hear_dve()
                elif s.name == "shares":
                    hear_dve()
                    begin(u)
                    for g in range(NG + 1):
                        for t in range(NT):
                            ins = mm(bank(u)[:, NE * g:NE * g + NE], SEL[:, t, g, :],
                                     RT[:, t, 104:112], t == 0, t == 1)
                    fin(ins, u)
                elif s.name == "gather":
                    for q in range(4):
                        begin(u + q)
                        for c in range(2):
                            ch = 2 * q + c
                            for t in range(NT):
                                ins = mm(bank(u + q)[:, c * S:c * S + S], XS[:, t, ch * P:ch * P + P],
                                         SEL[:, t, 2 * a:2 * a + 2, :].rearrange("p a b -> p (a b)"),
                                         t == 0, t == 1)
                        fin(ins, u + q)
                    nx += 4
                    norm_u = None
                elif s.name == "selt":
                    for q in range(3):
                        begin(u + q)
                        for g in range(2 * q, min(2 * q + 2, NG + 1)):
                            for t in range(NT):
                                c = (g % 2) * S + t * P
                                ins = tr(bank(u + q)[:, c:c + P], SEL[:, t, g, :])
                        fin(ins, u + q)
                    selt = [u, u + 1, u + 2]
                elif s.name == "ein":
                    rows_by_cols(XT, s.k, u, nt=1, x_waits=a % (EXPERTS // 2) == 0, c0=P * (a // NE % 2))
                    gated = u
                elif s.name == "etr":
                    done_wait(pe, gated)
                    begin(u)
                    for c in range(2):
                        ins = tr(bank(u)[:, c * P:c * P + P], AE[:, c * P:c * P + P])
                    fin(ins, u)
                    acts = u
                elif s.name == "edown":
                    g, e = divmod(a, NE)
                    if e == 0:
                        if g < 2:
                            pe.wait_ge(acc_free, 2 * nacc)
                        else:
                            pe.wait_ge(y_free, g - 1)
                    done_wait(pe, acts)
                    for j in range(2):
                        tile_ready(s.k + j)
                        for c in range(2):
                            ins = mm3(ACC[:, 2 * (g % 2) + c, :], xs_(OT, j, 0, P),
                                      w(s.k + j, 512 * c, 512 * c + 512), e == 0 and j == 0,
                                      e == NE - 1 and j == 1)
                        ins.then_inc(y_full if e == NE - 1 and j == 1 else used, 1)
                elif s.name == "overflow":
                    pe.wait_ge(ov_known, 1)
                    flag = pe.value_load(OVI[0:1, 0:1], min_val=0, max_val=1)
                    with pe.If(flag > 0):
                        pe.wait_ge(y_free, NG)
                        done_wait(pe, gated)
                        done_wait(pe, acts)
                        done_wait(pe, gated - 2)
                        done_wait(pe, acts - 2)
                        for q in range(2):
                            for c in range(4):
                                for t in range(NT):
                                    ch = 4 * q + c
                                    ins = mm(work[q][:, c * P:c * P + P], XS[:, t, ch * P:ch * P + P],
                                             SEL[:, t, NG, :], t == 0, t == 1)
                        ins.then_inc(ov, 1)
                        pe.wait_ge(ov, 2)
                        with pe.Fori(0, NE) as e:
                            pe.wait_ge(ov_loaded, e * 16 + 16)
                            pe.wait_ge(ov, e * 7 + 2)
                            for kc in range(KC):
                                c = 512 * (kc % 2)
                                ins = mm(work[0][:], XF[:, kc, 0:P], OVW[:, kc // 2, c:c + 512], kc == 0, kc == 7)
                            ins.then_inc(ov, 1)
                            pe.wait_ge(ov, e * 7 + 5)
                            for c in range(2):
                                ins = tr(work[1][:, c * P:c * P + P], AE[:, c * P:c * P + P])
                            ins.then_inc(ov, 1)
                            pe.wait_ge(ov, e * 7 + 7)
                            for c in range(2):
                                mm(work[2 + c][:], OVT[:, 0, :], OVW[:, 4, 512 * c:512 * c + 512], True, False)
                                ins = mm(work[2 + c][:], OVT[:, 1, :], OVW[:, 5, 512 * c:512 * c + 512], False, True)
                            ins.then_inc(ov, 1)
                        pe.wait_ge(ov, 7 * NE + 2)
                elif s.name == "scatter":
                    wait_units(selt)
                    pe.wait_ge(y_free, NG)
                    pe.wait_ge(y_zero, 1)
                    for t in range(NT):
                        for c in range(2):
                            for g in range(NG + 1):
                                ins = mm(ACC[:, 2 * t + c, :], SELT[:, g, t * P:t * P + P],
                                         YG[:, g, 512 * c:512 * c + 512], g == 0, g == NG)
                        ins.then_inc(acc_full, 1)
                    nacc += 1
                elif s.name == "sb":
                    h, layer_sb = a, s.sb
                    if h == 0:
                        for x in steps:
                            if x.name in ("tblk", "nblk") and x.arg[0][0] == "s" and x.sb == layer_sb:
                                for q in range(x.nu):
                                    done_wait(pe, x.u + q)
                    if h < SBH:
                        r, c = 64 * (h % 2), h // 2
                        begin(u)
                        b = bank(u)
                        mm(b[:, 0:S], KT[r:r + 64, c, 0:P], QT[r:r + 64, c, :], True, True)
                        mm(b[:, S:S + P], KT[r:r + 64, c, P:S], QT[r:r + 64, c, P:S], False, True,
                           skip_group_check=True)
                        mm(b[:, 0:P], IDB[:], DROP[:], False, True, skip_group_check=True)
                        fin(mm(b[:, S:S + P], IDB[:], DROP[:], False, True, skip_group_check=True), u)
                        z_units[h] = u
                    if 2 <= h < SBH + 2:
                        nlogs += 1
                        pe.wait_ge(logs_ready, nlogs)
                        b, sp = bank(z_units[h - 2]), SPB[:, (h - 2) % 4, :]
                        mm(b[:, 0:S], cst("neg_ge"), sp[:, 0:S], False, True, skip_group_check=True)
                        mm(b[:, P:S], cst("neg_one"), sp[:, S:S + P], False, True, skip_group_check=True)
                        mm(b[:, S:S + P], cst("neg_ge"), sp[:, S:S + P], False, True,
                           skip_group_check=True).then_inc(z_full, 1)
                    if h >= 4 and h % 2 == 0:
                        c = (h - 4) // 2
                        if c == 0:
                            pe.wait_ge(acc_free, 2 * nacc)
                        if c >= 4:
                            pe.wait_ge(sums_free, 8 * layer_sb + c - 3)
                        for hh in (h - 4, h - 3):
                            done_wait(pe, z_units[hh])
                            o = ACC[64 * (hh % 2):64 * (hh % 2) + 64, c % 4, :]
                            mm(o[:, 0:S], VT[:, 0, 64 * hh:64 * hh + 64], WX[:, hh % 4, 0:S], True, False)
                            ins = mm(o[:, P:S], VT[:, 1, 64 * hh:64 * hh + 64], WX[:, hh % 4, S:S + P],
                                     False, True)
                        ins.then_inc(sums_full, 1)
                elif s.name == "galow":
                    pe.wait_ge(x_lo, nx)
                    hear_dve()
                    begin(u)
                    for kc in range(KC):
                        ins = mm(bank(u)[0:16, 0:S], SMW[:, kc, 44:60], XF[:, kc, :], kc == 0, kc == 7)
                    fin(ins, u)
                    galow = u
                elif s.name == "gates":
                    done_wait(pe, galow)
                    for t in range(NT):
                        begin(u + t)
                        fin(mm(bank(u + t)[:], ALT[0:17, t * P:t * P + P], GUP[:]), u + t)
                    gates = u
                elif s.name == "gcum":
                    for t in range(NT):
                        done_wait(pe, gates + t)
                    for q in range(2):
                        begin(u + q)
                        for h in (2 * q, 2 * q + 1):
                            for t in range(NT):
                                ins = mm(bank(u + q)[:, (h % 2) * S + t * P:(h % 2) * S + t * P + P],
                                         LG[:, t, h * P:h * P + P], TRI)
                        fin(ins, u + q)
                    begin(u + 2)
                    fin(mm(bank(u + 2)[:], cst("after"), LG[:, 0, :]), u + 2)
                    begin(u + 3)
                    for x in steps:
                        if x.name == "tblk" and x.arg[0] == "gk":
                            done_wait(pe, x.u)
                    for h in range(GH):
                        ins = tr(bank(u + 3)[:, h * P:h * P + P], GK[:, h, 0:P])
                    fin(ins, u + 3)
                elif s.name == "gscore":
                    hear_dve(3 if a == 0 else 1)
                    begin(u)
                    for t in range(NT):
                        for h in range(GH):
                            m = GSUB * (GH * t + h)
                            ins = mm(bank(u)[:, m:m + GSUB], KBB[:, a % 2, h, t * P:t * P + P],
                                     QGL[:, h, t * P + GSUB * a:t * P + GSUB * a + GSUB])
                    fin(ins, u)
                    gscores = gscores + [u] if a else [u]
                elif s.name == "gout":
                    wait_units(gscores)
                    for x in steps:
                        if x.name == "nblk" and x.arg[0] == "gv":
                            for q in range(2):
                                done_wait(pe, x.u + q)
                    for q in range(2):
                        begin(u + q)
                        for h in (2 * q, 2 * q + 1):
                            ins = mm(bank(u + q)[:, (h % 2) * 256:(h % 2) * 256 + 256],
                                     KDG[:, h * P:h * P + P], GV[:, 0, 256 * h:256 * h + 256])
                        fin(ins, u + q)
                    for q in range(4):
                        t = q // 2
                        if q == 2:
                            done_wait(pe, u)
                            done_wait(pe, u + 1)
                        begin(u + 2 + q)
                        for h in (2 * (q % 2), 2 * (q % 2) + 1):
                            o = bank(u + 2 + q)[:, (h % 2) * 256:(h % 2) * 256 + 256]
                            if t:
                                mm(o, QI[:, h, :], S1G[:, h, :], True, False)
                            ins = mm(o, STT[:, t, h, :], GV[:, t, 256 * h:256 * h + 256], t == 0, True)
                        fin(ins, u + 2 + q)
                elif s.name == "ffn":
                    def up(b, k, ub, it=None, x_waits=False):
                        rows_by_cols(XT, k, ub, it=it, per=FFN_PER, x_waits=x_waits)

                    def hid_tr(ub, nh, it=None):
                        eu = 0 if it is None else it * FFN_PER["unit"]
                        for t in range(NT):
                            pe.wait_ge(hid_ready, (0 if it is None else it * NT) + (nh + t + 1))
                            begin(ub + 2 + t, eu)
                            for c in range(4):
                                ins = tr(bank(ub + 2 + t)[:, c * P:c * P + P], HID[:, t, c * P:c * P + P])
                            fin(ins, ub + 2 + t)

                    def down(ub, k, first, last, it=None):
                        eu = 0 if it is None else it * FFN_PER["unit"]
                        done_wait(pe, ub + 2, eu)
                        done_wait(pe, ub + 3, eu)
                        rows_acc(OT, range(4), k, first, last, it, FFN_PER)

                    def one(b, it=None):
                        k = s.k + 4 + 8 * b
                        up(b + 1, k, u + 4 * (b + 1), it)
                        down(u + 4 * b, k + 4, b == 0, False, it)
                        hid_tr(u + 4 * (b + 1), nhid + NT * (b + 1), it)

                    up(0, s.k, u, x_waits=True)
                    hid_tr(u, nhid)
                    one(0)
                    with pe.Fori(0, FBLK - 2) as it:
                        one(1, it)
                    down(u + 4 * (FBLK - 1), s.k + s.nk - 4, False, True)
                    nhid += NT * FBLK
                if s.name == "tblk" and a[0] == "cb":
                    nx += 1
                    if a[1] == 3:
                        norm_u = None

        @block.vector
        def _(dve):
            chain = n_a2d = n_d2a = n_d2p = n_hi = nx = nvar = nacc = ngb = nz = nh = 0
            cc_units, pre_units, delta = {}, {}, {}

            def link(ins):
                nonlocal chain
                chain += 1
                return ins.then_inc(dve_chain, 1)

            def sync():
                dve.wait_ge(dve_chain, chain)

            def tell_act(ins):
                nonlocal n_d2a
                n_d2a += 1
                ins.then_inc(d2a, 1)

            def tell_pe(ins):
                nonlocal n_d2p
                n_d2p += 1
                ins.then_inc(d2p, 1)

            def hear_act(n=1):
                nonlocal n_a2d
                n_a2d += n
                dve.wait_ge(a2d, n_a2d)

            split = Splitter(make_lo)

            def v2(u):
                return bank(u)[:].rearrange("p (a b) -> p a b", a=2)

            def v4(u):
                return bank(u)[:].rearrange("p (a b) -> p a b", a=4)

            def free(ins, u):
                return ins.then_inc(done[u % WB], 1)

            def ev_lo(u, dst, hi, src, extra=0):
                nonlocal n_hi
                n_hi += 1
                dve.wait_ge(hi_out, extra + n_hi)
                free(dve.tensor_tensor(dst, src, hi.bitcast(F32), ALU.subtract), u)

            def x_rest(j, hi, lo):
                nonlocal nx
                nx += 1
                dve.wait_ge(x_hi, nx)
                dve.tensor_tensor(lo[:, 2 * j:2 * j + 2, :], XF[:, 2 * j:2 * j + 2, :],
                                  hi[:, 2 * j:2 * j + 2, :].bitcast(F32), ALU.subtract).then_inc(x_lo, 1)

            def sum_sq(col, x, junk):
                return dve.tensor_tensor_reduce(junk, x, x, 1.0, 0.0, ALU.mult, ALU.add,
                                                accum_out=SS[:, col:col + 1])

            def inv_rms(c0, n, scale):
                nonlocal nvar
                nvar += 1
                dve.tensor_scalar(VAR[:, (nvar - 1) % 2, 0:n], SS[:, c0:c0 + n], scale, EPS,
                                  ALU.mult, ALU.add).then_inc(var_ready, 1)
                return nvar

            def roots(req):
                dve.wait_ge(rs_ready, req)
                return RS[:, (req - 1) % 2, :]

            def ask(t, c0):
                hear_act()
                return inv_rms(c0 + t, 1, 1.0 / D)

            def update(t, row, req=None):
                nonlocal nh
                acc = ACC[:, 2 * t:2 * t + 2, :].rearrange("p a b -> p (a b)")
                dve.wait_ge(acc_full, 2 * nacc + 1 + t)
                if req is None:
                    ins = dve.tensor_tensor(XS[:, t, :], acc, row, ALU.mult)
                else:
                    ins = dve.scalar_tensor_tensor(XS[:, t, :], acc, roots(req)[:, 0:1], row,
                                                   ALU.mult, ALU.mult)
                ins.then_inc(acc_free, 1)
                dve.wait_ge(acc_free, 2 * nacc + 1 + t)
                dve.tensor_tensor(H[:, t, :], H[:, t, :], XS[:, t, :], ALU.add).then_inc(h_ready, 1)
                nh += 1

            def scale(t, req):
                tell_pe(dve.tensor_scalar(XS[:, t, :], H[:, t, :], roots(req)[:, 0:1], None, ALU.mult))

            def gb_row():
                nonlocal ngb
                dve.wait_ge(gb_loaded[ngb % 2], 16 * (ngb // 2 + 1))
                ngb += 1
                return GB[:, (ngb - 1) % 2, :]

            def col(v, n, w):
                return v.unsqueeze(2).broadcast_to([P, n, w])

            def level(lev):
                mask = cst("levels")[:, P * lev:P * lev + P]
                tell_pe(dve.tensor_tensor(NTL, NMT, over(mask, 8), ALU.mult))

            for s in steps:
                u, a = s.u, s.arg
                if s.name in ("tblk", "mod", "nblk", "up"):
                    split.upto(s.k + s.nk + SPL)
                elif s.name == "wout":
                    split.upto(s.k + s.nk)
                if s.name == "params":
                    dve.wait_ge(load_const, 16 * NCONST)
                    full_wait(dve, u)
                    free(dve.tensor_copy(COLP[:], bank(u)[:, 0:ROWS1 + ROWS2]), u)
                    dve.memset(REL[32:33, :], 1.0).then_inc(rel_set, 1)
                    link(dve.memset(VAR[:], 1.0))
                    link(dve.memset(MH[:], -0.5))
                    link(dve.tensor_copy(IDB[:], IDENT))
                    link(dve.tensor_scalar(DROP[:], cst("strict"), 1.0, DROPPED, ALU.subtract, ALU.mult))
                    link(dve.memset(PRE[:, :, 0:3], 0.0))
                elif s.name == "cond":
                    hear_act()
                    tell_act(dve.tensor_copy(XF[:, :, 0:P], col(CC[:, 2, :], KC, P)))
                    nx += 1
                    dve.wait_ge(x_hi, nx)
                    dve.tensor_tensor(OTl[:, :, 0:P], XF[:, :, 0:P], OTh[:, :, 0:P].bitcast(F32),
                                      ALU.subtract).then_inc(x_lo, 1)
                elif s.name == "mod":
                    mod_u = u
                elif s.name == "modcols":
                    u = mod_u
                    sec, half = divmod(a, 2)
                    j, kind = divmod(sec, 3)
                    full_wait(dve, u)
                    if kind == 2:
                        dve.wait_ge(gb_loaded[j], 16)
                        g = GB[:, j, 512 * half:512 * half + 512]
                        free(dve.tensor_tensor(g, bank(u)[:], g, ALU.add), u)
                    else:
                        row = 4 if kind else 2 * j
                        mc = MODC[:, row, 4 * half:4 * half + 4]
                        for i in range(4):
                            ins = dve.tensor_tensor_reduce(
                                JUNK[:, i, :], bank(u)[:, i * P:i * P + P], IDENT, 1.0, 0.0,
                                ALU.mult, ALU.add, accum_out=mc[:, i:i + 1])
                        free(ins, u)
                        done_wait(dve, u)
                        bm = COLP[:, R_BM + 8 * sec + 4 * half:][:, 0:4]
                        link(dve.tensor_tensor(mc, mc, bm, ALU.add))
                        if kind == 1:
                            sync()
                            nw = COLP[:, (R_N1, R_N2)[j] + 4 * half:][:, 0:4]
                            ins = dve.scalar_tensor_tensor(MODC[:, 2 * j + 1, 4 * half:4 * half + 4],
                                                           mc, 1.0, nw, ALU.add, ALU.mult)
                            if half:
                                tell_act(ins)
                elif s.name == "norm":
                    if a == 0:
                        dve.wait_ge(load_rest, 16 * NREST)
                        req = [ask(t, 0) for t in range(NT)]
                        for t in range(NT):
                            scale(t, req[t])
                    if a == 1:
                        pass
                    elif a in FULL_NORMS:
                        for q in range(4):
                            x_rest(q, XTh, XTl)
                    else:
                        for q in range(4):
                            nx += 1
                            dve.wait_ge(x_hi, nx)
                            for c in range(2):
                                ch = 2 * q + c
                                gain = COLP[:, R_PRE + 8 * (a - 2) + ch:][:, 0:1]
                                ins = dve.scalar_tensor_tensor(XTl[:, ch, :], v2(u + q)[:, c, :], gain,
                                                               XTh[:, ch, :].bitcast(F32),
                                                               ALU.mult, ALU.subtract)
                            free(ins, u + q)
                elif s.name == "ba":
                    full_wait(dve, u)
                    ba = bank(u)[:, 0:16].rearrange("p (t k h) -> p t k h", t=2, k=2)
                    dt = over(SROW[:, S_DT:S_DT + 4], 2)
                    link(dve.tensor_copy(BT[:, 0, :].rearrange("p (t h) -> p t h", t=2), ba[:, :, 0, :]))
                    free(dve.tensor_tensor(BT[:, 1, :].rearrange("p (t h) -> p t h", t=2),
                                           ba[:, :, 1, :], dt, ALU.add), u)
                    done_wait(dve, u)
                    tell_act(dve.tensor_scalar(BT[:, 7, :], BT[:, 1, :], 0.0, None, ALU.max))
                    hear_act()
                    link(dve.tensor_scalar(BT[:, 2, :], BT[:, 2, :], 1.0, None, ALU.add))
                    link(dve.tensor_tensor(BT[:, 7, :], BT[:, 7, :], BT[:, 5, :], ALU.add))
                    sync()
                    link(dve.reciprocal(BT[:, 2, :], BT[:, 2, :]))
                    link(dve.scalar_tensor_tensor(
                        BT[:, 7, :].rearrange("p (t h) -> p t h", t=2),
                        BT[:, 7, :].rearrange("p (t h) -> p t h", t=2), -1.0,
                        over(BT[:, 6, 0:4], 2), ALU.mult, ALU.mult))
                elif s.name == "conv":
                    done_wait(dve, pre_units[a])
                    for tap in range(4):
                        for ch in (2 * a, 2 * a + 1):
                            w = COLP[:, R_CW + 12 * tap + ch:][:, 0:1]
                            src = PRE[:, ch, tap:tap + S]
                            if tap == 0:
                                ins = dve.tensor_scalar(POST[:, ch, :], src, w, None, ALU.mult)
                            else:
                                ins = dve.scalar_tensor_tensor(POST[:, ch, :], src, w,
                                                               POST[:, ch, :], ALU.mult, ALU.add)
                        if tap < 3:
                            link(ins)
                            sync()
                        else:
                            ins.then_inc(conv_done, 1)
                elif s.name == "dtok":
                    for q in range(4):
                        done_wait(dve, u + q)
                        for h in range(HB):
                            link(sum_sq(4 * q + h, TOK[:, q // 2, q % 2, h * P:h * P + P],
                                        area(9252, 16, P)[:, 4 * q + h, :]))
                    sync()
                    norm_req = inv_rms(0, 16, 1.0)
                    for q in range(4, 6):
                        done_wait(dve, u + q)
                elif s.name == "decay":
                    sync()
                    tell_pe(dve.tensor_copy(NTL[:], col(BT[:, 7, :], 8, P)))
                    rqk = roots(norm_req)
                    link(dve.tensor_scalar(rqk[:, 0:8], rqk[:, 0:8], float(P) ** -0.5, None, ALU.mult))
                    hear_act()
                    free(dve.tensor_copy(GC[:], bank(u)[:, 0:24]), u)
                    done_wait(dve, u)
                elif s.name == "decay_rows":
                    for t in range(NT):
                        full_wait(dve, u + t)
                        if t == 1:
                            hear_act()
                        for h in range(HB):
                            m = 4 * t + h
                            ins = dve.tensor_scalar(DTI[:, m, :], bank(u + t)[:, h * P:h * P + P],
                                                    GC[:, m:m + 1], 0.0, ALU.subtract, ALU.min)
                        free(ins, u + t)
                elif s.name == "dtr":
                    k8 = TOK[:, 1, :, :].rearrange("p t (h d) -> p (t h) d", h=HB)
                    q8 = TOK[:, 0, :, :].rearrange("p t (h d) -> p (t h) d", h=HB)
                    v8 = TOK[:, 2, :, :].rearrange("p t (h d) -> p (t h) d", h=HB)
                    kb8 = KBK[:].rearrange("p t (h d) -> p (t h) d", h=HB)

                    def heads(v):
                        return v.rearrange("p (h d) -> p h d", h=HB)

                    tell_pe(dve.tensor_tensor(k8, k8, col(rqk[:, 8:16], 8, P), ALU.mult))
                    dve.wait_ge(d2p, n_d2p)
                    tell_pe(dve.tensor_tensor(kb8, k8, col(BT[:, 2, :], 8, P), ALU.mult))
                    tell_pe(dve.tensor_tensor(q8, q8, col(rqk[:, 0:8], 8, P), ALU.mult))
                    dve.wait_ge(d2p, n_d2p)
                    link(dve.tensor_tensor(heads(KBG), kb8[:, 4:8, :], col(EG[:, 4:8], 4, P), ALU.mult))
                    link(dve.tensor_tensor(heads(KD), k8[:, 0:4, :], col(EG[:, 8:12], 4, P), ALU.mult))
                    link(dve.tensor_tensor(v8, v8, col(BT[:, 2, :], 8, P), ALU.mult))
                    hear_act()
                    link(dve.tensor_tensor(DTI, DTI, over(TRI, 8), ALU.mult))
                    sync()
                    link(dve.tensor_tensor(DTS, DTI, over(cst("strict"), 8), ALU.mult))
                    link(dve.tensor_copy(XI, over(IDENT, 8)))
                    link(dve.tensor_copy(XTI, over(IDENT, 8)))
                    qnt_units = (u + 4, u + 5)
                elif s.name == "dmat":
                    sync()
                    for q in range(4):
                        kind, t = divmod(q, 2)
                        full_wait(dve, u + q)
                        dst, dec = (PTM, DTI) if kind else (NMT, DTS)
                        free(dve.tensor_tensor(dst[:, 4 * t:4 * t + 4, :], v4(u + q),
                                               dec[:, 4 * t:4 * t + 4, :], ALU.mult), u + q)
                    done_wait(dve, qnt_units[1])
                    done_wait(dve, u + 1)
                    link(dve.tensor_tensor(QGT.rearrange("p (h d) -> p h d", h=HB), QNT[:, 1],
                                           ER.rearrange("p (h d) -> p h d", h=HB), ALU.mult))
                    sync()
                    level(0)
                elif s.name == "inv_x":
                    for q in range(s.nu):
                        dst = XI if s.nu == 4 and q < 2 else XTI
                        d = dst[:, 4 * (q % 2):4 * (q % 2) + 4, :]
                        full_wait(dve, u + q)
                        if q % 2 == 0 and q == s.nu - 2:
                            full_wait(dve, u + q + 1)
                        free(dve.tensor_tensor(d, d, v4(u + q), ALU.subtract), u + q)
                    done_wait(dve, u + s.nu - 1)
                    if a < LEVELS - 1:
                        level(a + 1)
                elif s.name == "du":
                    delta["du"] = u
                elif s.name == "dnew":
                    full_wait(dve, u)
                    done_wait(dve, delta["du"] + 1)
                    free(dve.tensor_tensor(VNW.rearrange("p (h d) -> p h d", h=HB), UI[:, 4:8, :],
                                           v4(u), ALU.subtract), u)
                    delta["dnew"] = u
                elif s.name == "dnorm":
                    for x in steps:
                        if x.name == "nblk" and x.arg[0] == "z":
                            zu = x.u
                        if x.name == "dstate":
                            du0 = x.u
                        if x.name == "dout":
                            do = x.u
                    done_wait(dve, zu)
                    done_wait(dve, zu + 1)
                    z8 = ZS[:].rearrange("p t (h d) -> p (t h) d", h=HB)
                    link(dve.tensor_tensor(z8, z8, over(SROW[:, S_ON:S_ON + P], 8), ALU.mult))
                    done_wait(dve, du0)
                    done_wait(dve, do)
                    sync()
                    for t in range(NT):
                        for h in range(HB):
                            link(sum_sq(4 * t + h, OB[:, t, h * P:h * P + P], YI[:, 4 * t + h, :]))
                    sync()
                    rs = roots(inv_rms(0, 8, 1.0 / P))
                    for t in range(NT):
                        for h in range(HB):
                            o = OB[:, t, h * P:h * P + P]
                            ins = dve.scalar_tensor_tensor(o, o, rs[:, 4 * t + h:4 * t + h + 1],
                                                           ZS[:, t, h * P:h * P + P], ALU.mult, ALU.mult)
                    tell_pe(ins)
                elif s.name == "dyt":
                    for q in range(2):
                        ev_lo(u + q, OTl[:, 4 + 2 * q:6 + 2 * q, :], OTh[:, 4 + 2 * q:6 + 2 * q, :], v2(u + q))
                elif s.name == "score":
                    if a % 4 == 0:
                        dve.wait_ge(bias_read[a // 4], 32)
                    g = a % 2
                    full_wait(dve, u)
                    free(dve.scalar_tensor_tensor(MS_[:, g, :], bank(u)[:, 0:384], HDA ** -0.5,
                                                  BIAS[:, a, :], ALU.mult, ALU.add), u)
                    done_wait(dve, u)
                    dve.tensor_reduce(SS[:, 2 * g:2 * g + 1], MS_[:, g, 0:P], AX, ALU.max, negate=True)
                    tell_act(dve.tensor_reduce(SS[:, 2 * g + 1:2 * g + 2], MS_[:, g, P:384], AX, ALU.max,
                                               negate=True))
                    hear_act()
                    link(dve.reciprocal(RS2[:, g, :], RS2[:, g, :]))
                    sync()
                    dve.tensor_scalar(MP[:, g, 0:P], MP[:, g, 0:P], RS2[:, g, 0:1], None, ALU.mult)
                    tell_pe(dve.tensor_scalar(MP[:, g, P:384], MP[:, g, P:384], RS2[:, g, 1:2], None,
                                              ALU.mult))
                elif s.name == "attend":
                    ev_lo(u, OTl[:, a, :], OTh[:, a, :], bank(u)[:, 0:S])
                elif s.name == "up":
                    kind, c = a
                    xp = XF[:, 2 * c:2 * c + 2, :]
                    for x in steps:
                        if x.name == "tblk" and x.arg == ("g" + kind, c):
                            done_wait(dve, x.u)
                    full_wait(dve, u)
                    if kind == "b":
                        free(dve.tensor_tensor(xp, v2(u), SGB[:, 2 * c:2 * c + 2, :], ALU.mult), u)
                    else:
                        free(dve.tensor_tensor(MTMP[:, c % 2], v2(u), SGA[:, 2 * c:2 * c + 2, :], ALU.mult), u)
                        done_wait(dve, u)
                        dve.tensor_tensor(xp, xp, MTMP[:, c % 2], ALU.add).then_inc(xf_ready, 1)
                        x_rest(c, XTh, XTl)
                elif s.name == "res1":
                    row = gb_row()
                    update(0, row)
                    split.upto(s.k + 1)
                    r0 = ask(0, 0)
                    update(1, row)
                    scale(0, r0)
                    split.upto(s.k + 2)
                    r1 = ask(1, 0)
                    scale(1, r1)
                    split.upto(s.k + 4)
                    nacc += 1
                elif s.name == "res2":
                    def final(t, req):
                        nonlocal nh
                        dve.scalar_tensor_tensor(H[:, t, :], H[:, t, :], roots(req)[:, 0:1], frow,
                                                 ALU.mult, ALU.mult).then_inc(h_ready, 1)
                        nh += 1

                    row = gb_row()
                    update(0, row)
                    update(1, row)
                    frow = gb_row()
                    f0 = ask(0, 4)
                    final(0, f0)
                    f1 = ask(1, 4)
                    final(1, f1)
                    r0 = ask(0, 0)
                    scale(0, r0)
                    r1 = ask(1, 0)
                    scale(1, r1)
                    split.upto(s.k + 4)
                    nacc += 1
                elif s.name == "router":
                    def r(c0, c1=None):
                        return RT[:, :, c0:c0 + 1 if c1 is None else c1]

                    def wide(c, w):
                        return r(c).broadcast_to([P, NT, w])

                    def op(o, x, y, f):
                        sync()
                        return link(dve.tensor_tensor(o, x, y, f))

                    def top(values, at_max, idx, onehot, w):
                        iota = over(cst("iota")[:, 0:w], NT)
                        sync()
                        link(dve.tensor_reduce(r(at_max), values, AX, ALU.max))
                        op(r(112, 112 + w), values, wide(at_max, w), ALU.is_lt)
                        sync()
                        link(dve.scalar_tensor_tensor(r(112, 112 + w), r(112, 112 + w), 8.0, iota,
                                                      ALU.mult, ALU.add))
                        sync()
                        link(dve.tensor_reduce(r(idx), r(112, 112 + w), AX, ALU.min))
                        op(onehot, iota, wide(idx, w), ALU.is_equal)

                    full_wait(dve, u)
                    free(dve.tensor_tensor(r(0, 36), bank(u)[:, 0:128].rearrange("p (t w) -> p t w", t=2)[:, :, 0:36],
                                           over(SROW[:, S_BR:S_BR + 36], NT), ALU.add), u)
                    done_wait(dve, u)
                    top(r(0, 4), 36, 52, r(48, 52), 4)
                    sync()
                    tell_pe(dve.tensor_copy(r(152, 156), r(48, 52)))
                    tell_act(dve.tensor_scalar(r(37), r(36), -1.0, None, ALU.mult))
                    full_wait(dve, u + 1)
                    b = bank(u + 1)
                    link(dve.tensor_tensor(r(128, 132), b[:, 0:8].rearrange("p (t g) -> p t g", t=2),
                                           r(48, 52), ALU.mult))
                    free(dve.tensor_scalar(OVF[:], b[:, 8:12], float(P), None, ALU.is_gt), u + 1)
                    sync()
                    link(dve.tensor_reduce(r(132), r(128, 132), AX, ALU.add))
                    sync()
                    link(dve.tensor_scalar(r(133), r(132), 1000.0, None, ALU.add))
                    link(dve.tensor_scalar(r(140), r(132), -float(P), None, ALU.add))
                    sync()
                    link(dve.scalar_tensor_tensor(r(136, 140), r(48, 52), -1000.0, wide(133, 4),
                                                  ALU.mult, ALU.add))
                    sync()
                    for t in range(NT):
                        for g in range(NG + 1):
                            ins = dve.tensor_scalar(SEL[:, t, g, :], cst("cols"), RT[:, t, 136 + g:137 + g],
                                                    None, ALU.is_equal)
                    tell_pe(ins)
                    done_wait(dve, u + 1)
                    link(dve.tensor_reduce(OVX[:, 0:1], OVF[:], AX, ALU.max))
                    sync()
                    link(dve.tensor_tensor(OVF[:], OVF[:], cst("iota")[:, 0:4], ALU.mult))
                    sync()
                    link(dve.tensor_reduce(OVX[:, 1:2], OVF[:], AX, ALU.max))
                    sync()
                    dve.tensor_copy(OVI[:], OVX[:]).then_inc(ov_known, 1)
                    for g in range(NG):
                        le = r(4 + 8 * g, 12 + 8 * g)
                        if g == 0:
                            op(r(56, 64), le, wide(48, 8), ALU.mult)
                        else:
                            op(r(120, 128), le, wide(48 + g, 8), ALU.mult)
                            op(r(56, 64), r(56, 64), r(120, 128), ALU.add)
                    top(r(56, 64), 64, 66, r(72, 80), 8)
                    sync()
                    link(dve.scalar_tensor_tensor(r(88, 96), r(72, 80), 2 * NEG, r(56, 64), ALU.mult, ALU.add))
                    top(r(88, 96), 65, 67, r(80, 88), 8)
                    sync()
                    tell_act(dve.tensor_tensor(r(97), r(65), r(64), ALU.subtract))
                    hear_act(3)
                    link(dve.reciprocal(r(45), r(44)))
                    sync()
                    link(dve.tensor_scalar(r(99), r(98), 1.0, None, ALU.add))
                    sync()
                    link(dve.reciprocal(r(100), r(99)))
                    op(r(101), r(100), r(45), ALU.mult)
                    op(r(102), r(101), r(98), ALU.mult)
                    op(r(104, 112), r(72, 80), wide(101, 8), ALU.mult)
                    op(r(120, 128), r(80, 88), wide(102, 8), ALU.mult)
                    sync()
                    tell_pe(dve.tensor_tensor(r(104, 112), r(104, 112), r(120, 128), ALU.add))
                elif s.name == "shares":
                    full_wait(dve, u)
                    free(dve.tensor_copy(CG, bank(u)[:, 0:NE * (NG + 1)]), u)
                    done_wait(dve, u)
                    dve.memset(YG[:, NG, :], 0.0).then_inc(y_zero, 1)
                elif s.name == "gather":
                    for q in range(4):
                        x_rest(q, XTh, XTl)
                elif s.name == "ein":
                    split.upto(s.k + 6)
                    hear_act()
                    free(dve.scalar_tensor_tensor(AE, SG, CG[:, a:a + 1], bank(u)[:, 256:512],
                                                  ALU.mult, ALU.mult), u)
                elif s.name == "edown":
                    split.upto(s.k + 6)
                elif s.name == "etr":
                    ev_lo(u, OTl[:, 0:2, 0:P], OTh[:, 0:2, 0:P],
                          bank(u)[:, 0:256].rearrange("p (a b) -> p a b", a=2))
                elif s.name == "overflow":
                    dve.wait_ge(ov_known, 1)
                    dve.wait_ge(y_zero, 1)
                    flag = dve.value_load(OVI[0:1, 0:1], min_val=0, max_val=1)
                    with dve.If(flag > 0):
                        with dve.Fori(0, NE) as e:
                            dve.wait_ge(ov, e * 7 + 4)
                            dve.scalar_tensor_tensor(AE, SG, CG[:, bass.ds(e + NG * NE, 1)],
                                                     work[0][:, 256:512], ALU.mult, ALU.mult).then_inc(ov, 1)
                            dve.wait_ge(ov, e * 7 + 8)
                            for c in range(2):
                                y = YG[:, NG, 512 * c:512 * c + 512]
                                ins = dve.tensor_tensor(y, y, work[2 + c][:], ALU.add)
                            ins.then_inc(ov, 1)
                elif s.name == "post":
                    row = gb_row()
                    p0 = ask(0, 4)
                    update(0, row, p0)
                    split.upto(s.k + 2)
                    if a == ("ffn", 3):
                        p1 = ask(1, 4)
                        update(1, row, p1)
                    else:
                        r0 = ask(0, 0)
                        p1 = ask(1, 4)
                        scale(0, r0)
                        update(1, row, p1)
                        split.upto(s.k + 3)
                        r1 = ask(1, 0)
                        scale(1, r1)
                        split.upto(s.k + 4)
                    nacc += 1
                elif s.name == "ffn":
                    def square(ub, extra=0):
                        for t in range(NT):
                            done_wait(dve, ub + t, extra)
                            dve.tensor_tensor(HID[:, t, :], HID[:, t, :], HID[:, t, :], ALU.mult)\
                                .then_inc(hid_ready, 1)

                    def t_lo(ut, extra=0):
                        for t in range(NT):
                            tt = slice(t * P, t * P + P)
                            ev_lo(ut + t, OTl[:, 0:4, tt], OTh[:, 0:4, tt], v4(ut + t), extra)

                    def one(b, k, ub, it=None):
                        for kk in range(k + 4, k + 8):
                            make_lo(kk, it, FFN_PER)
                        square(ub, 0 if it is None else it * FFN_PER["unit"])
                        for kk in range(k + 8, k + 12):
                            make_lo(kk, it, FFN_PER)
                        t_lo(ub + 2, 0 if it is None else 2 * it)

                    split.upto(s.k + 4)
                    square(u)
                    split.upto(s.k + 8)
                    t_lo(u + 2)
                    one(0, s.k + 4, u + 4)
                    with dve.Fori(0, FBLK - 2) as it:
                        one(1, s.k + 12, u + 8, it)
                    n_hi += 2 * (FBLK - 3)
                    split.next = s.k + s.nk
                elif s.name == "sb":
                    h = a
                    if h < SBH:
                        hear_act()
                        b = h % 4
                        dve.scalar_tensor_tensor(SPB[:, b, :], bank(u)[:, 0:384], 0.0, LN[:, b, :],
                                                 ALU.max, ALU.add).then_inc(logs_ready, 1)
                    if h >= 4 and h % 2 == 0:
                        c = (h - 4) // 2
                        n_hi += 1
                        dve.wait_ge(hi_out, n_hi)
                        dve.tensor_tensor(OTl[:, c, :], ACC[:, c % 4, 0:S], OTh[:, c, :].bitcast(F32),
                                          ALU.subtract).then_inc(sums_free, 1)
                elif s.name == "tblk":
                    kind, c = a
                    if kind == "pre":
                        pre_units[c] = u
                    elif kind == "cc":
                        cc_units[c] = u
                        if c == 0:
                            link(dve.memset(HP[:, :, 0:2], 0.0))
                    elif kind == "cu":
                        done_wait(dve, cc_units[c])
                        full_wait(dve, u)
                        free(dve.tensor_tensor(HP[:, 2 * c:2 * c + 2, 2:2 + S], v2(u),
                                               CB[:, 2 * c:2 * c + 2, :], ALU.mult), u)
                        if c == 0:
                            sync()
                        done_wait(dve, u)
                        for tap in range(3):
                            for ch in (2 * c, 2 * c + 1):
                                w = COLP[:, R_CW2 + 8 * tap + ch:][:, 0:1]
                                src = HP[:, ch, tap:tap + S]
                                if tap == 0:
                                    ins = dve.tensor_scalar(CV[:, ch, :], src, w, None, ALU.mult)
                                else:
                                    ins = dve.scalar_tensor_tensor(CV[:, ch, :], src, w, CV[:, ch, :],
                                                                   ALU.mult, ALU.add)
                            link(ins)
                            if tap < 2:
                                sync()
                    elif kind == "cb":
                        sync()
                        full_wait(dve, u)
                        free(dve.tensor_tensor(XF[:, 2 * c:2 * c + 2, :], v2(u), CV[:, 2 * c:2 * c + 2, :], ALU.mult), u)
                        x_rest(c, OTh, OTl)
                elif s.name == "galow":
                    tell_pe(dve.memset(ALT[0:17, :], 1.0))
                elif s.name == "gates":
                    for t in range(NT):
                        hear_act()
                        free(dve.scalar_tensor_tensor(LG[:, t, :], bank(u + t)[:], 0.0, GTM[:, t, :],
                                                      ALU.min, ALU.subtract), u + t)
                elif s.name == "gcum":
                    gcum, score_units = u, {}
                    link(dve.memset(REF[:, :, 0:1], 0.0))
                    done_wait(dve, u)
                    done_wait(dve, u + 1)
                    cum8 = CUM[:].rearrange("p h (t i) -> p (h t) i", t=NT)
                    link(dve.tensor_copy(REF[:, :, 1:4], cum8[:, :, GSUB - 1:P - 1:GSUB]))
                elif s.name == "gkeys":
                    if a == 0:
                        sync()
                        cum32 = CUM[:].rearrange("p h (b i) -> p (h b) i", i=GSUB)
                        ref32 = REF[:].rearrange("p a b -> p (a b)")
                        qgl = QGL[:].rearrange("p h (b i) -> p (h b) i", i=GSUB)
                        tell_act(dve.tensor_tensor(qgl, cum32, col(ref32, 32, GSUB), ALU.subtract))
                    if a >= 2:
                        dve.wait_ge(full[score_units[a - 2] % WB], score_units[a - 2] // WB + 1)
                    kb = KBB[:, a % 2].rearrange("p h (t i) -> p (h t) i", t=NT)
                    link(dve.tensor_tensor(kb, cum8, REF[:, :, a:a + 1].broadcast_to([P, GH * NT, P]),
                                           ALU.subtract))
                    sync()
                    tell_act(dve.tensor_scalar(kb, kb, -GCLAMP, None, ALU.max))
                    if a == 0:
                        hear_act()
                        link(dve.tensor_tensor(QI, QI, GQ[:, :, P:S], ALU.mult))
                        hear_act()
                        tell_pe(dve.tensor_tensor(QGL, QGL, GQ, ALU.mult))
                        done_wait(dve, gcum + 2)
                        done_wait(dve, gcum + 3)
                        tell_pe(dve.tensor_tensor(KDG, KTK, ES, ALU.mult))
                    hear_act()
                    tell_pe(dve.tensor_tensor(KBB[:, a % 2], KBB[:, a % 2], GK, ALU.mult))
                elif s.name == "gscore":
                    score_units[a] = u
                    full_wait(dve, u)
                    i = slice(GSUB * a, GSUB * a + GSUB)
                    free(dve.tensor_tensor(STT[:].rearrange("p t h i -> p (t h) i")[:, :, i],
                                           bank(u)[:, 0:S].rearrange("p (m i) -> p m i", i=GSUB),
                                           over(TRI[:, i], 8), ALU.mult), u)
                elif s.name == "gout":
                    gout_units = u
                    row = gb_row()
                    for x in steps:
                        if x.name == "nblk" and x.arg[0] == "gg":
                            done_wait(dve, x.u)
                            done_wait(dve, x.u + 1)
                    for t in range(NT):
                        ins = dve.tensor_tensor(GG[:, t, :], GG[:, t, :], row, ALU.mult)
                    ins.then_inc(gb_free, 1)
                elif s.name == "gyt":
                    for q in range(4):
                        done_wait(dve, gout_units + 2 + q)
                    for t in range(NT):
                        for h in range(GH):
                            link(sum_sq(4 * t + h, XS[:, t, 256 * h:256 * h + 256],
                                        area(0, 8, 256)[:, 4 * t + h, :]))
                    sync()
                    rs = roots(inv_rms(0, 8, 1.0 / 256))
                    dve.wait_ge(gb_free, 1)
                    for t in range(NT):
                        for h in range(GH):
                            o = XS[:, t, 256 * h:256 * h + 256]
                            ins = dve.scalar_tensor_tensor(o, o, rs[:, 4 * t + h:4 * t + h + 1],
                                                           GG[:, t, 256 * h:256 * h + 256],
                                                           ALU.mult, ALU.mult)
                    tell_pe(ins)
                    for q in range(4):
                        ev_lo(u + q, OTl[:, 2 * q:2 * q + 2, :], OTh[:, 2 * q:2 * q + 2, :], v2(u + q))


def pack(i):
    win = i["w_in"][0]
    gains = i["norm_gains_2"]
    steps = schedule()
    prows = np.concatenate([
        i["norm1_w"].reshape(8, P), i["norm2_w"].reshape(8, P), i["b_mod"].reshape(48, P),
        np.stack([gains[:, 0], gains[:, 2]], axis=1).reshape(64, P),
        i["conv_w"].reshape(48, P), i["conv_w_2"].reshape(24, P)])
    bm = i["b_mod"].reshape(6, D)
    experts = np.stack([np.stack(
        tile_n(np.concatenate([i["w_e_gate"][0, g, x], i["w_e_up"][0, g, x]], axis=1), 0)
        + tile_rows(i["w_e_down"][0, g, x]), axis=1) for g in range(NG) for x in range(NE)])
    smw = np.concatenate([win[:, C_BA:C_BA + 8], i["w_rg"][0], i["w_re"][0],
                          i["gla_w_in_2"][0][:, 3 * D:3 * D + 16]], axis=1)
    return {k: np.ascontiguousarray(v) for k, v in {
        "experts": experts, "x": i["x"], "weights": weight_tiles(i, steps), "cst": constants()[0], "prows": prows,
        "c": i["c"],
        "srow": np.concatenate([i["dt_bias"].ravel(), i["a_log"].ravel(), i["b_rg"].ravel(),
                                i["b_re"].ravel(), i["onorm_w"].ravel()]),
        "smw": smw.reshape(KC, P, 60).transpose(1, 0, 2),
        "gup": np.concatenate([i["gla_w_gate_up_2"][0], i["gla_b_gate_2"]]),
        "rel_bias": i["rel_bias"], "oh": bucket_rows(),
        "brow": np.concatenate([bm[2:3], bm[5:6], i["final_norm_w"].reshape(1, D),
                                np.stack([gains[:, 1], gains[:, 3]], axis=1).reshape(8, D),
                                i["gla_head_norm_2"].reshape(1, D)]),
    }.items()}


def kernel(**inputs):
    import concourse.bacc as _bacc
    from concourse.bass_utils import run_bass_kernel_spmd as _run

    arrays = pack({n: np.asarray(a) for n, a in inputs.items()})
    nc = _bacc.Bacc("TRN2", target_bir_lowering=False, num_devices=1)
    aps = {n: nc.dram_tensor("in_" + n, a.shape, F32, kind="ExternalInput").ap()
           for n, a in arrays.items()}
    aps["out"] = nc.dram_tensor("out", (1, S, D), F32, kind="ExternalOutput").ap()
    build(nc, aps)
    r = _run(nc, [{"in_" + n: a for n, a in arrays.items()}], core_ids=[0])
    return r.results[0]["out"]
```
